# Optimizing a Trainium2 kernel written in Bass

```python
import jax, jax.numpy as jnp
from jax import lax
import numpy as np

D_MODEL = 1024
BATCH = 1
SEQ = 256
DEPTH = 2
DEC_BATCH = 1
DEC_SEQ = 256
PAST_LEN = 128

N_EVEN = (DEPTH + 1) // 2
N_ODD = DEPTH // 2
EPS = 1e-6

SSD_HEADS = 16
SSD_HEAD_DIM = 64
SSD_INNER = SSD_HEADS * SSD_HEAD_DIM
SSD_GROUPS = 2
SSD_HPG = SSD_HEADS // SSD_GROUPS
SSD_STATE = 128
SSD_CONV = 3
SSD_CHUNK = 128
SSD_CONV_DIM = SSD_INNER + 2 * SSD_GROUPS * SSD_STATE

MLA_HEADS = 8
MLA_Q_LORA = 256
MLA_KV_LORA = 128
MLA_NOPE = 128
MLA_ROPE = 64
MLA_V = 128
MLA_QBLOCK = 128
ROPE_THETA = 10000.0

EVEN_IN = SSD_INNER + SSD_CONV_DIM + 2 * SSD_HEADS + MLA_Q_LORA + MLA_KV_LORA + MLA_ROPE
EVEN_MIX = SSD_INNER + MLA_HEADS * MLA_V

GLA_HEADS = 4
GLA_KEY = D_MODEL // 2
GLA_VAL = D_MODEL
GLA_HK = GLA_KEY // GLA_HEADS
GLA_HV = GLA_VAL // GLA_HEADS
GLA_GATE_RANK = 16
GLA_GATE_NORM = 16.0
GLA_CHUNK = 64
ODD_IN = 2 * GLA_KEY + 2 * GLA_VAL + 2 * GLA_GATE_RANK

D_FF = 2816
FFN_CONV = 3

kernel_name = 'hybrid_ssd_mla_gla_encoder'

def rmsnorm(x, w):
    xf = x.astype(jnp.float32)
    y = xf * lax.rsqrt(jnp.mean(xf * xf, axis=-1, keepdims=True) + EPS)
    return (y * w.astype(jnp.float32)).astype(x.dtype)

def dwconv_centred(x, w, b):
    k, c = w.shape
    y = lax.conv_general_dilated(x, w[:, None, :].astype(x.dtype), window_strides=(1,),
                                 padding=[(k // 2, k // 2)],
                                 dimension_numbers=('NWC', 'WIO', 'NWC'),
                                 feature_group_count=c)
    return y + b.astype(x.dtype)

def to_chunks(t, size):
    b, s = t.shape[:2]
    return jnp.moveaxis(t.reshape((b, s // size, size) + t.shape[2:]), 1, 0)

def from_chunks(t):
    t = jnp.moveaxis(t, 0, 1)
    return t.reshape((t.shape[0], t.shape[1] * t.shape[2]) + t.shape[3:])

def flip_seq(t):
    return jnp.flip(t, axis=1)

def ssd_scan(x, dt, a, b_in, c_in):
    bsz, _, g, e, p = x.shape
    n = b_in.shape[-1]
    causal = jnp.tril(jnp.ones((SSD_CHUNK, SSD_CHUNK), dtype=bool))[None, :, :, None, None]

    def step(state, inp):
        xc, dtc, bc, cc = inp
        acum = jnp.cumsum(dtc * a, axis=1)
        diff = acum[:, :, None] - acum[:, None, :]
        decay = jnp.exp(jnp.where(causal, diff, -jnp.inf))
        cb = jnp.einsum('blgn,bsgn->blsg', cc, bc)
        scores = cb[..., None] * decay * dtc[:, None]
        y = jnp.einsum('blsge,bsgep->blgep', scores, xc)
        y = y + jnp.einsum('blgn,bgepn->blgep', cc, state) * jnp.exp(acum)[..., None]
        w_end = jnp.exp(acum[:, -1:] - acum) * dtc
        state = state * jnp.exp(acum[:, -1])[..., None, None] + jnp.einsum('bsge,bsgep,bsgn->bgepn', w_end, xc, bc)
        return state, y

    state0 = jnp.zeros((bsz, g, e, p, n), jnp.float32)
    _, ys = lax.scan(step, state0, (to_chunks(x, SSD_CHUNK), to_chunks(dt, SSD_CHUNK),
                                    to_chunks(b_in, SSD_CHUNK), to_chunks(c_in, SSD_CHUNK)))
    return from_chunks(ys)

def rope_tables(s):
    inv = 1.0 / (ROPE_THETA ** (jnp.arange(0, MLA_ROPE, 2, dtype=jnp.float32) / MLA_ROPE))
    ang = jnp.arange(s, dtype=jnp.float32)[:, None] * inv[None, :]
    return jnp.cos(ang), jnp.sin(ang)

def apply_rope(t, cos, sin):
    t1, t2 = jnp.split(t.astype(jnp.float32), 2, axis=-1)
    return jnp.concatenate([t1 * cos - t2 * sin, t1 * sin + t2 * cos], axis=-1).astype(t.dtype)

def mla_attention(q_a, kv_a, q_norm_w, w_qb, kv_norm_w, w_kvb):
    bsz, s, _ = q_a.shape
    q = jnp.einsum('bsr,rf->bsf', rmsnorm(q_a, q_norm_w), w_qb).reshape(bsz, s, MLA_HEADS, MLA_NOPE + MLA_ROPE)
    q_nope, q_rope = q[..., :MLA_NOPE], q[..., MLA_NOPE:]
    c_kv = rmsnorm(kv_a[..., :MLA_KV_LORA], kv_norm_w)
    k_rope = kv_a[..., MLA_KV_LORA:]
    cos, sin = rope_tables(s)
    q_rope = apply_rope(q_rope, cos[None, :, None], sin[None, :, None])
    k_rope = apply_rope(k_rope, cos[None], sin[None])
    w_kvb = w_kvb.reshape(MLA_KV_LORA, MLA_HEADS, MLA_NOPE + MLA_V)
    w_uk, w_uv = w_kvb[..., :MLA_NOPE], w_kvb[..., MLA_NOPE:]
    q_lat = jnp.einsum('bshd,chd->bshc', q_nope, w_uk)
    scale = (MLA_NOPE + MLA_ROPE) ** -0.5

    def block(qs):
        ql, qr = qs
        sc = jnp.einsum('bqhc,bkc->bhqk', ql, c_kv) + jnp.einsum('bqhr,bkr->bhqk', qr, k_rope)
        pr = jax.nn.softmax(sc.astype(jnp.float32) * scale, axis=-1).astype(c_kv.dtype)
        return jnp.einsum('bhqk,bkc->bqhc', pr, c_kv)

    o_lat = from_chunks(lax.map(block, (to_chunks(q_lat, MLA_QBLOCK), to_chunks(q_rope, MLA_QBLOCK))))
    o = jnp.einsum('bshc,chd->bshd', o_lat, w_uv)
    return o.reshape(bsz, s, MLA_HEADS * MLA_V)

def ssd_mla_mixer(h, w_in, conv_w, conv_b, a_log, dt_bias, d_skip, ssd_norm_w,
                  q_norm_w, w_qb, kv_norm_w, w_kvb, w_out):
    bsz, s, _ = h.shape
    f32 = jnp.float32
    proj = jnp.einsum('bsd,df->bsf', h, w_in)
    o1 = SSD_INNER
    o2 = o1 + SSD_CONV_DIM
    o3 = o2 + 2 * SSD_HEADS
    o4 = o3 + MLA_Q_LORA
    z, xbc, dt_raw, q_a, kv_a = jnp.split(proj, [o1, o2, o3, o4], axis=-1)
    xbc = jax.nn.silu(dwconv_centred(xbc, conv_w, conv_b))
    xs, b_in, c_in = jnp.split(xbc, [SSD_INNER, SSD_INNER + SSD_GROUPS * SSD_STATE], axis=-1)
    xs = xs.reshape(bsz, s, SSD_GROUPS, SSD_HPG, SSD_HEAD_DIM).astype(f32)
    b_in = b_in.reshape(bsz, s, SSD_GROUPS, SSD_STATE).astype(f32)
    c_in = c_in.reshape(bsz, s, SSD_GROUPS, SSD_STATE).astype(f32)
    dt = jax.nn.softplus(dt_raw.astype(f32).reshape(bsz, s, 2, SSD_GROUPS, SSD_HPG)
                         + dt_bias.astype(f32).reshape(2, SSD_GROUPS, SSD_HPG))
    a = -jnp.exp(a_log.astype(f32)).reshape(2, SSD_GROUPS, SSD_HPG)
    y_fwd = ssd_scan(xs, dt[:, :, 0], a[0], b_in, c_in)
    y_bwd = flip_seq(ssd_scan(flip_seq(xs), flip_seq(dt[:, :, 1]), a[1], flip_seq(b_in), flip_seq(c_in)))
    y = y_fwd + y_bwd + xs * d_skip.astype(f32).reshape(SSD_GROUPS, SSD_HPG)[:, :, None]
    gate = jax.nn.silu(z.astype(f32)).reshape(bsz, s, SSD_GROUPS, SSD_INNER // SSD_GROUPS)
    y = y.reshape(bsz, s, SSD_GROUPS, SSD_INNER // SSD_GROUPS) * gate
    y = rmsnorm(y, ssd_norm_w.reshape(SSD_GROUPS, SSD_INNER // SSD_GROUPS)).reshape(bsz, s, SSD_INNER).astype(h.dtype)
    o_mla = mla_attention(q_a, kv_a, q_norm_w, w_qb, kv_norm_w, w_kvb)
    return jnp.einsum('bsf,fd->bsd', jnp.concatenate([y, o_mla], axis=-1), w_out)

def gla_scan(q, k, v, g):
    bsz, _, nh, dk = q.shape
    dv = v.shape[-1]
    causal = jnp.tril(jnp.ones((GLA_CHUNK, GLA_CHUNK), dtype=bool))[None, :, :, None]

    def step(state, inp):
        qc, kc, vc, gc = inp
        gcum = jnp.cumsum(gc, axis=1)
        q_t = qc * jnp.exp(gcum)
        k_t = kc * jnp.exp(-gcum)
        att = jnp.where(causal, jnp.einsum('blhk,bshk->blsh', q_t, k_t), 0.0)
        o = jnp.einsum('blsh,bshv->blhv', att, vc) + jnp.einsum('blhk,bhkv->blhv', q_t, state)
        g_end = gcum[:, -1]
        state = state * jnp.exp(g_end)[..., None] + jnp.einsum('bshk,bshv->bhkv', kc * jnp.exp(g_end[:, None] - gcum), vc)
        return state, o

    state0 = jnp.zeros((bsz, nh, dk, dv), jnp.float32)
    _, os_ = lax.scan(step, state0, (to_chunks(q, GLA_CHUNK), to_chunks(k, GLA_CHUNK),
                                     to_chunks(v, GLA_CHUNK), to_chunks(g, GLA_CHUNK)))
    return from_chunks(os_)

def gla_mixer(h, w_in, w_gk2, b_gk, norm_w, w_out):
    bsz, s, _ = h.shape
    f32 = jnp.float32
    proj = jnp.einsum('bsd,df->bsf', h, w_in)
    q, k, v, g, lr = jnp.split(proj, [GLA_KEY, 2 * GLA_KEY, 2 * GLA_KEY + GLA_VAL, 2 * GLA_KEY + 2 * GLA_VAL], axis=-1)
    lr = lr.reshape(bsz, s, 2, GLA_GATE_RANK).astype(f32)
    gk = jax.nn.log_sigmoid(jnp.einsum('bsdr,drk->bsdk', lr, w_gk2.astype(f32)) + b_gk.astype(f32)) / GLA_GATE_NORM
    gk = gk.reshape(bsz, s, 2, GLA_HEADS, GLA_HK)
    q = q.reshape(bsz, s, GLA_HEADS, GLA_HK).astype(f32) * GLA_HK ** -0.5
    k = k.reshape(bsz, s, GLA_HEADS, GLA_HK).astype(f32)
    v = v.reshape(bsz, s, GLA_HEADS, GLA_HV).astype(f32)
    o = gla_scan(q, k, v, gk[:, :, 0]) + flip_seq(gla_scan(flip_seq(q), flip_seq(k), flip_seq(v), flip_seq(gk[:, :, 1])))
    o = rmsnorm(o, norm_w) * jax.nn.silu(g.reshape(bsz, s, GLA_HEADS, GLA_HV).astype(f32))
    return jnp.einsum('bsf,fd->bsd', o.reshape(bsz, s, GLA_VAL).astype(h.dtype), w_out)

def conv_ffn(h, w_in, conv_w, conv_b, w_out):
    u = dwconv_centred(jnp.einsum('bsd,df->bsf', h, w_in), conv_w, conv_b)
    gate, up = jnp.split(u, 2, axis=-1)
    return jnp.einsum('bsf,fd->bsd', jax.nn.gelu(gate, approximate=True) * up, w_out)

def trunk(x, p):
    for layer in range(DEPTH):
        i = layer // 2
        h = rmsnorm(x, p['norm_w'][layer, 0])
        if layer % 2 == 0:
            m = ssd_mla_mixer(h, p['hyb_w_in'][i], p['ssd_conv_w'][i], p['ssd_conv_b'][i], p['ssd_a_log'][i],
                              p['ssd_dt_bias'][i], p['ssd_d'][i], p['ssd_norm_w'][i], p['mla_q_norm_w'][i],
                              p['mla_w_qb'][i], p['mla_kv_norm_w'][i], p['mla_w_kvb'][i], p['hyb_w_out'][i])
        else:
            m = gla_mixer(h, p['gla_w_in'][i], p['gla_w_gk2'][i], p['gla_b_gk'][i], p['gla_norm_w'][i], p['gla_w_out'][i])
        x = x + rmsnorm(m, p['norm_w'][layer, 1])
        h = rmsnorm(x, p['norm_w'][layer, 2])
        f = conv_ffn(h, p['ffn_w_in'][layer], p['ffn_conv_w'][layer], p['ffn_conv_b'][layer], p['ffn_w_out'][layer])
        x = x + rmsnorm(f, p['norm_w'][layer, 3])
    return x

def setup_inputs(seed: int = 0) -> dict:
    key = jax.random.key(seed)
    ks = iter(jax.random.split(key, 32))
    f32 = jnp.float32

    def w(shape, fan_in):
        return jax.random.normal(next(ks), shape, f32) * fan_in ** -0.5

    def gain(shape):
        return 1.0 + 0.05 * jax.random.normal(next(ks), shape, f32)

    def small(shape):
        return 0.01 * jax.random.normal(next(ks), shape, f32)

    x_prompt = jax.random.normal(next(ks), (BATCH, SEQ, D_MODEL), f32)
    x_sample = jax.random.normal(next(ks), (DEC_BATCH, DEC_SEQ, D_MODEL), f32)
    hyb_w_in = w((N_EVEN, D_MODEL, EVEN_IN), D_MODEL)
    ssd_conv_w = w((N_EVEN, SSD_CONV, SSD_CONV_DIM), SSD_CONV)
    ssd_conv_b = small((N_EVEN, SSD_CONV_DIM))
    ssd_a_log = jnp.log(jax.random.uniform(next(ks), (N_EVEN, 2, SSD_HEADS), f32, 1.0, 16.0))
    dt0 = jnp.exp(jax.random.uniform(next(ks), (N_EVEN, 2, SSD_HEADS), f32, float(np.log(1e-3)), float(np.log(1e-1))))
    ssd_dt_bias = dt0 + jnp.log(-jnp.expm1(-dt0))
    ssd_d = 1.0 + 0.1 * jax.random.normal(next(ks), (N_EVEN, SSD_HEADS), f32)
    ssd_norm_w = gain((N_EVEN, SSD_INNER))
    mla_q_norm_w = gain((N_EVEN, MLA_Q_LORA))
    mla_w_qb = w((N_EVEN, MLA_Q_LORA, MLA_HEADS * (MLA_NOPE + MLA_ROPE)), MLA_Q_LORA)
    mla_kv_norm_w = gain((N_EVEN, MLA_KV_LORA))
    mla_w_kvb = w((N_EVEN, MLA_KV_LORA, MLA_HEADS * (MLA_NOPE + MLA_V)), MLA_KV_LORA)
    hyb_w_out = w((N_EVEN, EVEN_MIX, D_MODEL), EVEN_MIX)
    gla_w_in = w((N_ODD, D_MODEL, ODD_IN), D_MODEL)
    gla_w_gk2 = w((N_ODD, 2, GLA_GATE_RANK, GLA_KEY), GLA_GATE_RANK)
    gla_b_gk = 0.1 * jax.random.normal(next(ks), (N_ODD, 2, GLA_KEY), f32)
    gla_norm_w = gain((N_ODD, GLA_HV))
    gla_w_out = w((N_ODD, GLA_VAL, D_MODEL), GLA_VAL)
    ffn_w_in = w((DEPTH, D_MODEL, 2 * D_FF), D_MODEL)
    ffn_conv_w = w((DEPTH, FFN_CONV, 2 * D_FF), FFN_CONV)
    ffn_conv_b = small((DEPTH, 2 * D_FF))
    ffn_w_out = w((DEPTH, D_FF, D_MODEL), D_FF)
    norm_w = gain((DEPTH, 4, D_MODEL))
    return {'x_prompt': x_prompt, 'x_sample': x_sample,
            'hyb_w_in': hyb_w_in, 'ssd_conv_w': ssd_conv_w, 'ssd_conv_b': ssd_conv_b,
            'ssd_a_log': ssd_a_log, 'ssd_dt_bias': ssd_dt_bias, 'ssd_d': ssd_d, 'ssd_norm_w': ssd_norm_w,
            'mla_q_norm_w': mla_q_norm_w, 'mla_w_qb': mla_w_qb, 'mla_kv_norm_w': mla_kv_norm_w,
            'mla_w_kvb': mla_w_kvb, 'hyb_w_out': hyb_w_out,
            'gla_w_in': gla_w_in, 'gla_w_gk2': gla_w_gk2, 'gla_b_gk': gla_b_gk,
            'gla_norm_w': gla_norm_w, 'gla_w_out': gla_w_out,
            'ffn_w_in': ffn_w_in, 'ffn_conv_w': ffn_conv_w, 'ffn_conv_b': ffn_conv_b, 'ffn_w_out': ffn_w_out,
            'norm_w': norm_w}

def reference(x_prompt, x_sample, hyb_w_in, ssd_conv_w, ssd_conv_b, ssd_a_log, ssd_dt_bias, ssd_d, ssd_norm_w,
              mla_q_norm_w, mla_w_qb, mla_kv_norm_w, mla_w_kvb, hyb_w_out,
              gla_w_in, gla_w_gk2, gla_b_gk, gla_norm_w, gla_w_out,
              ffn_w_in, ffn_conv_w, ffn_conv_b, ffn_w_out, norm_w):
    params = dict(hyb_w_in=hyb_w_in, ssd_conv_w=ssd_conv_w, ssd_conv_b=ssd_conv_b, ssd_a_log=ssd_a_log,
                  ssd_dt_bias=ssd_dt_bias, ssd_d=ssd_d, ssd_norm_w=ssd_norm_w,
                  mla_q_norm_w=mla_q_norm_w, mla_w_qb=mla_w_qb, mla_kv_norm_w=mla_kv_norm_w,
                  mla_w_kvb=mla_w_kvb, hyb_w_out=hyb_w_out,
                  gla_w_in=gla_w_in, gla_w_gk2=gla_w_gk2, gla_b_gk=gla_b_gk, gla_norm_w=gla_norm_w,
                  gla_w_out=gla_w_out, ffn_w_in=ffn_w_in, ffn_conv_w=ffn_conv_w, ffn_conv_b=ffn_conv_b,
                  ffn_w_out=ffn_w_out, norm_w=norm_w)
    y_prompt = trunk(x_prompt, params)
    y_sample = trunk(x_sample, params)
    return (y_prompt, y_sample)


_drawn_inputs = setup_inputs


def setup_inputs(seed=0):
    import zlib

    import numpy as np

    out = dict(_drawn_inputs(seed))
    spreads = {}
    factors = {'ssd_conv_b': 13.257,
     'mla_q_norm_w': 7.316,
     'mla_kv_norm_w': 4.346,
     'ffn_conv_b': 4.053,
     'ssd_d': 4.194,
     'ssd_norm_w': 4.375}
    for name, (base, spread) in spreads.items():
        noise = np.random.default_rng([zlib.crc32(name.encode()), seed]).standard_normal(out[name].shape)
        drawn = base * np.exp(spread * noise) if base else spread * noise
        out[name] = __import__('jax').numpy.asarray(drawn.astype(out[name].dtype))
    for name, factor in factors.items():
        out[name] = (out[name] * factor).astype(out[name].dtype)
    return out
```

```python
from contextlib import ExitStack

import concourse.bass as bass
import numpy as np
from concourse import mybir

F32, F32R = mybir.dt.float32, mybir.dt.float32r
ACT, ALU, AX = mybir.ActivationFunctionType, mybir.AluOpType, mybir.AxisListType

P = 128
D = 1024
KD = D // P
SEQ, NREQ = 256, 2
T = SEQ * NREQ
NBLK = T // P
EPS = 1e-6

HEADS, HDIM = 16, 64
GHEADS = 8
QLORA, NOPE, ROPE, MHEADS = 256, 128, 64, 8
QSCALE = float(NOPE + ROPE) ** -0.5
GLA_HEADS, CH = 4, 64
NCH = SEQ // CH
GK_NORM = 1.0 / 16.0
QG = float(P) ** -0.5
FF = 2816 // P

STREAM = [("hin", 24, KD), ("mla", 4, 10), ("hout", 16, KD), ("fin0", 2 * FF, KD), ("fout0", 16, FF // 2),
          ("gin", 25, KD), ("gout", 8, KD), ("fin1", 2 * FF, KD), ("fout1", 16, FF // 2)]
BASE, _at = {}, 0
for _n, _c, _k in STREAM:
    BASE[_n] = _at
    _at += _c
TOTAL = _at
KT_OF = [k for _, c, k in STREAM for _ in range(c)]
KT_MAX = max(KT_OF)

PCOLS = {}
_at = 0
for _n, _c in [("norm", 64), ("cw", 36), ("cb", 12), ("dtb", 1), ("alog", 1), ("dskip", 8), ("ssdn", 8), ("qn", 2),
               ("kvn", 1), ("bgk", 8), ("glan", 2), ("fw0", 132), ("fw1", 132), ("fb0", 44), ("fb1", 44), ("eps", 1)]:
    PCOLS[_n] = _at
    _at += _c
NPARAM = _at

CCOLS = {"ident": 0, "maskF": 128, "maskB": 512, "rot": 896, "seldup": 1024, "selrot": 1152}
NCONST = 1280


def build_program(nc, x_in, w_stream, w_gk, params, consts, rope, glac, out):
    ctx = ExitStack()
    with ctx:
        sems = {}

        def sem(name):
            if name not in sems:
                sems[name] = ctx.enter_context(nc.semaphore(name))
            return sems[name]

        def sb(name, cols, dtype=F32, stack=ctx, parts=P):
            return stack.enter_context(nc.sbuf_tensor(name, [parts, cols], dtype))

        xres = sb("xres", KD * T)
        raw = [sb(f"raw{i}", KT_MAX * P) for i in range(2)]
        whi = [sb(f"whi{i}", KT_MAX * P, F32R) for i in range(2)]
        wlo = [sb(f"wlo{i}", KT_MAX * P, F32R) for i in range(2)]
        rstd = sb("rstd", T)
        sqacc = sb("sqacc", T)
        ubuf = [sb(f"ubuf{i}", T) for i in range(2)]
        cbuf = [sb(f"cbuf{i}", T) for i in range(4)]
        par = sb("par", NPARAM)
        ident = sb("ident", P)
        ones = sb("ones", SEQ)
        small = sb("small", 4)
        with ExitStack() as s:
            xw_hi = sb("xw_hi", KD * T, F32R, s)
            xw_lo = sb("xw_lo", KD * T, F32R, s)
        with ExitStack() as s:
            m_ffn = sb("m_ffn", KD * T, F32, s)
        with ExitStack() as s:
            xdt = sb("xdt", 2 * NBLK * D, F32, s)
        sb("xw_region", 2 * KD * T)

        with ExitStack() as s:
            with ExitStack() as q:
                vp = [None, sb("vp1", NBLK * 2 * P, F32, q)]
                prob = [None, sb("prob1", 4 * SEQ, F32, q)]
                probT = sb("probT", 4 * SEQ, F32, q)
            zbuf = sb("zbuf", KD * T, F32, s)
            mq = sb("mq", 4 * T, F32, s)
            co_hi = sb("co_hi", MHEADS * T, F32R, s)
            co_lo = sb("co_lo", MHEADS * T, F32R, s)
            cosin = sb("cosin", 2 * T, F32, s)
            cst = sb("cst", NCONST - P, F32, s)
            with ExitStack() as q:
                xbc = sb("xbc", 12 * T, F32, q)
                ytok = sb("ytok", NBLK * D, F32, q)
            with ExitStack() as q:
                m_hyb = sb("m_hyb", KD * T, F32, q)
            with ExitStack() as q:
                qn_hi = sb("qn_hi", 2 * T, F32R, q)
                qn_lo = sb("qn_lo", 2 * T, F32R, q)
                ckv_hi = sb("ckv_hi", T, F32R, q)
                ckv_lo = sb("ckv_lo", T, F32R, q)
                kre = [sb(f"kre{i}", T, F32, q) for i in range(2)]
                qh = [sb(f"qh{i}", T, F32, q) for i in range(2)]
                qr = sb("qr", T, F32, q)
                kh = [sb(f"kh{i}", T, F32, q) for i in range(2)]
                vp0 = sb("vp0", NBLK * 2 * P, F32, q)
                prob0 = sb("prob0", 4 * SEQ, F32, q)
                stat = sb("stat", 32, F32, q)
            vp[0], prob[0] = vp0, prob0
        with ExitStack() as s:
            sb("zbuf_mq", 12 * T, F32, s)
            ebuf = [sb(f"ebuf{i}", 3 * T, F32, s) for i in range(2)]
            cbm = sb("cbm", 4 * 3 * SEQ, F32, s)
            at_hi = sb("at_hi", T, F32R, s, 64)
            at_lo = sb("at_lo", T, F32R, s, 64)
            onehot = [sb(f"onehot{i}", 2 * P, F32R, s, 64) for i in range(2)]
            dtt = sb("dtt", NBLK * 64, F32, s)
            acol = sb("acol", NBLK * 64, F32, s)
        with ExitStack() as s:
            g_hi = sb("g_hi", FF * T, F32R, s)
            g_lo = sb("g_lo", FF * T, F32R, s)
        with ExitStack() as s:
            gqkv = sb("gqkv", 16 * T, F32, s)
            gg = sb("gg", 8 * T, F32, s)
            with ExitStack() as q:
                vtok = sb("vtok", NBLK * D, F32, q)
                lrk = sb("lrk", T, F32, q)
                gcum = sb("gcum", T, F32, q)
                gend = sb("gend", NREQ * NCH, F32, q)
                ek = sb("ek", T, F32, q)
                ecr = sb("ecr", NREQ * 6 * CH, F32, q)
                qt = [sb(f"qt{i}", T, F32, q) for i in range(2)]
                kk = [sb(f"kk{i}", NREQ * NCH * SEQ, F32, q) for i in range(2)]
                att = sb("att", NREQ * 2 * SEQ, F32, q)
                dg = sb("dg", NREQ * SEQ, F32, q)
                wgk = sb("wgk", 2 * 4 * P, F32, q)
                gmask = sb("gmask", T + CH, F32, q)
                tri = sb("tri", 2 * P, F32, q)
            with ExitStack() as q:
                m_gla = sb("m_gla", KD * T, F32, q)
        bank = [ctx.enter_context(nc.psum_tensor(f"bank{i}", [P, T], F32)) for i in range(8)]

        def ck(t, c, n=1):
            return t[:, bass.ds(c * T, n * T)]

        def prm(name, c=0):
            return par[:, bass.ds(PCOLS[name] + c, 1)]

        def con(name, n=P):
            return cst[:, CCOLS[name] - P:CCOLS[name] - P + n]

        def req(ap):
            return ap.rearrange("p (r s) -> p r s", r=NREQ)

        ADDS = {"res_hi": 8, "res_sq": 8, "res_lo": 8, "res_acc": 7, "res_ss": 1, "res_sd": 1, "res_rstd": 1,
                "res_rstdm": 1, "res_t": 8, "res_x": 8, "out_m": 8, "out_sq": 8, "out_acc": 7, "out_ss": 1,
                "out_sd": 1, "fin_u": 2 * FF, "fin_mid": 2 * FF, "fin_taps": 4 * FF, "fin_gelu": FF,
                "fin_prod": FF, "fin_hi": FF, "fin_lo": FF}
        FROM_START = ("res_hi", "res_sq", "res_lo", "res_acc", "res_ss", "res_sd", "res_rstd")

        def of(name, k):
            return ADDS[name] * (k + 1 if name in FROM_START else k)

        raw_in = [sem("raw_in0"), sem("raw_in1")]
        w_hi, w_lo, mm = sem("w_hi"), sem("w_lo"), sem("mm_block")

        def turns(eng, t0, t1, body):
            body(t0, t0)
            if t1 - t0 > 3:
                with eng.Fori(t0 + 1, t1) as t:
                    body(t, t0 + 1)
            else:
                for t in range(t0 + 1, t1):
                    body(t, t)

        def hi(act, base, j, fj):
            f = base + fj
            if f >= TOTAL:
                return
            s, n = f % 2, KT_OF[f] * P
            act.wait_ge(raw_in[s], (j - fj) * 8 + (f // 2 + 1) * 16)
            if f >= 2:
                act.wait_ge(mm, base + j - 1)
            nc.scalar.activation(whi[s][:, 0:n], raw[s][:, 0:n], ACT.Copy).then_inc(w_hi, 1)

        def lo(pool, base, j, fj):
            f = base + fj
            if f >= TOTAL:
                return
            s, n = f % 2, KT_OF[f] * P
            pool.wait_ge(w_hi, base + j + 1)
            nc.gpsimd.tensor_tensor(wlo[s][:, 0:n], raw[s][:, 0:n], whi[s][:, 0:n].bitcast(F32),
                                    ALU.subtract).then_inc(w_lo, 1)

        def product(pe, base, j, fj, out_ap, a_hi, a_lo, kts=None, k0=0, w0=0, start=True, stop=True, by_chunk=None,
                    last_of_block=True, wait=True):
            f = base + fj
            s = f % 2
            kts = KT_OF[f] if kts is None else kts
            if wait:
                pe.wait_ge(w_lo, base + j + 1)
            for k in range(kts):
                if by_chunk is not None:
                    pe.wait_ge(sem(by_chunk[0]), of(*by_chunk) + k0 + k + 1)
                ah, al = ck(a_hi, k0 + k), ck(a_lo, k0 + k)
                wh, wl = whi[s][:, (w0 + k) * P:(w0 + k + 1) * P], wlo[s][:, (w0 + k) * P:(w0 + k + 1) * P]
                nc.tensor.matmul(out_ap, wh, ah, start=start and k == 0, stop=False)
                nc.tensor.matmul(out_ap, wh, al, start=False, stop=False)
                last = nc.tensor.matmul(out_ap, wl, ah, start=False, stop=stop and k == kts - 1)
            if last_of_block:
                last.then_inc(mm, 1)
            return last

        def m_norm(k):
            return (k // 2) * 32 + (k % 2) * 16 + 8

        def x_norm(k):
            return ((k + 1) // 2) * 32 + ((k + 1) % 2) * 16

        def pe_out(pe, k, name, per, a_of_block):
            base = BASE[name]

            def body(t, ft):
                for u in range(2):
                    c, fc = 2 * t + u, 2 * ft + u
                    if fc >= 2:
                        pe.wait_ge(sem("out_sq"), of("out_sq", k) + c - 1)
                    for b in range(per):
                        src_hi, src_lo, k0, ready = a_of_block(b)
                        if ready is not None and fc == 0:
                            for stage, n in ready:
                                pe.wait_ge(sem(stage), n)
                        product(pe, base, c * per + b, fc * per + b, bank[2 + u][:], src_hi, src_lo, k0=k0,
                                start=b == 0, stop=b == per - 1)
            turns(pe, 0, KD // 2, body)
            pe.wait_ge(sem("out_acc"), of("out_acc", k) + KD - 1)
            nc.tensor.matmul(bank[7][:], ones[:, 0:P], sqacc[:], start=True, stop=True).then_inc(sem("out_ss"), 1)

        def act_out(act, k, name, per, m_tile):
            base = BASE[name]

            def body(t, ft):
                for u in range(2):
                    c, fc = 2 * t + u, 2 * ft + u
                    for b in range(per):
                        hi(act, base, c * per + b + 2, fc * per + b + 2)
                    act.wait_ge(mm, base + (c + 1) * per)
                    nc.scalar.activation(ck(m_tile, c), bank[2 + u][:], ACT.Copy).then_inc(sem("out_m"), 1)
                    if fc > 2:
                        act.wait_ge(sem("out_acc"), of("out_acc", k) + c - 2)
                    nc.scalar.activation(sqacc[:] if fc == 0 else cbuf[u][:], bank[2 + u][:],
                                         ACT.Square).then_inc(sem("out_sq"), 1)
            body(0, 0)
            body(1, 1)
            body(2, 2)
            body(3, 3)
            act.wait_ge(sem("out_ss"), of("out_ss", k) + 1)
            nc.scalar.activation(ubuf[0][:], bank[7][:], ACT.Sqrt, bias=prm("eps"),
                                 scale=1.0 / D).then_inc(sem("out_sd"), 1)

        def pool_add_square(pool, k, what, c, fc, u):
            pool.wait_ge(sem(f"{what}_sq"), of(f"{what}_sq", k) + c + 1)
            if fc > 1:
                pool.wait_ge(sem(f"{what}_acc"), of(f"{what}_acc", k) + c - 1)
            nc.gpsimd.tensor_tensor(sqacc[:], sqacc[:], cbuf[u][:], ALU.add).then_inc(sem(f"{what}_acc"), 1)

        def pool_out(pool, k, name, per):
            base = BASE[name]
            for c in range(KD):
                for b in range(per):
                    lo(pool, base, c * per + b + 2, c * per + b + 2)
                if c:
                    pool_add_square(pool, k, "out", c, c, c % 2)

        def dve_res(dve, k, m_tile):
            if k >= 0:
                dve.wait_ge(sem("out_sd"), of("out_sd", k) + 1)
                nc.vector.reciprocal(rstd[:], ubuf[0][:]).then_inc(sem("res_rstdm"), 1)
                dve.wait_ge(sem("res_rstdm"), of("res_rstdm", k) + 1)
                dve.wait_ge(sem("out_m"), of("out_m", k) + KD)

            def low(c):
                dve.wait_ge(sem("res_hi"), of("res_hi", k) + c + 1)
                nc.vector.scalar_tensor_tensor(out=ck(xw_lo, c), in0=ck(xres, c), scalar=prm("norm", x_norm(k) + c),
                                               in1=ck(xw_hi, c).bitcast(F32), op0=ALU.mult,
                                               op1=ALU.subtract).then_inc(sem("res_lo"), 1)
            for c in range(KD):
                if k >= 0:
                    if c > 1:
                        dve.wait_ge(sem("res_x"), of("res_x", k) + c - 1)
                    m = cbuf[2 + c % 2]
                    nc.vector.scalar_tensor_tensor(out=m[:], in0=ck(m_tile, c), scalar=prm("norm", m_norm(k) + c),
                                                   in1=rstd[:], op0=ALU.mult, op1=ALU.mult).then_inc(sem("res_t"), 1)
                    dve.wait_ge(sem("res_t"), of("res_t", k) + c + 1)
                    nc.vector.tensor_tensor(ck(xres, c), ck(xres, c), m[:], ALU.add).then_inc(sem("res_x"), 1)
                if k < 3 and c:
                    low(c - 1)
            if k < 3:
                low(KD - 1)
            if k < 3:
                dve.wait_ge(sem("res_sd"), of("res_sd", k) + 1)
                nc.vector.reciprocal(rstd[:], ubuf[0][:]).then_inc(sem("res_rstd"), 1)
                dve.wait_ge(sem("res_rstd"), of("res_rstd", k) + 1)

        def act_res(act, k):
            for c in range(KD):
                if k < 0:
                    act.wait_ge(sem(f"x_in{c}"), 16)
                    if c == 0:
                        act.wait_ge(sem("par_in"), 16)
                else:
                    act.wait_ge(sem("res_x"), of("res_x", k) + c + 1)
                nc.scalar.activation(ck(xw_hi, c), ck(xres, c), ACT.Copy,
                                     scale=prm("norm", x_norm(k) + c)).then_inc(sem("res_hi"), 1)
                if c > 2:
                    act.wait_ge(sem("res_acc"), of("res_acc", k) + c - 2)
                nc.scalar.activation(sqacc[:] if c == 0 else cbuf[c % 2][:], ck(xres, c),
                                     ACT.Square).then_inc(sem("res_sq"), 1)
            act.wait_ge(sem("res_ss"), of("res_ss", k) + 1)
            nc.scalar.activation(ubuf[0][:], bank[7][:], ACT.Sqrt, bias=prm("eps"),
                                 scale=1.0 / D).then_inc(sem("res_sd"), 1)

        def pool_res(pool, k):
            for c in range(1, KD):
                pool_add_square(pool, k, "res", c, c, c % 2)

        def pe_res(pe, k):
            pe.wait_ge(sem("res_acc"), of("res_acc", k) + KD - 1)
            nc.tensor.matmul(bank[7][:], ones[:, 0:P], sqacc[:], start=True, stop=True).then_inc(sem("res_ss"), 1)

        def dve_taps(dve, src, dst, w, n, of, center, taps, count):
            dve.wait_ge(sem(center), count + 1)
            nc.vector.scalar_tensor_tensor(out=req(dst[:])[:, :, 1:SEQ], in0=req(src[:])[:, :, 0:SEQ - 1],
                                           scalar=prm(w, of), in1=req(dst[:])[:, :, 1:SEQ], op0=ALU.mult,
                                           op1=ALU.add).then_inc(sem(taps), 1)
            dve.wait_ge(sem(taps), 2 * count + 1)
            nc.vector.scalar_tensor_tensor(out=req(dst[:])[:, :, 0:SEQ - 1], in0=req(src[:])[:, :, 1:SEQ],
                                           scalar=prm(w, of + 2 * n), in1=req(dst[:])[:, :, 0:SEQ - 1], op0=ALU.mult,
                                           op1=ALU.add).then_inc(sem(taps), 1)

        def scaled(dve, out_ap, src):
            return nc.vector.tensor_tensor(out_ap, src[:], rstd[:], ALU.mult)

        def pe_fin(pe, l):
            base = BASE[f"fin{l}"]
            r = 2 * l

            def body(t, ft):
                for u in range(2):
                    if ft >= 1:
                        pe.wait_ge(sem("fin_u"), of("fin_u", l) + 2 * t - 1 + u)
                    product(pe, base, 2 * t + u, 2 * ft + u, bank[u][:], xw_hi, xw_lo,
                            by_chunk=("res_lo", r) if ft == 0 and u == 0 else None)
                    if ft == 0 and u == 0:
                        pe_res(pe, r)
            turns(pe, 0, FF, body)

        def act_fin(act, l):
            base = BASE[f"fin{l}"]

            def body(t, ft):
                for u in range(2):
                    j = 2 * t + u
                    hi(act, base, j + 2, 2 * ft + u + 2)
                    act.wait_ge(sem("fin_u"), of("fin_u", l) + j + 1)
                    if u == 0 and ft >= 1:
                        act.wait_ge(sem("fin_prod"), of("fin_prod", l) + t)
                    nc.scalar.activation(cbuf[u][:], ubuf[u][:], ACT.Identity, bias=prm(f"fb{l}", u * FF + t),
                                         scale=prm(f"fw{l}", 2 * FF + u * FF + t)).then_inc(sem("fin_mid"), 1)
                    if u == 0:
                        act.wait_ge(sem("fin_taps"), of("fin_taps", l) + 4 * t + 2)
                        if ft >= 1:
                            act.wait_ge(sem("fin_prod"), of("fin_prod", l) + t)
                        nc.scalar.activation(cbuf[2][:], cbuf[0][:], ACT.Gelu_apprx_tanh).then_inc(
                            sem("fin_gelu"), 1)
                act.wait_ge(sem("fin_prod"), of("fin_prod", l) + t + 1)
                nc.scalar.activation(ck(g_hi, t), cbuf[3][:], ACT.Copy).then_inc(sem("fin_hi"), 1)
            turns(act, 0, FF - 1, body)
            body(FF - 1, FF - 1)

        def dve_fin(dve, l):
            base = BASE[f"fin{l}"]

            def body(t, ft):
                for u in range(2):
                    j = 2 * t + u
                    dve.wait_ge(mm, base + j + 1)
                    if ft >= 1:
                        dve.wait_ge(sem("fin_taps"), of("fin_taps", l) + 2 * j - 2)
                    scaled(dve, ubuf[u][:], bank[u]).then_inc(sem("fin_u"), 1)
                    dve_taps(dve, ubuf[u], cbuf[u], f"fw{l}", 2 * FF, u * FF + t, "fin_mid", "fin_taps",
                             2 * FF * l + j)
                dve.wait_ge(sem("fin_taps"), of("fin_taps", l) + 4 * t + 4)
                dve.wait_ge(sem("fin_gelu"), of("fin_gelu", l) + t + 1)
                if ft >= 1:
                    dve.wait_ge(sem("fin_lo"), of("fin_lo", l) + t)
                nc.vector.tensor_tensor(cbuf[3][:], cbuf[2][:], cbuf[1][:], ALU.mult).then_inc(
                    sem("fin_prod"), 1)
                dve.wait_ge(sem("fin_hi"), of("fin_hi", l) + t + 1)
                nc.vector.tensor_tensor(ck(g_lo, t), cbuf[3][:], ck(g_hi, t).bitcast(F32), ALU.subtract).then_inc(
                    sem("fin_lo"), 1)
            turns(dve, 0, FF, body)

        def pool_fin(pool, l):
            base = BASE[f"fin{l}"]

            def body(t, ft):
                for u in range(2):
                    lo(pool, base, 2 * t + u + 2, 2 * ft + u + 2)
            turns(pool, 0, FF - 1, body)
            body(FF - 1, FF - 1)

        def ffn_operand(l):
            half = FF // 2
            return lambda b: (g_hi, g_lo, b * half, [("fin_lo", of("fin_lo", l) + half * (b + 1))])


        CONV0, Z0 = 2, 8

        def pe_hin(pe):
            base = BASE["hin"]
            pe.wait_ge(sem("ones_set"), 1)

            def body(t, ft):
                for u in range(2):
                    if ft >= 1:
                        pe.wait_ge(sem("hin_u"), 2 * t - 1 + u)
                    product(pe, base, 2 * t + u, 2 * ft + u, bank[u][:], xw_hi, xw_lo,
                            by_chunk=("res_lo", -1) if ft == 0 and u == 0 else None)
                    if ft == 0 and u == 0:
                        pe_res(pe, -1)
            turns(pe, 0, 12, body)

        def act_hin(act):
            base = BASE["hin"]

            def his(t, ft, u):
                hi(act, base, 2 * t + u + 2, 2 * ft + u + 2)

            def conv(t, ft):
                for u in range(2):
                    c, fc = 2 * t + u - 4, 2 * ft + u - 4
                    his(t, ft, u)
                    act.wait_ge(sem("hin_u"), 2 * t + u + 1)
                    if fc >= 2:
                        act.wait_ge(sem("hin_silu"), c - 1)
                    nc.scalar.activation(cbuf[u][:], ubuf[u][:], ACT.Identity, bias=prm("cb", c),
                                         scale=prm("cw", 12 + c)).then_inc(sem("hin_mid"), 1)
                    act.wait_ge(sem("hin_taps"), 2 * c + 2)
                    nc.scalar.activation(ck(xbc, c), cbuf[u][:], ACT.Silu).then_inc(sem("hin_silu"), 1)

            def gate(t, ft):
                for u in range(2):
                    his(t, ft, u)
                    act.wait_ge(sem("hin_u"), 2 * t + u + 1)
                    nc.scalar.activation(ck(zbuf, 2 * t + u - 16), ubuf[u][:], ACT.Silu).then_inc(sem("hin_zsilu"), 1)
            for t in range(CONV0):
                for u in range(2):
                    his(t, t, u)
            turns(act, CONV0, Z0, conv)
            for t in range(Z0, 12):
                gate(t, t)

        def dve_hin(dve):
            base = BASE["hin"]
            for j in range(4):
                dve.wait_ge(mm, base + j + 1)
                if j == 0:
                    dve.wait_ge(sem("res_rstd"), of("res_rstd", -1) + 1)
                scaled(dve, ck(mq, j), bank[j % 2]).then_inc(sem("hin_u"), 1)

            def conv(t, ft):
                for u in range(2):
                    c, fc = 2 * t + u - 4, 2 * ft + u - 4
                    dve.wait_ge(mm, base + 2 * t + u + 1)
                    if fc >= 2:
                        dve.wait_ge(sem("hin_taps"), 2 * c - 2)
                    scaled(dve, ubuf[u][:], bank[u]).then_inc(sem("hin_u"), 1)
                    dve_taps(dve, ubuf[u], cbuf[u], "cw", 12, c, "hin_mid", "hin_taps", c)
            turns(dve, CONV0, Z0, conv)
            for t in range(Z0, 12):
                for u in range(2):
                    dve.wait_ge(mm, base + 2 * t + u + 1)
                    if t == Z0:
                        dve.wait_ge(sem("hin_taps"), 22 + 2 * u)
                    else:
                        dve.wait_ge(sem("hin_zsilu"), 2 * (t - Z0) + u - 1)
                    scaled(dve, ubuf[u][:], bank[u]).then_inc(sem("hin_u"), 1)

        def pool_hin(pool):
            base = BASE["hin"]

            def body(t, ft):
                for u in range(2):
                    lo(pool, base, 2 * t + u + 2, 2 * ft + u + 2)
            turns(pool, 0, 11, body)
            body(11, 11)

        dt_f, dta_f, a_f = (ebuf[0][0:64, i * T:(i + 1) * T] for i in range(3))

        def act_dt(act):
            act.wait_ge(sem("hin_taps"), 24)
            nc.scalar.activation(cbuf[2][0:64, :], mq[0:64, 0:T], ACT.Abs,
                                 bias=prm("dtb")[0:64]).then_inc(sem("dt_act"), 1)
            act.wait_ge(sem("dt_act"), 1)
            nc.scalar.activation(cbuf[2][0:64, :], cbuf[2][0:64, :], ACT.Exp, scale=-1.0).then_inc(sem("dt_act"), 1)
            act.wait_ge(sem("dt_act"), 2)
            nc.scalar.activation(cbuf[3][0:64, :], cbuf[2][0:64, :], ACT.Ln,
                                 bias=ones[0:64, 0:1]).then_inc(sem("dt_act"), 1)
            nc.scalar.activation(small[0:64, 0:1], prm("alog")[0:64], ACT.Exp).then_inc(sem("dt_act"), 1)

        def dve_dt(dve):
            n = [0]

            def step(ins):
                n[0] += 1
                ins.then_inc(sem("dt_dve"), 1)

            def done(k):
                dve.wait_ge(sem("dt_dve"), k)
            step(nc.vector.tensor_scalar(dt_f, mq[0:64, 0:T], prm("dtb")[0:64], 0.0, ALU.add, ALU.max))
            dve.wait_ge(sem("dt_act"), 3)
            done(1)
            step(nc.vector.tensor_tensor(dt_f, dt_f, cbuf[3][0:64, :], ALU.add))
            dve.wait_ge(sem("dt_act"), 4)
            done(2)
            step(nc.vector.tensor_scalar(dta_f, dt_f, small[0:64, 0:1], -1.0, ALU.mult, ALU.mult))
            done(3)
            for r in range(NREQ):
                f = slice(r * SEQ, (r + 1) * SEQ)
                step(nc.vector.tensor_tensor_scan(out=a_f[0:32, f], data0=ones[0:32, 0:SEQ], data1=dta_f[0:32, f],
                                                  initial=0.0, op0=ALU.mult, op1=ALU.add))
                step(nc.vector.tensor_tensor_scan(out=a_f[32:64, f][:, ::-1], data0=ones[32:64, 0:SEQ],
                                                  data1=dta_f[32:64, f][:, ::-1],
                                                  initial=0.0, op0=ALU.mult, op1=ALU.add))
            done(7)
            step(nc.vector.tensor_copy(at_hi[:], a_f))
            done(8)
            step(nc.vector.tensor_tensor(at_lo[:], a_f, at_hi[:].bitcast(F32), ALU.subtract))
            dve.wait_ge(sem("dt_T"), 1)
            by_token = bank[2][:].rearrange("p (b w n) -> p b w n", b=NBLK, w=2)
            step(nc.vector.tensor_copy(dtt[:].rearrange("p (b n) -> p b n", b=NBLK), by_token[:, :, 0, :]))
            acol4 = acol[:].rearrange("p (b n) -> p b n", b=NBLK)
            step(nc.vector.tensor_copy(acol4[:, :, 0:32], by_token[:, :, 1, 0:32]))
            step(nc.vector.tensor_scalar(acol4[:, :, 32:64], by_token[:, :, 1, 32:64], -1.0, None, ALU.mult))
            dve.wait_ge(mm, BASE["hin"] + 24)
            done(12)
            for i in range(2 * NBLK):
                blk, half = i // 2, i % 2
                dve.wait_ge(sem("xs_T"), i + 1)
                for d in range(2):
                    at = (d * NBLK + blk) * D + half * T
                    h0 = blk * 64 + d * 32 + half * 8
                    nc.vector.tensor_tensor(xdt[:, at:at + T].rearrange("p (h e) -> p h e", e=HDIM),
                                            bank[4 + i % 2][:].rearrange("p (h e) -> p h e", e=HDIM),
                                            dtt[:, h0:h0 + 8].unsqueeze(2).broadcast_to([P, 8, HDIM]),
                                            ALU.mult).then_inc(sem("xdt_set"), 1)
            for i in range(4):
                g, r = i // 2, i % 2
                dve.wait_ge(sem("cb_mm"), i + 1)
                ps = bank[6 + i % 2]
                for d, a, b, s0 in ((0, 0, 256, 0), (0, 256, 384, 384), (1, 0, 128, 0), (1, 128, 384, 256)):
                    at = ((g * 2 + d) * 2 + r) * 384
                    nc.vector.tensor_tensor(cbm[:, at + a:at + b], ps[:, s0:s0 + b - a],
                                            con("maskB" if d else "maskF", 384)[:, a:b],
                                            ALU.mult).then_inc(sem("cb_set"), 1)

        def pe_dt(pe):
            pe.wait_ge(sem("dt_dve"), 7)
            for b in range(NBLK):
                for w, src in enumerate((dt_f, a_f)):
                    last = nc.tensor.transpose(bank[2][:, b * P + w * 64:b * P + w * 64 + 64],
                                               src[:, b * P:(b + 1) * P], ident[0:64, 0:64])
            last.then_inc(sem("dt_T"), 1)
            pe.wait_ge(sem("hin_silu"), 12)
            for i in range(2 * NBLK):
                blk, half = i // 2, i % 2
                if i >= 2:
                    pe.wait_ge(sem("xdt_set"), 2 * i - 2)
                for c in range(4):
                    last = nc.tensor.transpose(bank[4 + i % 2][:, c * P:(c + 1) * P],
                                               ck(xbc, half * 4 + c)[:, blk * P:(blk + 1) * P], ident[:])
                last.then_inc(sem("xs_T"), 1)
            for i in range(4):
                g, r = i // 2, i % 2
                if i >= 2:
                    pe.wait_ge(sem("cb_set"), 4 * i - 4)
                for s in range(2):
                    last = nc.tensor.matmul(bank[6 + i % 2][:, s * SEQ:(s + 1) * SEQ],
                                            ck(xbc, 8 + g)[:, r * SEQ + s * P:r * SEQ + (s + 1) * P],
                                            ck(xbc, 10 + g)[:, r * SEQ:(r + 1) * SEQ], start=True, stop=True)
                last.then_inc(sem("cb_mm"), 1)

        TILES = [[(r, s, a, b, l0) for r in range(NREQ) for s, a, b, l0 in t]
                 for t in (((0, 0, 256, 0), (1, 256, 384, P)), ((0, 0, 128, 0), (1, 128, 384, 0)))]

        def dve_ssd(dve):
            def pick(n, v, first):
                if not first:
                    dve.wait_ge(sem("a_mm"), 2 * n - 2)
                for d in range(2):
                    nc.vector.tensor_copy(onehot[v][:, d * P:(d + 1) * P],
                                          ident[0:64, bass.ds(32 * d + n, 1)].to_broadcast([64, P])).then_inc(
                                              sem("onehot_set"), 1)

            def least(n, v, first=False):
                dve.wait_ge(sem("a_mm"), 2 * n + 2)
                if not first:
                    dve.wait_ge(sem("y_mm"), n - 1)
                for r, s, a, b, l0 in TILES[1]:
                    nc.vector.tensor_scalar(ebuf[v][:, 768 + r * 384 + a:768 + r * 384 + b],
                                            bank[2 + v][:, r * SEQ + l0:r * SEQ + l0 + b - a],
                                            acol[:, bass.ds((2 * r + s) * 64 + 32 + n, 1)], 0.0, ALU.add,
                                            ALU.min).then_inc(sem("ssd_min"), 1)

            def m(n, v, g):
                dve.wait_ge(sem("ssd_exp"), 2 * n + 2)
                nc.vector.tensor_tensor(ebuf[v][:], ebuf[v][:], cbm[:, g * 3 * T:(g + 1) * 3 * T],
                                        ALU.mult).then_inc(sem("ssd_m"), 1)
            dve.wait_ge(sem("cb_set"), 16)
            pick(0, 0, True)
            pick(1, 1, True)
            least(0, 0, True)

            def turn(t, g, first=False):
                least(2 * t + 1, 1, first)
                m(2 * t, 0, g)
                pick(2 * t + 2, 0, False)
                least(2 * t + 2, 0)
                m(2 * t + 1, 1, g)
                pick(2 * t + 3, 1, False)
            for g in range(2):
                if g == 0:
                    turn(0, 0, True)
                with dve.Fori(4 * g + 1 - g, 4 * g + 4 - g) as t:
                    turn(t, g)
                if g == 0:
                    for b in (2, 3):
                        dve.wait_ge(sem("y_mm"), 8)
                        nc.vector.tensor_copy(ytok[:, b * D:b * D + T], bank[4 + b][:]).then_inc(sem("ytok_dve"), 1)
            least(15, 1)
            m(14, 0, 1)
            m(15, 1, 1)
            dve.wait_ge(sem("y_mm"), 16)
            for b in (2, 3):
                nc.vector.tensor_copy(ytok[:, b * D + T:(b + 1) * D], bank[4 + b][:]).then_inc(sem("ytok_dve"), 1)
            for c in range(KD):
                dve.wait_ge(sem("y_T"), c + 1)
                nc.vector.scalar_tensor_tensor(out=ck(xbc, c), in0=ck(xbc, c), scalar=prm("dskip", c),
                                               in1=bank[c % 4][:], op0=ALU.mult, op1=ALU.add).then_inc(sem("ssd_y"), 1)
                dve.wait_ge(sem("ssd_y"), 2 * c + 1)
                nc.vector.tensor_tensor(ck(zbuf, c), ck(zbuf, c), ck(xbc, c), ALU.mult).then_inc(sem("ssd_y"), 1)
            for g in range(2):
                dve.wait_ge(sem("ssd_sd"), g + 1)
                nc.vector.reciprocal(ubuf[g][:], ubuf[g][:]).then_inc(sem("ssd_rs"), 1)
            dve.wait_ge(sem("ssd_rs"), 2)
            for c in range(KD):
                nc.vector.tensor_tensor(ck(zbuf, c), ck(zbuf, c), ubuf[c // 4][:], ALU.mult).then_inc(sem("ssd_n"), 1)

        def act_ssd(act):
            def exps(n, v, first):
                act.wait_ge(sem("a_mm"), 2 * n + 2)
                if not first:
                    act.wait_ge(sem("y_mm"), n - 1)
                for r, s, a, b, l0 in TILES[0]:
                    nc.scalar.activation(ebuf[v][:, r * 384 + a:r * 384 + b],
                                         bank[v][:, r * SEQ + l0:r * SEQ + l0 + b - a], ACT.Relu, scale=-1.0,
                                         bias=acol[:, bass.ds((2 * r + s) * 64 + n, 1)]).then_inc(
                                             sem("ssd_rel"), 1)
                act.wait_ge(sem("ssd_rel"), 4 * n + 4)
                nc.scalar.activation(ebuf[v][:, 0:768], ebuf[v][:, 0:768], ACT.Exp, scale=-1.0).then_inc(
                    sem("ssd_exp"), 1)
                act.wait_ge(sem("ssd_min"), 4 * n + 4)
                nc.scalar.activation(ebuf[v][:, 768:1536], ebuf[v][:, 768:1536], ACT.Exp).then_inc(
                    sem("ssd_exp"), 1)
            act.wait_ge(sem("dt_dve"), 12)
            exps(0, 0, True)
            exps(1, 1, True)
            with act.Fori(1, 4) as t:
                exps(2 * t, 0, False)
                exps(2 * t + 1, 1, False)
            act.wait_ge(sem("y_mm"), 8)
            for b in (0, 1):
                nc.scalar.activation(ytok[:, b * D:b * D + T], bank[4 + b][:], ACT.Copy).then_inc(sem("ytok_act"), 1)
            with act.Fori(4, 8) as t:
                exps(2 * t, 0, False)
                exps(2 * t + 1, 1, False)
            act.wait_ge(sem("y_mm"), 16)
            for b in (0, 1):
                nc.scalar.activation(ytok[:, b * D + T:(b + 1) * D], bank[4 + b][:],
                                     ACT.Copy).then_inc(sem("ytok_act"), 1)
            for c in range(KD):
                act.wait_ge(sem("ssd_y"), 2 * c + 2)
                if c >= 4:
                    act.wait_ge(sem("ssd_ss"), c - 3)
                nc.scalar.activation(cbuf[c % 4][:], ck(zbuf, c), ACT.Square).then_inc(sem("ssd_sq"), 1)
            for g in range(2):
                act.wait_ge(sem("ssd_ss"), 4 * g + 4)
                nc.scalar.activation(ubuf[g][:], bank[4 + g][:], ACT.Sqrt, bias=prm("eps"),
                                     scale=2.0 / D).then_inc(sem("ssd_sd"), 1)
            for c in range(KD):
                act.wait_ge(sem("ssd_n"), c + 1)
                nc.scalar.activation(ck(xw_hi, c), ck(zbuf, c), ACT.Copy,
                                     scale=prm("ssdn", c)).then_inc(sem("ssd_hi"), 1)

        def dve_ssd_low(dve):
            for c in range(KD):
                dve.wait_ge(sem("ssd_hi"), c + 1)
                nc.vector.scalar_tensor_tensor(out=ck(xw_lo, c), in0=ck(zbuf, c), scalar=prm("ssdn", c),
                                               in1=ck(xw_hi, c).bitcast(F32), op0=ALU.mult,
                                               op1=ALU.subtract).then_inc(sem("ssd_lo"), 1)

        def pe_ssd(pe):
            def spread(n, v, first):
                pe.wait_ge(sem("onehot_set"), 2 * n + 2)
                if not first:
                    pe.wait_ge(sem("ssd_rel"), 4 * n - 4)
                    pe.wait_ge(sem("ssd_min"), 4 * n - 4)
                for d in range(2):
                    nc.tensor.matmul(bank[2 * d + v][:], onehot[v][:, d * P:(d + 1) * P], at_hi[:],
                                     start=True, stop=False)
                    nc.tensor.matmul(bank[2 * d + v][:], onehot[v][:, d * P:(d + 1) * P], at_lo[:],
                                     start=False, stop=True).then_inc(sem("a_mm"), 1)

            def y(n, v, col):
                pe.wait_ge(sem("ssd_m"), n + 1)
                for r in range(NREQ):
                    for lb in range(2):
                        parts = [(0, s, lb * P if s == 0 else 256) for s in range(lb + 1)]
                        parts += [(1, s, 0 if s == 0 else P + lb * P) for s in range(lb, 2)]
                        for i, (d, s, a) in enumerate(parts):
                            at = (d * 2 + r) * 384 + a
                            last = nc.tensor.matmul(bank[4 + 2 * r + lb][:, bass.ds(col, HDIM)], ebuf[v][:, at:at + P],
                                                    xdt[:, bass.ds((d * NBLK + 2 * r + s) * D + n * HDIM, HDIM)],
                                                    start=i == 0, stop=i == len(parts) - 1)
                last.then_inc(sem("y_mm"), 1)
            pe.wait_ge(sem("dt_dve"), 12)
            spread(0, 0, True)
            spread(1, 1, True)
            for g in range(2):
                if g:
                    pe.wait_ge(sem("ytok_act"), 2)
                    pe.wait_ge(sem("ytok_dve"), 2)
                else:
                    pe.wait_ge(sem("cb_set"), 16)
                with pe.Fori(4 * g, 4 * g + 4 - g) as t:
                    for v in range(2):
                        spread(2 * t + v + 2, v, False)
                        y(2 * t + v, v, (2 * t + v - 8 * g) * HDIM)
            y(14, 0, 6 * HDIM)
            y(15, 1, 7 * HDIM)
            pe.wait_ge(sem("ytok_act"), 4)
            pe.wait_ge(sem("ytok_dve"), 4)
            pe.wait_ge(sem("ssd_exp"), 32)
            for c in range(KD):
                if c >= 4:
                    pe.wait_ge(sem("ssd_y"), 2 * c - 7)
                for b in range(NBLK):
                    last = nc.tensor.transpose(bank[c % 4][:, b * P:(b + 1) * P],
                                               ytok[:, b * D + c * P:b * D + (c + 1) * P], ident[:])
                last.then_inc(sem("y_T"), 1)
            for c in range(KD):
                pe.wait_ge(sem("ssd_sq"), c + 1)
                nc.tensor.matmul(bank[4 + c // 4][:], ones[:, 0:P], cbuf[c % 4][:], start=c % 4 == 0,
                                 stop=c % 4 == 3).then_inc(sem("ssd_ss"), 1)

        def act_mla_prep(act):
            act.wait_ge(sem("ssd_ss"), 8)
            for i, c in enumerate((1, 2, 3)):
                nc.scalar.activation(cbuf[i][:], ck(mq, c), ACT.Square).then_inc(sem("mla_sq"), 1)
            act.wait_ge(sem("ssd_n"), 8)
            for i, n in enumerate((P, QLORA)):
                act.wait_ge(sem("mla_ss"), i + 1)
                nc.scalar.activation(ubuf[i][:], bank[6 + i][:], ACT.Sqrt, bias=prm("eps"),
                                     scale=1.0 / n).then_inc(sem("mla_sd"), 1)
            for i, (dst, w) in enumerate(((ckv_hi[:], prm("kvn")), (ck(qn_hi, 0), prm("qn", 0)),
                                          (ck(qn_hi, 1), prm("qn", 1)))):
                act.wait_ge(sem("mla_n"), i + 1)
                nc.scalar.activation(dst, ck(mq, 1 + i), ACT.Copy, scale=w).then_inc(sem("mla_hi"), 1)

        def dve_mla_low(dve):
            for i, (dst, src, w) in enumerate(((ckv_lo[:], ckv_hi[:], prm("kvn")),
                                               (ck(qn_lo, 0), ck(qn_hi, 0), prm("qn", 0)),
                                               (ck(qn_lo, 1), ck(qn_hi, 1), prm("qn", 1)))):
                dve.wait_ge(sem("mla_hi"), i + 1)
                nc.vector.scalar_tensor_tensor(out=dst, in0=ck(mq, 1 + i), scalar=w, in1=src.bitcast(F32),
                                               op0=ALU.mult, op1=ALU.subtract).then_inc(sem("mla_lo"), 1)

        def pe_mla_prep(pe):
            pe.wait_ge(sem("ssd_y"), 16)
            nc.tensor.matmul(bank[0][:], con("seldup"), ck(mq, 0), start=True, stop=True)
            nc.tensor.matmul(bank[1][:], con("selrot"), ck(mq, 0), start=True, stop=True).then_inc(sem("mla_kr"), 1)
            pe.wait_ge(sem("mla_sq"), 3)
            nc.tensor.matmul(bank[6][:], ones[:, 0:P], cbuf[0][:], start=True, stop=True).then_inc(sem("mla_ss"), 1)
            nc.tensor.matmul(bank[7][:], ones[:, 0:P], cbuf[1][:], start=True, stop=False)
            nc.tensor.matmul(bank[7][:], ones[:, 0:P], cbuf[2][:], start=False, stop=True).then_inc(sem("mla_ss"), 1)

        def dve_mla_prep(dve):
            for i in range(2):
                dve.wait_ge(sem("mla_sd"), i + 1)
                nc.vector.reciprocal(ubuf[i][:], ubuf[i][:]).then_inc(sem("mla_rs"), 1)
            dve.wait_ge(sem("mla_rs"), 2)
            for i in range(3):
                nc.vector.tensor_tensor(ck(mq, 1 + i), ck(mq, 1 + i), ubuf[min(i, 1)][:],
                                        ALU.mult).then_inc(sem("mla_n"), 1)
            dve_mla_low(dve)
            dve.wait_ge(sem("mla_n"), 3)
            dve.wait_ge(sem("mla_kr"), 1)
            dve.wait_ge(sem("y_T"), 8)
            nc.vector.tensor_tensor(ubuf[0][:], bank[0][:], cosin[:, 0:T], ALU.mult).then_inc(sem("mla_kd"), 1)
            nc.vector.tensor_tensor(ubuf[1][:], bank[1][:], cosin[:, T:2 * T], ALU.mult).then_inc(sem("mla_kd"), 1)
            dve.wait_ge(sem("mla_kd"), 2)
            for u in range(2):
                on, off = slice(64 * u, 64 * u + 64), slice(64 - 64 * u, 128 - 64 * u)
                nc.vector.tensor_tensor(kre[u][on, :], ubuf[0][on, :], ubuf[1][on, :],
                                        ALU.add).then_inc(sem("mla_kd"), 1)
                nc.vector.memset(kre[u][off, :], 0.0).then_inc(sem("mla_kd"), 1)

        def pe_mla(pe):
            base = BASE["mla"]

            def gen(i):
                s = (base + i) % 2
                outs = [("q", 0, 0, 2), ("q", 1, 2, 2), ("r", 0, 4, 2), ("k", 0, 6, 1), ("k", 1, 7, 1)]
                pe.wait_ge(w_lo, base + i + 1)
                if i == 0:
                    pe.wait_ge(sem("mla_lo"), 3)
                    pe.wait_ge(sem("mla_kd"), 6)
                for e, (kind, u, w0, kts) in enumerate(outs):
                    if e >= 2:
                        pe.wait_ge(sem("mla_gen"), 8 * i + e - 1)
                    elif i:
                        pe.wait_ge(sem("mla_gen"), 8 * i - 1 + e)
                    a_hi, a_lo = (ckv_hi, ckv_lo) if kind == "k" else (qn_hi, qn_lo)
                    product(pe, base, i, i, bank[e % 2][:], a_hi, a_lo, kts=kts, w0=w0, last_of_block=False,
                            wait=False).then_inc(sem("mla_g"), 1)
                for e in (5, 6):
                    pe.wait_ge(sem("mla_gen"), 8 * i + e - 1)
                    for h in range(2):
                        blk = 2 * (e - 5) + h
                        o = bank[e % 2][:, h * 256:(h + 1) * 256]
                        tok = slice(blk * P, (blk + 1) * P)
                        nc.tensor.matmul(o, ckv_hi[:, tok], whi[s][:, 8 * P:10 * P], start=True, stop=False)
                        nc.tensor.matmul(o, ckv_lo[:, tok], whi[s][:, 8 * P:10 * P], start=False, stop=False)
                        last = nc.tensor.matmul(o, ckv_hi[:, tok], wlo[s][:, 8 * P:10 * P], start=False, stop=True)
                    last.then_inc(mm if e == 6 else sem("mla_g"), 1)
                pe.wait_ge(sem("mla_gen"), 8 * i + 6)
                nc.tensor.matmul(bank[1][:], con("rot"), ubuf[0][:], start=True, stop=True).then_inc(sem("mla_g"), 1)

            def scores(n):
                i, u = n // 2, n % 2
                pe.wait_ge(sem("mla_gen"), 8 * i + 8)
                if n:
                    pe.wait_ge(sem("mla_exp"), 4 * n)
                for r in range(NREQ):
                    keys = slice(r * SEQ, (r + 1) * SEQ)
                    for qb in range(2):
                        o = bank[2 + r][:, qb * SEQ:(qb + 1) * SEQ]
                        q = slice(r * SEQ + qb * P, r * SEQ + (qb + 1) * P)
                        nc.tensor.matmul(o, qh[u][:, q], kh[u][:, keys], start=True, stop=False)
                        last = nc.tensor.matmul(o, qr[:, q], kre[u][:, keys], start=False, stop=True)
                    last.then_inc(sem("mla_s"), 1)

            def values(n):
                i, u = n // 2, n % 2
                pe.wait_ge(sem("mla_p"), 2 * n + 2)
                for r in range(NREQ):
                    if n:
                        pe.wait_ge(sem("mla_pT_dve" if r else "mla_pT_act"), n)
                    for kb in range(2):
                        for qb in range(2):
                            at = (2 * r + qb) * SEQ + kb * P
                            last = nc.tensor.transpose(bank[4 + r][:, kb * SEQ + qb * P:kb * SEQ + (qb + 1) * P],
                                                       prob[u][:, at:at + P], ident[:])
                    last.then_inc(sem("mla_T"), 1)
                if n >= 2:
                    pe.wait_ge(sem("mla_olo"), n - 1)
                for r in range(NREQ):
                    pe.wait_ge(sem("mla_pT_dve" if r else "mla_pT_act"), n + 1)
                    for kb in range(2):
                        at = (2 * r + kb) * 2 * P + u * P
                        last = nc.tensor.matmul(bank[6 + u][:, r * SEQ:(r + 1) * SEQ], vp[i % 2][:, at:at + P],
                                                probT[:, r * T + kb * SEQ:r * T + (kb + 1) * SEQ],
                                                start=kb == 0, stop=kb == 1)
                last.then_inc(sem("mla_o"), 1)
            for i in range(MHEADS // 2):
                gen(i)
                scores(2 * i)
                if i:
                    values(2 * i - 1)
                scores(2 * i + 1)
                values(2 * i)
            values(MHEADS - 1)

        def act_mla(act):
            base = BASE["mla"]

            def gen(i):
                for e, dst in ((0, qh[0]), (1, qh[1]), (3, kh[0]), (4, kh[1]), (5, None), (6, None)):
                    if e < 6:
                        act.wait_ge(sem("mla_g"), 7 * i + e + 1)
                    else:
                        act.wait_ge(mm, base + i + 1)
                    act.wait_ge(sem("mla_gen"), 8 * i + e)
                    if dst is not None:
                        if i and e == 0:
                            act.wait_ge(sem("mla_s"), 4 * i)
                        out_ap = dst[:]
                    else:
                        if i >= 2:
                            act.wait_ge(sem("mla_o"), 2 * i - 2)
                        out_ap = vp[i % 2][:, (e - 5) * T:(e - 4) * T]
                    nc.scalar.activation(out_ap, bank[e % 2][:], ACT.Copy).then_inc(sem("mla_gen"), 1)
                hi(act, base, i + 2, i + 2)

            def soft(n):
                u = n % 2
                act.wait_ge(sem("mla_nm"), n + 1)
                if n >= 2:
                    act.wait_ge(sem("mla_T"), 2 * n - 2)
                for i in range(4):
                    nc.scalar.activation(prob[u][:, i * SEQ:(i + 1) * SEQ],
                                         bank[2 + i // 2][:, (i % 2) * SEQ:(i % 2 + 1) * SEQ], ACT.Exp,
                                         bias=stat[:, 16 * u + 4 + i:16 * u + 5 + i], scale=QSCALE,
                                         accum_out=stat[:, 16 * u + 8 + i:16 * u + 9 + i]).then_inc(sem("mla_exp"), 1)

            def outs(n):
                act.wait_ge(sem("mla_T"), 2 * n + 1)
                if n:
                    act.wait_ge(sem("mla_o"), n)
                nc.scalar.activation(probT[:, 0:T], bank[4][:], ACT.Copy).then_inc(sem("mla_pT_act"), 1)
                act.wait_ge(sem("mla_o"), n + 1)
                nc.scalar.activation(ck(co_hi, n), bank[6 + n % 2][:], ACT.Copy).then_inc(sem("mla_ohi"), 1)
            for i in range(MHEADS // 2):
                gen(i)
                soft(2 * i)
                if i:
                    outs(2 * i - 1)
                soft(2 * i + 1)
                outs(2 * i)
            outs(MHEADS - 1)

        def dve_mla(dve):
            def gen(i):
                dve.wait_ge(sem("mla_g"), 7 * i + 3)
                dve.wait_ge(sem("mla_gen"), 8 * i + 2)
                nc.vector.tensor_copy(ubuf[0][:], bank[0][:]).then_inc(sem("mla_gen"), 1)
                dve.wait_ge(sem("mla_gen"), 8 * i + 7)
                if i:
                    dve.wait_ge(sem("mla_s"), 4 * i)
                nc.vector.tensor_tensor(qr[:], ubuf[0][:], cosin[:, 0:T], ALU.mult).then_inc(sem("mla_qr"), 1)
                dve.wait_ge(sem("mla_g"), 7 * i + 7)
                nc.vector.tensor_tensor(ubuf[1][:], bank[1][:], cosin[:, T:2 * T], ALU.mult).then_inc(sem("mla_qr"), 1)
                dve.wait_ge(sem("mla_qr"), 2 * i + 2)
                nc.vector.tensor_tensor(qr[:], qr[:], ubuf[1][:], ALU.add).then_inc(sem("mla_gen"), 1)

            def top(n):
                u = n % 2
                for r in range(NREQ):
                    dve.wait_ge(sem("mla_s"), 2 * n + r + 1)
                    nc.vector.tensor_reduce(stat[:, 16 * u + 2 * r:16 * u + 2 * r + 2], req(bank[2 + r][:]), AX.X,
                                            ALU.max).then_inc(sem("mla_mx"), 1)
                dve.wait_ge(sem("mla_mx"), 2 * n + 2)
                nc.vector.tensor_scalar(stat[:, 16 * u + 4:16 * u + 8], stat[:, 16 * u:16 * u + 4], -QSCALE, None,
                                        ALU.mult).then_inc(sem("mla_nm"), 1)

            def norm(n):
                u = n % 2
                dve.wait_ge(sem("mla_exp"), 4 * n + 4)
                nc.vector.reciprocal(stat[:, 16 * u + 12:16 * u + 16],
                                     stat[:, 16 * u + 8:16 * u + 12]).then_inc(sem("mla_p"), 1)
                dve.wait_ge(sem("mla_p"), 2 * n + 1)
                pr = prob[u][:].rearrange("p (i k) -> p i k", i=4)
                nc.vector.tensor_tensor(pr, pr, stat[:, 16 * u + 12:16 * u + 16].unsqueeze(2).broadcast_to(
                    [P, 4, SEQ]), ALU.mult).then_inc(sem("mla_p"), 1)

            def outs(n):
                dve.wait_ge(sem("mla_T"), 2 * n + 2)
                if n:
                    dve.wait_ge(sem("mla_o"), n)
                nc.vector.tensor_copy(probT[:, T:2 * T], bank[5][:]).then_inc(sem("mla_pT_dve"), 1)
                dve.wait_ge(sem("mla_ohi"), n + 1)
                nc.vector.tensor_tensor(ck(co_lo, n), bank[6 + n % 2][:], ck(co_hi, n).bitcast(F32),
                                        ALU.subtract).then_inc(sem("mla_olo"), 1)
            for i in range(MHEADS // 2):
                gen(i)
                top(2 * i)
                norm(2 * i)
                if i:
                    outs(2 * i - 1)
                top(2 * i + 1)
                norm(2 * i + 1)
                outs(2 * i)
            outs(MHEADS - 1)

        def pool_mla(pool):
            for i in range(4):
                lo(pool, BASE["mla"], i + 2, i + 2)


        LR = 16

        def pe_gin(pe):
            base = BASE["gin"]

            def body(t, ft):
                for u in range(2):
                    if ft >= 1:
                        pe.wait_ge(sem("gin_u"), 2 * t - 1 + u)
                    product(pe, base, 2 * t + u, 2 * ft + u, bank[u][:], xw_hi, xw_lo,
                            by_chunk=("res_lo", 1) if ft == 0 and u == 0 else None)
                    if ft == 0 and u == 0:
                        pe_res(pe, 1)
            turns(pe, 0, 8, body)
            pe.wait_ge(sem("gin_u"), LR - 1)
            product(pe, base, LR, LR, bank[0][:], xw_hi, xw_lo)

            def gate(t, ft):
                for u in range(2):
                    j = LR + 1 + 2 * t + u
                    pe.wait_ge(sem("gin_u"), j - 1)
                    product(pe, base, j, LR + 1 + 2 * ft + u, bank[1 - u][:], xw_hi, xw_lo)
            turns(pe, 0, 4, gate)

        def act_gin(act):
            base = BASE["gin"]

            def body(t, ft):
                for u in range(2):
                    hi(act, base, 2 * t + u + 2, 2 * ft + u + 2)
            act.wait_ge(sem("out_m"), of("out_m", 1) + KD)
            act.dma_start(wgk[:], w_gk).then_inc(sem("wgk_in"), 16)
            act.dma_start(gmask[:], glac[:, 0:T + CH]).then_inc(sem("gmask_in"), 16)
            act.dma_start(tri[:], glac[:, T + CH:T + CH + 2 * P]).then_inc(sem("tri_in"), 16)
            turns(act, 0, 8, body)
            hi(act, base, LR + 2, LR + 2)

            def gate(t, ft):
                for u in range(2):
                    j = LR + 1 + 2 * t + u
                    hi(act, base, j + 2, LR + 3 + 2 * ft + u)
                    act.wait_ge(sem("gin_u"), j + 1)
                    nc.scalar.activation(ck(gg, 2 * t + u), ubuf[u][:], ACT.Silu).then_inc(sem("gin_silu"), 1)
            for t in range(4):
                gate(t, t)

        def dve_gin(dve):
            base = BASE["gin"]

            def body(t, ft):
                for u in range(2):
                    dve.wait_ge(mm, base + 2 * t + u + 1)
                    if ft == 0 and u == 0:
                        dve.wait_ge(sem("res_rstd"), of("res_rstd", 1) + 1)
                    scaled(dve, ck(gqkv, 2 * t + u), bank[u]).then_inc(sem("gin_u"), 1)
            turns(dve, 0, 8, body)
            dve.wait_ge(mm, base + LR + 1)
            scaled(dve, lrk[:], bank[0]).then_inc(sem("gin_u"), 1)
            for t in range(4):
                for u in range(2):
                    j = LR + 1 + 2 * t + u
                    dve.wait_ge(mm, base + j + 1)
                    if t:
                        dve.wait_ge(sem("gin_silu"), 2 * t + u - 1)
                    scaled(dve, ubuf[u][:], bank[1 - u]).then_inc(sem("gin_u"), 1)

        def pool_gin(pool):
            base = BASE["gin"]

            def body(t, ft):
                for u in range(2):
                    lo(pool, base, 2 * t + u + 2, 2 * ft + u + 2)
            turns(pool, 0, 11, body)
            for j in range(22, 25):
                lo(pool, base, j + 2, j + 2)

        def kks(d):
            return kk[d][:].rearrange("p (r x) -> p r x", r=NREQ)

        def cross(d, c):
            n = CH * (c if d == 0 else NCH - 1 - c)
            return (0 if d == 0 else CH * (c + 1)), n, (0, 0, CH, 3 * CH)[n // CH]

        def pe_gla(pe):
            pe.wait_ge(sem("gin_u"), 25)
            for i in range(2 * NBLK):
                blk, half = i // 2, i % 2
                if i >= 2:
                    pe.wait_ge(sem("vtok_dve" if i % 2 else "vtok_act"), i // 2)
                for c in range(4):
                    last = nc.tensor.transpose(bank[2 + i % 2][:, c * P:(c + 1) * P],
                                               ck(gqkv, 8 + half * 4 + c)[:, blk * P:(blk + 1) * P], ident[:])
                last.then_inc(sem("v_T"), 1)
            pe.wait_ge(sem("wgk_in"), 16)

            def gates(n):
                hd, d = n // 2, n % 2
                if n:
                    pe.wait_ge(sem("gla_mn"), n)
                nc.tensor.matmul(bank[4][:], wgk[:, (d * 4 + hd) * P:(d * 4 + hd + 1) * P], lrk[:],
                                 start=True, stop=True).then_inc(sem("gla_gk"), 1)

            def scores(n):
                hd, d = n // 2, n % 2
                pe.wait_ge(sem("gla_kk"), 7 * n + 7)
                if hd:
                    pe.wait_ge(sem("gla_att_set"), 8 * hd)
                elif d == 0:
                    pe.wait_ge(sem("vtok_act"), 4)
                    pe.wait_ge(sem("vtok_dve"), 4)
                for r in range(NREQ):
                    for c in range(NCH):
                        for s in (range(c // 2 + 1) if d == 0 else range(c // 2, 2)):
                            last = nc.tensor.matmul(bank[2 * d + r][:, s * SEQ + c * CH:s * SEQ + (c + 1) * CH],
                                                    kks(d)[:, r, c * SEQ + s * P:c * SEQ + (s + 1) * P],
                                                    qt[d][:, r * SEQ + c * CH:r * SEQ + (c + 1) * CH],
                                                    start=True, stop=True)
                last.then_inc(sem("gla_s"), 1)

            def values(hd):
                pe.wait_ge(sem("gla_att_set"), 8 * hd + 8)
                for w in range(2):
                    if hd:
                        pe.wait_ge(sem("gla_osq"), 2 * hd - 1 + w)
                    for r in range(NREQ):
                        for s in range(2):
                            at = (2 * r + s) * D + hd * 2 * P + w * P
                            last = nc.tensor.matmul(bank[5 + w][:, r * SEQ:(r + 1) * SEQ], vtok[:, at:at + P],
                                                    att[:, (2 * r + s) * SEQ:(2 * r + s + 1) * SEQ],
                                                    start=s == 0, stop=s == 1)
                    last.then_inc(sem("gla_o"), 1)

            def sums(hd):
                pe.wait_ge(sem("gla_osq"), 2 * hd + 2)
                if hd:
                    pe.wait_ge(sem("gla_ss_set"), hd)
                nc.tensor.matmul(bank[7][:], ones[:, 0:P], cbuf[2][:], start=True, stop=False)
                nc.tensor.matmul(bank[7][:], ones[:, 0:P], cbuf[3][:], start=False, stop=True).then_inc(
                    sem("gla_ss"), 1)
            gates(0)
            for n in range(8):
                if n < 7:
                    gates(n + 1)
                scores(n)
                if n % 2:
                    values(n // 2)
                    sums(n // 2)

        def act_gla(act):
            for i in range(0, 2 * NBLK, 2):
                act.wait_ge(sem("v_T"), i + 1)
                nc.scalar.activation(vtok[:, i // 2 * D:i // 2 * D + T], bank[2][:], ACT.Copy).then_inc(
                    sem("vtok_act"), 1)

            def logsig(n):
                hd, d = n // 2, n % 2
                act.wait_ge(sem("gla_gk"), n + 1)
                if n:
                    act.wait_ge(sem("gla_ls"), n)
                nc.scalar.activation(cbuf[0][:], bank[4][:], ACT.Abs, bias=prm("bgk", d * 4 + hd)).then_inc(
                    sem("gla_a"), 1)
                act.wait_ge(sem("gla_a"), 3 * n + 1)
                nc.scalar.activation(cbuf[0][:], cbuf[0][:], ACT.Exp, scale=-1.0).then_inc(sem("gla_a"), 1)
                act.wait_ge(sem("gla_a"), 3 * n + 2)
                nc.scalar.activation(cbuf[1][:], cbuf[0][:], ACT.Ln, bias=ones[:, 0:1]).then_inc(sem("gla_a"), 1)

            def exps(n):
                d = n % 2
                act.wait_ge(sem("gla_ge"), n + 1)
                if n:
                    act.wait_ge(sem("gla_kk"), 7 * n)
                if n >= 2:
                    act.wait_ge(sem("gla_s"), n - 1)
                nc.scalar.activation(qt[d][:], ubuf[1][:], ACT.Exp, scale=GK_NORM).then_inc(sem("gla_e"), 1)
                nc.scalar.activation(ek[:], ubuf[1][:], ACT.Exp, scale=-GK_NORM).then_inc(sem("gla_e"), 1)
                for r in range(NREQ):
                    for c in range(NCH):
                        s0, m, at = cross(d, c)
                        if m:
                            nc.scalar.activation(ecr[:, r * 6 * CH + at:r * 6 * CH + at + m],
                                                 gcum[:, r * SEQ + s0:r * SEQ + s0 + m], ACT.Exp,
                                                 scale=-GK_NORM, bias=gend[:, r * NCH + c:r * NCH + c + 1]).then_inc(
                                                     sem("gla_e"), 1)

            def cross_scores(hd):
                act.wait_ge(sem("gla_dg"), 4 * hd + 4)
                for r in range(NREQ):
                    nc.scalar.activation(att[:, 2 * r * SEQ + P:2 * r * SEQ + 2 * P], bank[r][:, P:2 * P],
                                         ACT.Copy).then_inc(sem("gla_att_set"), 2)
                    nc.scalar.activation(att[:, (2 * r + 1) * SEQ:(2 * r + 1) * SEQ + P],
                                         bank[2 + r][:, SEQ:SEQ + P], ACT.Copy).then_inc(sem("gla_att_set"), 2)

            def outs(hd):
                for w in range(2):
                    act.wait_ge(sem("gla_o"), 2 * hd + w + 1)
                    nc.scalar.activation(ck(gqkv, 8 + 2 * hd + w), bank[5 + w][:], ACT.Copy).then_inc(
                        sem("gla_om"), 1)
                    if hd:
                        act.wait_ge(sem("gla_ss"), hd)
                    nc.scalar.activation(cbuf[2 + w][:], bank[5 + w][:], ACT.Square).then_inc(sem("gla_osq"), 1)
            for n in range(8):
                logsig(n)
                exps(n)
                if n % 2:
                    cross_scores(n // 2)
                    outs(n // 2)
            for hd in range(GLA_HEADS):
                act.wait_ge(sem("gla_ss_set"), hd + 1)
                nc.scalar.activation(ck(gqkv, 4 + hd), ck(gqkv, 4 + hd), ACT.Sqrt, bias=prm("eps"),
                                     scale=1.0 / (2 * P)).then_inc(sem("gla_sd"), 1)
            for c in range(KD):
                act.wait_ge(sem("gla_fin"), 2 * c + 2)
                nc.scalar.activation(ck(xw_hi, c), ck(gg, c), ACT.Copy).then_inc(sem("gla_hi"), 1)

        def dve_gla(dve):
            for d in range(2):
                for c in ((0, 2) if d == 0 else (1, 3)):
                    s0 = CH * (c + 1) if d == 0 else CH * (c - 1)
                    nc.vector.memset(kks(d)[:, :, c * SEQ + s0:c * SEQ + s0 + CH], 0.0).then_inc(sem("kk_zero"), 1)
            for i in range(1, 2 * NBLK, 2):
                dve.wait_ge(sem("v_T"), i + 1)
                nc.vector.tensor_copy(vtok[:, i // 2 * D + T:(i // 2 + 1) * D], bank[3][:]).then_inc(
                    sem("vtok_dve"), 1)
            dve.wait_ge(sem("gmask_in"), 16)
            dve.wait_ge(sem("tri_in"), 16)

            def logsig(n):
                hd, d = n // 2, n % 2
                dve.wait_ge(sem("gla_a"), 3 * n + 1)
                if n:
                    dve.wait_ge(sem("gla_sc"), 3 * n)
                nc.vector.tensor_scalar(ubuf[0][:], bank[4][:], prm("bgk", d * 4 + hd), 0.0, ALU.add,
                                        ALU.min).then_inc(sem("gla_mn"), 1)
                dve.wait_ge(sem("gla_a"), 3 * n + 3)
                dve.wait_ge(sem("gla_mn"), n + 1)
                nc.vector.tensor_tensor(ubuf[0][:], ubuf[0][:], cbuf[1][:], ALU.subtract).then_inc(sem("gla_ls"), 1)
                dve.wait_ge(sem("gla_ls"), n + 1)
                if n:
                    dve.wait_ge(sem("gla_e"), 8 * n)

                def way(ap):
                    return ap[:, ::-1] if d else ap
                nc.vector.tensor_tensor_scan(out=way(ubuf[1][:]), data0=way(gmask[:, d:d + T]), data1=way(ubuf[0][:]),
                                             initial=0.0, op0=ALU.mult, op1=ALU.add).then_inc(sem("gla_sc"), 1)
                for r in range(NREQ):
                    f = slice(r * SEQ, (r + 1) * SEQ)
                    nc.vector.tensor_tensor_scan(out=way(gcum[:, f]), data0=ones[:, 0:SEQ], data1=way(ubuf[0][:, f]),
                                                 initial=0.0, op0=ALU.mult, op1=ALU.add).then_inc(sem("gla_sc"), 1)
                dve.wait_ge(sem("gla_sc"), 3 * n + 3)
                g4 = gend[:].rearrange("p (r c) -> p r c", r=NREQ)
                g3 = gcum[:].rearrange("p (r c x) -> p r c x", r=NREQ, x=CH)
                src = g3[:, :, 0:3, CH - 1] if d == 0 else g3[:, :, 1:4, 0]
                nc.vector.tensor_scalar(g4[:, :, 1:4] if d == 0 else g4[:, :, 0:3], src, GK_NORM, None,
                                        ALU.mult).then_inc(sem("gla_ge"), 1)

            def keys(n):
                hd, d = n // 2, n % 2
                dve.wait_ge(sem("gla_e"), 8 * n + 8)
                if hd:
                    dve.wait_ge(sem("gla_s"), n - 1)
                nc.vector.scalar_tensor_tensor(out=qt[d][:], in0=ck(gqkv, hd), scalar=QG, in1=qt[d][:],
                                               op0=ALU.mult, op1=ALU.mult).then_inc(sem("gla_q"), 1)
                dve.wait_ge(sem("gla_q"), n + 1)
                k = req(ck(gqkv, 4 + hd))
                for c in range(NCH):
                    own = slice(c * CH, (c + 1) * CH)
                    nc.vector.tensor_tensor(kks(d)[:, :, c * SEQ + c * CH:c * SEQ + (c + 1) * CH], k[:, :, own],
                                            req(ek[:])[:, :, own], ALU.mult).then_inc(sem("gla_kk"), 1)
                    s0, m, at = cross(d, c)
                    if m:
                        e = ecr[:].rearrange("p (r x) -> p r x", r=NREQ)[:, :, at:at + m]
                        nc.vector.tensor_tensor(kks(d)[:, :, c * SEQ + s0:c * SEQ + s0 + m], k[:, :, s0:s0 + m], e,
                                                ALU.mult).then_inc(sem("gla_kk"), 1)

            def own_scores(hd):
                if hd:
                    dve.wait_ge(sem("gla_o"), 2 * hd)
                dve.wait_ge(sem("gla_s"), 2 * hd + 2)
                for r in range(NREQ):
                    for s in range(2):
                        a = att[:, (2 * r + s) * SEQ + s * P:(2 * r + s) * SEQ + (s + 1) * P]
                        b = dg[:, (2 * r + s) * P:(2 * r + s + 1) * P]
                        f = slice(s * SEQ + s * P, s * SEQ + (s + 1) * P)
                        nc.vector.tensor_tensor(a, bank[r][:, f], tri[:, 0:P], ALU.mult).then_inc(sem("gla_d"), 1)
                        nc.vector.tensor_tensor(b, bank[2 + r][:, f], tri[:, P:2 * P], ALU.mult).then_inc(
                            sem("gla_d"), 1)
                dve.wait_ge(sem("gla_d"), 8 * hd + 8)
                for i in range(4):
                    r, s = i // 2, i % 2
                    a = att[:, (2 * r + s) * SEQ + s * P:(2 * r + s) * SEQ + (s + 1) * P]
                    nc.vector.tensor_tensor(a, a, dg[:, (2 * r + s) * P:(2 * r + s + 1) * P], ALU.add).then_inc(
                        sem("gla_dg"), 1)

            def sums(hd):
                dve.wait_ge(sem("gla_ss"), hd + 1)
                nc.vector.tensor_copy(ck(gqkv, 4 + hd), bank[7][:]).then_inc(sem("gla_ss_set"), 1)
            for n in range(8):
                logsig(n)
                keys(n)
                if n % 2:
                    own_scores(n // 2)
                    if n > 2:
                        sums(n // 2 - 1)
            sums(GLA_HEADS - 1)
            for hd in range(GLA_HEADS):
                dve.wait_ge(sem("gla_sd"), hd + 1)
                nc.vector.reciprocal(ck(gqkv, 4 + hd), ck(gqkv, 4 + hd)).then_inc(sem("gla_rs"), 1)
            for c in range(KD):
                hd, w = c // 2, c % 2
                dve.wait_ge(sem("gla_rs"), hd + 1)
                if c >= 2:
                    dve.wait_ge(sem("gla_fin"), 2 * c - 2)
                nc.vector.scalar_tensor_tensor(out=ubuf[w][:], in0=ck(gqkv, 8 + c), scalar=prm("glan", w),
                                               in1=ck(gqkv, 4 + hd), op0=ALU.mult, op1=ALU.mult).then_inc(
                                                   sem("gla_fin"), 1)
                dve.wait_ge(sem("gla_fin"), 2 * c + 1)
                nc.vector.tensor_tensor(ck(gg, c), ck(gg, c), ubuf[w][:], ALU.mult).then_inc(sem("gla_fin"), 1)

        def pool_gla(pool):
            for c in range(KD):
                pool.wait_ge(sem("gla_hi"), c + 1)
                nc.gpsimd.tensor_tensor(ck(xw_lo, c), ck(gg, c), ck(xw_hi, c).bitcast(F32),
                                        ALU.subtract).then_inc(sem("gla_lo"), 1)

        block = ctx.enter_context(nc.Block())

        @block.sync
        def _(sp):
            sp.dma_start(par[:], params).then_inc(sem("par_in"), 16)
            for c in range(KD):
                sp.dma_start(ck(xres, c), x_in[:, c * T:(c + 1) * T]).then_inc(sem(f"x_in{c}"), 16)
            sp.dma_start(ident[:], consts[:, 0:P]).then_inc(sem("ident_in"), 16)
            g = 0
            for name, count, kt in STREAM:
                n = kt * P
                base = BASE[name]
                for u in range(2):
                    if g >= 2:
                        sp.wait_ge(w_lo, base + u - 1)
                    sp.dma_start(raw[(base + u) % 2][:, 0:n], w_stream[name][u]).then_inc(raw_in[(base + u) % 2], 16)
                with sp.Fori(1, count // 2) as t:
                    for u in range(2):
                        sp.wait_ge(w_lo, 2 * t + (base + u - 1))
                        sp.dma_start(raw[(base + u) % 2][:, 0:n],
                                     w_stream[name][bass.ds(2 * t + u, 1)].rearrange("b p n -> (b p) n")).then_inc(
                                         raw_in[(base + u) % 2], 16)
                if count % 2:
                    sp.wait_ge(w_lo, base + count - 2)
                    sp.dma_start(raw[(base + count - 1) % 2][:, 0:n], w_stream[name][count - 1]).then_inc(
                        raw_in[(base + count - 1) % 2], 16)
                g += count
            for c in range(KD):
                sp.wait_ge(sem("res_x"), of("res_x", 3) + c + 1)
                sp.dma_start(out[:, c * T:(c + 1) * T], ck(xres, c)).then_inc(sem("out_stored"), 16)
            sp.wait_ge(sem("out_stored"), KD * 16)

        def first_two(eng, split):
            for j in range(2):
                split(eng, 0, j, j)

        @block.scalar
        def _(act):
            act.dma_start(cst[:], consts[:, P:NCONST]).then_inc(sem("cst_in"), 16)
            act.dma_start(cosin[:], rope).then_inc(sem("rope_in"), 16)
            first_two(act, hi)
            act_res(act, -1)
            act_hin(act)
            act_dt(act)
            act_ssd(act)
            act_mla_prep(act)
            act_mla(act)
            act_out(act, 0, "hout", 2, m_hyb)
            act_res(act, 0)
            act_fin(act, 0)
            act_out(act, 1, "fout0", 2, m_ffn)
            act_res(act, 1)
            act_gin(act)
            act_gla(act)
            act_out(act, 2, "gout", 1, m_gla)
            act_res(act, 2)
            act_fin(act, 1)
            act_out(act, 3, "fout1", 2, m_ffn)

        @block.gpsimd
        def _(pool):
            first_two(pool, lo)
            pool_res(pool, -1)
            pool_hin(pool)
            pool_mla(pool)
            pool_out(pool, 0, "hout", 2)
            pool_res(pool, 0)
            pool_fin(pool, 0)
            pool_out(pool, 1, "fout0", 2)
            pool_res(pool, 1)
            pool_gin(pool)
            pool_gla(pool)
            pool_out(pool, 2, "gout", 1)
            pool_res(pool, 2)
            pool_fin(pool, 1)
            pool_out(pool, 3, "fout1", 2)

        @block.vector
        def _(dve):
            nc.vector.memset(ones[:], 1.0).then_inc(sem("ones_set"), 1)
            dve.wait_ge(sem("ones_set"), 1)
            dve_res(dve, -1, None)
            dve_hin(dve)
            dve.wait_ge(sem("cst_in"), 16)
            dve.wait_ge(sem("ident_in"), 16)
            dve.wait_ge(sem("rope_in"), 16)
            dve_dt(dve)
            dve_ssd(dve)
            dve_ssd_low(dve)
            dve_mla_prep(dve)
            dve_mla(dve)
            dve_res(dve, 0, m_hyb)
            dve_fin(dve, 0)
            dve_res(dve, 1, m_ffn)
            dve_gin(dve)
            dve_gla(dve)
            dve_res(dve, 2, m_gla)
            dve_fin(dve, 1)
            dve_res(dve, 3, m_ffn)

        @block.tensor
        def _(pe):
            pe_hin(pe)
            pe.wait_ge(sem("ident_in"), 16)
            pe.wait_ge(sem("cst_in"), 16)
            pe_dt(pe)
            pe_ssd(pe)
            pe_mla_prep(pe)
            pe_mla(pe)
            pe_out(pe, 0, "hout", 2,
                   lambda b: (co_hi, co_lo, 0, [("mla_olo", MHEADS)]) if b else (xw_hi, xw_lo, 0, [("ssd_lo", KD)]))
            pe_fin(pe, 0)
            pe_out(pe, 1, "fout0", 2, ffn_operand(0))
            pe_gin(pe)
            pe_gla(pe)
            pe_out(pe, 2, "gout", 1, lambda b: (xw_hi, xw_lo, 0, [("gla_lo", KD)]))
            pe_fin(pe, 1)
            pe_out(pe, 3, "fout1", 2, ffn_operand(1))


def _tiles(w, cols):
    kt = w.shape[0] // P
    return w[:, cols].reshape(kt, P, -1, P).transpose(2, 1, 0, 3)


def _by_chunk(v):
    return v.reshape(-1, P).T


def _layout(i):
    a = np.arange
    f32 = np.float32
    sample = {}
    x = np.concatenate([i["x_prompt"][0], i["x_sample"][0]], 0)
    sample["x"] = x.T.reshape(KD, P, T).transpose(1, 0, 2).reshape(P, KD * T)
    dt0, q0, kv0 = 2560, 2592, 2848
    kr0 = kv0 + P
    misc = np.concatenate([dt0 + a(16), kr0 + a(16), dt0 + 16 + a(16), kr0 + a(16), kr0 + a(ROPE)])
    cols = np.concatenate([misc, kv0 + a(P), q0 + a(QLORA), 1024 + a(1536), a(1024)])
    sample["hin"] = _tiles(i["hyb_w_in"][0], cols)
    qb, kvb = i["mla_w_qb"][0], i["mla_w_kvb"][0]
    pairs = []
    for h in range(0, MHEADS, 2):
        q_at, kv_at = h * (NOPE + ROPE), h * 2 * P
        nope = [q_at + a(P), q_at + NOPE + ROPE + a(P)]
        rope = np.concatenate([q_at + NOPE + a(ROPE), q_at + 2 * NOPE + ROPE + a(ROPE)])
        parts = [_tiles(qb, c)[0] for c in (*nope, rope)]
        parts += [kvb[:, kv_at + o:kv_at + o + P].reshape(P, 1, P) for o in (0, 2 * P, P, 3 * P)]
        pairs.append(np.concatenate(parts, 1))
    sample["mla"] = np.stack(pairs)
    sample["hout"] = _tiles(i["hyb_w_out"][0], a(D)).reshape(KD, P, 2, KD, P).transpose(0, 2, 1, 3, 4)
    for l in range(2):
        inner = np.stack([a(FF * P).reshape(FF, P), FF * P + a(FF * P).reshape(FF, P)], 1).reshape(-1)
        sample[f"fin{l}"] = _tiles(i["ffn_w_in"][l], inner)
        sample[f"fout{l}"] = _tiles(i["ffn_w_out"][l], a(D)).reshape(KD, P, 2, FF // 2, P).transpose(0, 2, 1, 3, 4)
    lr0 = 3072
    lr = np.concatenate([lr0 + a(16), lr0 + a(16), lr0 + 16 + a(16), lr0 + a(16), lr0 + a(32), lr0 + a(32)])
    sample["gin"] = _tiles(i["gla_w_in"][0], np.concatenate([a(2048), lr, 2048 + a(1024)]))
    sample["gout"] = _tiles(i["gla_w_out"][0], a(D))
    for n, c, k in STREAM:
        sample[n] = np.ascontiguousarray(sample[n]).reshape(c, P, k * P)
    wgk = np.zeros((P, 2, 4 * P), f32)
    wgk[0:16, 0] = i["gla_w_gk2"][0, 0]
    wgk[32:48, 1] = i["gla_w_gk2"][0, 1]
    sample["wgk"] = wgk.reshape(P, -1)
    par = np.zeros((P, NPARAM), f32)

    def put(name, v, rows=slice(None)):
        par[rows, PCOLS[name]:PCOLS[name] + v.shape[1]] = v
    put("norm", _by_chunk(i["norm_w"]))
    put("cw", _by_chunk(i["ssd_conv_w"][0]))
    put("cb", _by_chunk(i["ssd_conv_b"][0]))
    for d in range(2):
        rows = slice(32 * d, 32 * d + 16)
        put("dtb", i["ssd_dt_bias"][0].reshape(2, 16, 1)[d], rows)
        put("alog", i["ssd_a_log"][0].reshape(2, 16, 1)[d], rows)
    put("dskip", _by_chunk(np.repeat(i["ssd_d"][0], HDIM)))
    put("ssdn", _by_chunk(i["ssd_norm_w"][0]))
    put("qn", _by_chunk(i["mla_q_norm_w"][0]))
    put("kvn", _by_chunk(i["mla_kv_norm_w"][0]))
    put("bgk", _by_chunk(i["gla_b_gk"][0]))
    put("glan", _by_chunk(i["gla_norm_w"][0]))
    for l in range(2):
        put(f"fw{l}", _by_chunk(i["ffn_conv_w"][l]))
        put(f"fb{l}", _by_chunk(i["ffn_conv_b"][l]))
    put("eps", np.full((P, 1), EPS, f32))
    sample["par"] = par
    return sample


def _constants():
    f32 = np.float32
    n = np.arange(P)
    eye = np.eye(P, dtype=f32)
    up = (n[None, :] >= n[:, None]).astype(f32)
    one = np.ones((P, P), f32)
    half = n % ROPE
    rot = np.zeros((P, P), f32)
    src = np.where(half < ROPE // 2, n + ROPE // 2, n - ROPE // 2)
    rot[src, n] = np.where(half < ROPE // 2, -1, 1)
    dup = np.zeros((P, P), f32)
    dup[64 + half, n] = 1
    selrot = np.zeros((P, P), f32)
    selrot[64 + src % ROPE, n] = np.where(half < ROPE // 2, -1, 1)
    cst = np.concatenate([eye, up, one, up, up.T, one, up.T, rot, dup, selrot], 1)
    inv = (f32(1.0) / (f32(10000.0) ** (np.arange(0, ROPE, 2, dtype=f32) / f32(ROPE)))).astype(f32)
    ang = np.arange(SEQ, dtype=f32)[:, None] * inv[None, :]
    table = [np.tile(np.tile(t(ang).T.astype(f32), (4, 1)), (1, NREQ)) for t in (np.cos, np.sin)]
    gmask = np.tile((np.arange(T + CH) % CH != 0).astype(f32), (P, 1))
    return cst, np.concatenate(table, 1), np.concatenate([gmask, up, up.T], 1)


def kernel(**inputs):
    import concourse.bacc as bacc
    from concourse.bass_utils import run_bass_kernel_spmd

    nc = bacc.Bacc("TRN2", target_bir_lowering=False, num_devices=1)
    data = _layout({k: np.asarray(v) for k, v in inputs.items()})
    cst, rope, glac = _constants()
    data |= {"cst": cst, "rope": rope, "glac": glac}
    arrays, aps = {}, {}
    for name, a in data.items():
        arrays[f"in_{name}"] = np.ascontiguousarray(a)
        aps[name] = nc.dram_tensor(f"in_{name}", a.shape, F32, kind="ExternalInput").ap()
    out = nc.dram_tensor("out_y", (P, KD * T), F32, kind="ExternalOutput").ap()
    build_program(nc, aps["x"], {n: aps[n] for n, _, _ in STREAM}, aps["wgk"], aps["par"], aps["cst"], aps["rope"],
                  aps["glac"], out)
    r = run_bass_kernel_spmd(nc, [arrays], core_ids=[0])
    y = r.results[0]["out_y"].reshape(P, KD, T).transpose(2, 1, 0).reshape(NREQ, SEQ, D)
    return np.ascontiguousarray(y[0:1]), np.ascontiguousarray(y[1:2])
```

```python
from contextlib import ExitStack

import concourse.bass as bass
import numpy as np
from concourse import mybir

F32, F32R = mybir.dt.float32, mybir.dt.float32r
ACT, ALU, AX = mybir.ActivationFunctionType, mybir.AluOpType, mybir.AxisListType

P = 128
D = 1024
KD = D // P
SEQ, NREQ = 256, 2
T = SEQ * NREQ
NBLK = T // P
EPS = 1e-6

HEADS, HDIM = 16, 64
GHEADS = 8
QLORA, NOPE, ROPE, MHEADS = 256, 128, 64, 8
QSCALE = float(NOPE + ROPE) ** -0.5
GLA_HEADS, CH = 4, 64
NCH = SEQ // CH
GK_NORM = 1.0 / 16.0
QG = float(P) ** -0.5
FF = 2816 // P

STREAM = [("hin", 24, KD), ("mla", 4, 10), ("hout", 16, KD), ("fin0", 2 * FF, KD), ("fout0", 16, FF // 2),
          ("gin", 25, KD), ("gout", 8, KD), ("fin1", 2 * FF, KD), ("fout1", 16, FF // 2)]
BASE, _at = {}, 0
for _n, _c, _k in STREAM:
    BASE[_n] = _at
    _at += _c
TOTAL = _at
KT_OF = [k for _, c, k in STREAM for _ in range(c)]
KT_MAX = max(KT_OF)

PCOLS = {}
_at = 0
for _n, _c in [("norm", 64), ("cw", 36), ("cb", 12), ("dtb", 1), ("alog", 1), ("dskip", 8), ("ssdn", 8), ("qn", 2),
               ("kvn", 1), ("bgk", 8), ("glan", 2), ("fw0", 132), ("fw1", 132), ("fb0", 44), ("fb1", 44), ("eps", 1)]:
    PCOLS[_n] = _at
    _at += _c
NPARAM = _at

CCOLS = {"ident": 0, "maskF": 128, "maskB": 512, "rot": 896, "seldup": 1024, "selrot": 1152}
NCONST = 1280


def build_program(nc, x_in, w_stream, w_gk, params, consts, rope, glac, out):
    ctx = ExitStack()
    with ctx:
        sems = {}

        def sem(name):
            if name not in sems:
                sems[name] = ctx.enter_context(nc.semaphore(name))
            return sems[name]

        def sb(name, cols, dtype=F32, stack=ctx, parts=P):
            return stack.enter_context(nc.sbuf_tensor(name, [parts, cols], dtype))

        xres = sb("xres", KD * T)
        raw = [sb(f"raw{i}", KT_MAX * P) for i in range(2)]
        whi = [sb(f"whi{i}", KT_MAX * P, F32R) for i in range(2)]
        wlo = [sb(f"wlo{i}", KT_MAX * P, F32R) for i in range(2)]
        rstd = sb("rstd", T)
        sqacc = sb("sqacc", T)
        ubuf = [sb(f"ubuf{i}", T) for i in range(2)]
        with ExitStack() as s:
            vp1 = sb("vp1", NBLK * 2 * P, F32, s)
            prob1 = sb("prob1", 4 * SEQ, F32, s)
        cbuf = [sb(f"cbuf{i}", T) for i in range(4)]
        par = sb("par", NPARAM)
        ident = sb("ident", P)
        ones = sb("ones", SEQ)
        small = sb("small", 4)
        with ExitStack() as s:
            xw_hi = sb("xw_hi", KD * T, F32R, s)
            xw_lo = sb("xw_lo", KD * T, F32R, s)
        with ExitStack() as s:
            m_ffn = sb("m_ffn", KD * T, F32, s)
        with ExitStack() as s:
            xdt = sb("xdt", 2 * NBLK * D, F32, s)
        with ExitStack() as s:
            kk = [sb(f"kk{i}", NREQ * NCH * SEQ, F32, s) for i in range(2)]
            att = [sb(f"att{i}", NREQ * 2 * SEQ, F32, s) for i in range(2)]
            ek = [sb(f"ek{i}", T, F32, s) for i in range(2)]
            qt = [sb(f"qt{i}", T, F32, s) for i in range(2)]
        sb("xw_region", 2 * KD * T)

        with ExitStack() as s:
            zbuf = sb("zbuf", KD * T, F32, s)
            mq = sb("mq", 4 * T, F32, s)
            co_hi = sb("co_hi", MHEADS * T, F32R, s)
            co_lo = sb("co_lo", MHEADS * T, F32R, s)
            cosin = sb("cosin", 2 * T, F32, s)
            cst = sb("cst", NCONST - P, F32, s)
            with ExitStack() as q:
                xbc = sb("xbc", 12 * T, F32, q)
                ebuf_late = [sb(f"ebuf{i}", 3 * T, F32, q) for i in (2, 3)]
                sqbuf = [sb(f"sqbuf{i}", T, F32, q) for i in range(2)]
            with ExitStack() as q:
                m_hyb = sb("m_hyb", KD * T, F32, q)
            with ExitStack() as q:
                qn_hi = sb("qn_hi", 2 * T, F32R, q)
                qn_lo = sb("qn_lo", 2 * T, F32R, q)
                ckv_hi = sb("ckv_hi", T, F32R, q)
                ckv_lo = sb("ckv_lo", T, F32R, q)
                kre = [sb(f"kre{i}", T, F32, q) for i in range(2)]
                qh = [sb(f"qh{i}", T, F32, q) for i in range(2)]
                qr = sb("qr", T, F32, q)
                kh = [sb(f"kh{i}", T, F32, q) for i in range(2)]
                vp0 = sb("vp0", NBLK * 2 * P, F32, q)
                prob0 = sb("prob0", 4 * SEQ, F32, q)
                probT = sb("probT", 4 * SEQ, F32, q)
                stat = sb("stat", 32, F32, q)
            vp, prob = [vp0, vp1], [prob0, prob1]
        with ExitStack() as s:
            sb("zbuf_mq", 12 * T, F32, s)
            ebuf = [sb(f"ebuf{i}", 3 * T, F32, s) for i in range(2)] + ebuf_late
            cbm = sb("cbm", 4 * 3 * SEQ, F32, s)
            at_hi = sb("at_hi", T, F32R, s, 64)
            at_lo = sb("at_lo", T, F32R, s, 64)
            onehot = [sb(f"onehot{i}", 2 * P, F32R, s, 64) for i in range(2)]
            dtt = sb("dtt", NBLK * 64, F32, s)
            acol = sb("acol", NBLK * 64, F32, s)
        with ExitStack() as s:
            g_hi = sb("g_hi", FF * T, F32R, s)
            g_lo = sb("g_lo", FF * T, F32R, s)
        with ExitStack() as s:
            gqkv = sb("gqkv", 16 * T, F32, s)
            gg = sb("gg", 8 * T, F32, s)
            with ExitStack() as q:
                vtok = sb("vtok", NBLK * D, F32, q)
                lrk = sb("lrk", T, F32, q)
                gl = sb("gl", 2 * GLA_HEADS * T, F32, q)
                carry = sb("carry", 2 * GLA_HEADS * NREQ * 6, F32, q)
                diag = sb("diag", 4 * P, F32, q)
                gsum = sb("gsum", 4 * NBLK, F32, q)
                dg = sb("dg", NREQ * SEQ, F32, q)
                wgk = sb("wgk", 2 * 4 * P, F32, q)
                wsel = sb("wsel", P, F32, q)
                gmask = sb("gmask", T + CH, F32, q)
                tri = sb("tri", 2 * P, F32, q)
            with ExitStack() as q:
                m_gla = sb("m_gla", KD * T, F32, q)
        bank = [ctx.enter_context(nc.psum_tensor(f"bank{i}", [P, T], F32)) for i in range(8)]

        def ck(t, c, n=1):
            return t[:, bass.ds(c * T, n * T)]

        def prm(name, c=0):
            return par[:, bass.ds(PCOLS[name] + c, 1)]

        def con(name, n=P):
            return cst[:, CCOLS[name] - P:CCOLS[name] - P + n]

        def req(ap):
            return ap.rearrange("p (r s) -> p r s", r=NREQ)

        ADDS = {"res_hi": 8, "res_sq": 8, "res_lo": 8, "res_acc": 7, "res_ss": 1, "res_sd": 1, "res_rstd": 1,
                "res_rstdm": 1, "res_t": 8, "res_x": 8, "out_m": 8, "out_sq": 8, "out_acc": 7, "out_ss": 1,
                "out_sd": 1, "fin_u": 2 * FF, "fin_mid": 2 * FF, "fin_taps": 4 * FF, "fin_gelu": FF,
                "fin_prod": FF, "fin_hi": FF, "fin_lo": FF, "ssd_lo": KD, "gla_lo": KD}
        FROM_START = ("res_hi", "res_sq", "res_lo", "res_acc", "res_ss", "res_sd", "res_rstd")

        def of(name, k):
            return ADDS[name] * (k + 1 if name in FROM_START else k)

        raw_in = [sem("raw_in0"), sem("raw_in1")]
        w_hi, w_lo, mm = sem("w_hi"), sem("w_lo"), sem("mm_block")

        def turns(eng, t0, t1, body):
            body(t0, t0)
            if t1 - t0 > 3:
                with eng.Fori(t0 + 1, t1) as t:
                    body(t, t0 + 1)
            else:
                for t in range(t0 + 1, t1):
                    body(t, t)

        def hi(act, base, j, fj):
            f = base + fj
            if f >= TOTAL:
                return
            s, n = f % 2, KT_OF[f] * P
            act.wait_ge(raw_in[s], (j - fj) * 8 + (f // 2 + 1) * 16)
            if f >= 2:
                act.wait_ge(mm, base + j - 1)
            nc.scalar.activation(whi[s][:, 0:n], raw[s][:, 0:n], ACT.Copy).then_inc(w_hi, 1)

        def lo(pool, base, j, fj):
            f = base + fj
            if f >= TOTAL:
                return
            s, n = f % 2, KT_OF[f] * P
            pool.wait_ge(w_hi, base + j + 1)
            nc.gpsimd.tensor_tensor(wlo[s][:, 0:n], raw[s][:, 0:n], whi[s][:, 0:n].bitcast(F32),
                                    ALU.subtract).then_inc(w_lo, 1)

        def product(pe, base, j, fj, out_ap, a_hi, a_lo, kts=None, k0=0, w0=0, start=True, stop=True, by_chunk=None,
                    last_of_block=True, wait=True):
            f = base + fj
            s = f % 2
            kts = KT_OF[f] if kts is None else kts
            if wait:
                pe.wait_ge(w_lo, base + j + 1)
            for k in range(kts):
                if by_chunk is not None:
                    pe.wait_ge(sem(by_chunk[0]), of(*by_chunk) + k0 + k + 1)
                ah, al = ck(a_hi, k0 + k), ck(a_lo, k0 + k)
                wh, wl = whi[s][:, (w0 + k) * P:(w0 + k + 1) * P], wlo[s][:, (w0 + k) * P:(w0 + k + 1) * P]
                nc.tensor.matmul(out_ap, wh, ah, start=start and k == 0, stop=False)
                nc.tensor.matmul(out_ap, wh, al, start=False, stop=False)
                last = nc.tensor.matmul(out_ap, wl, ah, start=False, stop=stop and k == kts - 1)
            if last_of_block:
                last.then_inc(mm, 1)
            return last

        def m_norm(k):
            return (k // 2) * 32 + (k % 2) * 16 + 8

        def x_norm(k):
            return ((k + 1) // 2) * 32 + ((k + 1) % 2) * 16

        def pe_out(pe, k, name, per, a_of_block, first_by_chunk=None):
            base = BASE[name]

            def body(t, ft):
                for u in range(2):
                    c, fc = 2 * t + u, 2 * ft + u
                    if fc >= 2:
                        pe.wait_ge(sem("out_sq"), of("out_sq", k) + c - 1)
                    for b in range(per):
                        src_hi, src_lo, k0, ready = a_of_block(b)
                        if ready is not None and fc == 0:
                            for stage, n in ready:
                                pe.wait_ge(sem(stage), n)
                        product(pe, base, c * per + b, fc * per + b, bank[2 + u][:], src_hi, src_lo, k0=k0,
                                start=b == 0, stop=b == per - 1,
                                by_chunk=first_by_chunk if fc == 0 and b == 0 else None)
            turns(pe, 0, KD // 2, body)
            pe.wait_ge(sem("out_acc"), of("out_acc", k) + KD - 1)
            nc.tensor.matmul(bank[7][:], ones[:, 0:P], sqacc[:], start=True, stop=True).then_inc(sem("out_ss"), 1)

        def act_out(act, k, name, per, m_tile):
            base = BASE[name]

            def body(t, ft):
                for u in range(2):
                    c, fc = 2 * t + u, 2 * ft + u
                    for b in range(per):
                        hi(act, base, c * per + b + 2, fc * per + b + 2)
                    act.wait_ge(mm, base + (c + 1) * per)
                    nc.scalar.activation(ck(m_tile, c), bank[2 + u][:], ACT.Copy).then_inc(sem("out_m"), 1)
                    if fc > 2:
                        act.wait_ge(sem("out_acc"), of("out_acc", k) + c - 2)
                    nc.scalar.activation(sqacc[:] if fc == 0 else cbuf[u][:], bank[2 + u][:],
                                         ACT.Square).then_inc(sem("out_sq"), 1)
            body(0, 0)
            body(1, 1)
            body(2, 2)
            body(3, 3)
            act.wait_ge(sem("out_ss"), of("out_ss", k) + 1)
            nc.scalar.activation(ubuf[0][:], bank[7][:], ACT.Sqrt, bias=prm("eps"),
                                 scale=1.0 / D).then_inc(sem("out_sd"), 1)

        def pool_add_square(pool, k, what, c, fc, u):
            pool.wait_ge(sem(f"{what}_sq"), of(f"{what}_sq", k) + c + 1)
            if fc > 1:
                pool.wait_ge(sem(f"{what}_acc"), of(f"{what}_acc", k) + c - 1)
            nc.gpsimd.tensor_tensor(sqacc[:], sqacc[:], cbuf[u][:], ALU.add).then_inc(sem(f"{what}_acc"), 1)

        def pool_out(pool, k, name, per):
            base = BASE[name]
            for c in range(KD):
                for b in range(per):
                    lo(pool, base, c * per + b + 2, c * per + b + 2)
                if c:
                    pool_add_square(pool, k, "out", c, c, c % 2)

        def dve_res(dve, k, m_tile):
            if k >= 0:
                dve.wait_ge(sem("out_sd"), of("out_sd", k) + 1)
                nc.vector.reciprocal(rstd[:], ubuf[0][:]).then_inc(sem("res_rstdm"), 1)
                dve.wait_ge(sem("res_rstdm"), of("res_rstdm", k) + 1)
                dve.wait_ge(sem("out_m"), of("out_m", k) + KD)

            def low(c):
                dve.wait_ge(sem("res_hi"), of("res_hi", k) + c + 1)
                nc.vector.scalar_tensor_tensor(out=ck(xw_lo, c), in0=ck(xres, c), scalar=prm("norm", x_norm(k) + c),
                                               in1=ck(xw_hi, c).bitcast(F32), op0=ALU.mult,
                                               op1=ALU.subtract).then_inc(sem("res_lo"), 1)
            for c in range(KD):
                if k >= 0:
                    if c > 1:
                        dve.wait_ge(sem("res_x"), of("res_x", k) + c - 1)
                    m = cbuf[2 + c % 2]
                    nc.vector.scalar_tensor_tensor(out=m[:], in0=ck(m_tile, c), scalar=prm("norm", m_norm(k) + c),
                                                   in1=rstd[:], op0=ALU.mult, op1=ALU.mult).then_inc(sem("res_t"), 1)
                    dve.wait_ge(sem("res_t"), of("res_t", k) + c + 1)
                    nc.vector.tensor_tensor(ck(xres, c), ck(xres, c), m[:], ALU.add).then_inc(sem("res_x"), 1)
                if k < 3 and c:
                    low(c - 1)
            if k < 3:
                low(KD - 1)
            if k < 3:
                dve.wait_ge(sem("res_sd"), of("res_sd", k) + 1)
                nc.vector.reciprocal(rstd[:], ubuf[0][:]).then_inc(sem("res_rstd"), 1)
                dve.wait_ge(sem("res_rstd"), of("res_rstd", k) + 1)

        def act_res(act, k):
            for c in range(KD):
                if k < 0:
                    act.wait_ge(sem(f"x_in{c}"), 16)
                    if c == 0:
                        act.wait_ge(sem("par_in"), 16)
                else:
                    act.wait_ge(sem("res_x"), of("res_x", k) + c + 1)
                nc.scalar.activation(ck(xw_hi, c), ck(xres, c), ACT.Copy,
                                     scale=prm("norm", x_norm(k) + c)).then_inc(sem("res_hi"), 1)
                if c > 2:
                    act.wait_ge(sem("res_acc"), of("res_acc", k) + c - 2)
                nc.scalar.activation(sqacc[:] if c == 0 else cbuf[c % 2][:], ck(xres, c),
                                     ACT.Square).then_inc(sem("res_sq"), 1)
            act.wait_ge(sem("res_ss"), of("res_ss", k) + 1)
            nc.scalar.activation(ubuf[0][:], bank[7][:], ACT.Sqrt, bias=prm("eps"),
                                 scale=1.0 / D).then_inc(sem("res_sd"), 1)

        def pool_res(pool, k):
            for c in range(1, KD):
                pool_add_square(pool, k, "res", c, c, c % 2)

        def pe_res(pe, k):
            pe.wait_ge(sem("res_acc"), of("res_acc", k) + KD - 1)
            nc.tensor.matmul(bank[7][:], ones[:, 0:P], sqacc[:], start=True, stop=True).then_inc(sem("res_ss"), 1)

        def dve_taps(dve, src, dst, w, n, of, center, taps, count):
            dve.wait_ge(sem(center), count + 1)
            nc.vector.scalar_tensor_tensor(out=req(dst[:])[:, :, 1:SEQ], in0=req(src[:])[:, :, 0:SEQ - 1],
                                           scalar=prm(w, of), in1=req(dst[:])[:, :, 1:SEQ], op0=ALU.mult,
                                           op1=ALU.add).then_inc(sem(taps), 1)
            dve.wait_ge(sem(taps), 2 * count + 1)
            nc.vector.scalar_tensor_tensor(out=req(dst[:])[:, :, 0:SEQ - 1], in0=req(src[:])[:, :, 1:SEQ],
                                           scalar=prm(w, of + 2 * n), in1=req(dst[:])[:, :, 0:SEQ - 1], op0=ALU.mult,
                                           op1=ALU.add).then_inc(sem(taps), 1)

        def scaled(dve, out_ap, src):
            return nc.vector.tensor_tensor(out_ap, src[:], rstd[:], ALU.mult)

        def pe_fin(pe, l):
            base = BASE[f"fin{l}"]
            r = 2 * l

            def body(t, ft):
                for u in range(2):
                    if ft >= 1:
                        pe.wait_ge(sem("fin_u"), of("fin_u", l) + 2 * t - 1 + u)
                    product(pe, base, 2 * t + u, 2 * ft + u, bank[u][:], xw_hi, xw_lo,
                            by_chunk=("res_lo", r) if ft == 0 and u == 0 else None)
                    if ft == 0 and u == 0:
                        pe_res(pe, r)
            turns(pe, 0, FF, body)

        def act_fin(act, l):
            base = BASE[f"fin{l}"]

            def body(t, ft):
                for u in range(2):
                    j = 2 * t + u
                    hi(act, base, j + 2, 2 * ft + u + 2)
                    act.wait_ge(sem("fin_u"), of("fin_u", l) + j + 1)
                    if u == 0 and ft >= 1:
                        act.wait_ge(sem("fin_prod"), of("fin_prod", l) + t)
                    nc.scalar.activation(cbuf[u][:], ubuf[u][:], ACT.Identity, bias=prm(f"fb{l}", u * FF + t),
                                         scale=prm(f"fw{l}", 2 * FF + u * FF + t)).then_inc(sem("fin_mid"), 1)
                    if u == 0:
                        act.wait_ge(sem("fin_taps"), of("fin_taps", l) + 4 * t + 2)
                        if ft >= 1:
                            act.wait_ge(sem("fin_prod"), of("fin_prod", l) + t)
                        nc.scalar.activation(cbuf[2][:], cbuf[0][:], ACT.Gelu_apprx_tanh).then_inc(
                            sem("fin_gelu"), 1)
                act.wait_ge(sem("fin_prod"), of("fin_prod", l) + t + 1)
                nc.scalar.activation(ck(g_hi, t), cbuf[3][:], ACT.Copy).then_inc(sem("fin_hi"), 1)
            turns(act, 0, FF - 1, body)
            body(FF - 1, FF - 1)

        def dve_fin(dve, l):
            base = BASE[f"fin{l}"]

            def body(t, ft):
                for u in range(2):
                    j = 2 * t + u
                    dve.wait_ge(mm, base + j + 1)
                    if ft >= 1:
                        dve.wait_ge(sem("fin_taps"), of("fin_taps", l) + 2 * j - 2)
                    scaled(dve, ubuf[u][:], bank[u]).then_inc(sem("fin_u"), 1)
                    dve_taps(dve, ubuf[u], cbuf[u], f"fw{l}", 2 * FF, u * FF + t, "fin_mid", "fin_taps",
                             2 * FF * l + j)
                dve.wait_ge(sem("fin_taps"), of("fin_taps", l) + 4 * t + 4)
                dve.wait_ge(sem("fin_gelu"), of("fin_gelu", l) + t + 1)
                if ft >= 1:
                    dve.wait_ge(sem("fin_lo"), of("fin_lo", l) + t)
                nc.vector.tensor_tensor(cbuf[3][:], cbuf[2][:], cbuf[1][:], ALU.mult).then_inc(
                    sem("fin_prod"), 1)
                dve.wait_ge(sem("fin_hi"), of("fin_hi", l) + t + 1)
                nc.vector.tensor_tensor(ck(g_lo, t), cbuf[3][:], ck(g_hi, t).bitcast(F32), ALU.subtract).then_inc(
                    sem("fin_lo"), 1)
            turns(dve, 0, FF, body)

        def pool_fin(pool, l):
            base = BASE[f"fin{l}"]

            def body(t, ft):
                for u in range(2):
                    lo(pool, base, 2 * t + u + 2, 2 * ft + u + 2)
            turns(pool, 0, FF - 1, body)
            body(FF - 1, FF - 1)

        def ffn_operand(l):
            half = FF // 2
            return lambda b: (g_hi, g_lo, b * half, [("fin_lo", of("fin_lo", l) + half * (b + 1))])


        CONV0, Z0 = 2, 8

        def pe_hin(pe):
            base = BASE["hin"]
            pe.wait_ge(sem("ones_set"), 1)

            def body(t, ft):
                for u in range(2):
                    if ft >= 1:
                        pe.wait_ge(sem("hin_u"), 2 * t - 1 + u)
                    product(pe, base, 2 * t + u, 2 * ft + u, bank[u][:], xw_hi, xw_lo,
                            by_chunk=("res_lo", -1) if ft == 0 and u == 0 else None)
                    if ft == 0 and u == 0:
                        pe_res(pe, -1)
            turns(pe, 0, 12, body)

        def act_hin(act):
            base = BASE["hin"]

            def his(t, ft, u):
                hi(act, base, 2 * t + u + 2, 2 * ft + u + 2)

            def conv(t, ft):
                for u in range(2):
                    c, fc = 2 * t + u - 4, 2 * ft + u - 4
                    his(t, ft, u)
                    act.wait_ge(sem("hin_u"), 2 * t + u + 1)
                    if fc >= 2:
                        act.wait_ge(sem("hin_silu"), c - 1)
                    nc.scalar.activation(cbuf[u][:], ubuf[u][:], ACT.Identity, bias=prm("cb", c),
                                         scale=prm("cw", 12 + c)).then_inc(sem("hin_mid"), 1)
                    act.wait_ge(sem("hin_taps"), 2 * c + 2)
                    nc.scalar.activation(ck(xbc, c), cbuf[u][:], ACT.Silu).then_inc(sem("hin_silu"), 1)

            def gate(t, ft):
                for u in range(2):
                    his(t, ft, u)
                    act.wait_ge(sem("hin_u"), 2 * t + u + 1)
                    nc.scalar.activation(ck(zbuf, 2 * t + u - 16), ubuf[u][:], ACT.Silu).then_inc(sem("hin_zsilu"), 1)
            for t in range(CONV0):
                for u in range(2):
                    his(t, t, u)
            turns(act, CONV0, Z0, conv)
            for t in range(Z0, 12):
                gate(t, t)

        def dve_hin(dve):
            base = BASE["hin"]
            for j in range(4):
                dve.wait_ge(mm, base + j + 1)
                if j == 0:
                    dve.wait_ge(sem("res_rstd"), of("res_rstd", -1) + 1)
                scaled(dve, ck(mq, j), bank[j % 2]).then_inc(sem("hin_u"), 1)

            def conv(t, ft):
                for u in range(2):
                    c, fc = 2 * t + u - 4, 2 * ft + u - 4
                    dve.wait_ge(mm, base + 2 * t + u + 1)
                    if fc >= 2:
                        dve.wait_ge(sem("hin_taps"), 2 * c - 2)
                    scaled(dve, ubuf[u][:], bank[u]).then_inc(sem("hin_u"), 1)
                    dve_taps(dve, ubuf[u], cbuf[u], "cw", 12, c, "hin_mid", "hin_taps", c)
            turns(dve, CONV0, Z0, conv)
            for t in range(Z0, 12):
                for u in range(2):
                    dve.wait_ge(mm, base + 2 * t + u + 1)
                    if t == Z0:
                        dve.wait_ge(sem("hin_taps"), 22 + 2 * u)
                    else:
                        dve.wait_ge(sem("hin_zsilu"), 2 * (t - Z0) + u - 1)
                    scaled(dve, ubuf[u][:], bank[u]).then_inc(sem("hin_u"), 1)

        def pool_hin(pool):
            base = BASE["hin"]

            def body(t, ft):
                for u in range(2):
                    lo(pool, base, 2 * t + u + 2, 2 * ft + u + 2)
            turns(pool, 0, 11, body)
            body(11, 11)

        group_rstd = [rstd, sqacc]
        dt_f, dta_f, a_f = (ebuf[0][0:64, i * T:(i + 1) * T] for i in range(3))

        def act_dt(act):
            act.wait_ge(sem("hin_taps"), 24)
            nc.scalar.activation(cbuf[2][0:64, :], mq[0:64, 0:T], ACT.Abs,
                                 bias=prm("dtb")[0:64]).then_inc(sem("dt_act"), 1)
            act.wait_ge(sem("dt_act"), 1)
            nc.scalar.activation(cbuf[2][0:64, :], cbuf[2][0:64, :], ACT.Exp, scale=-1.0).then_inc(sem("dt_act"), 1)
            act.wait_ge(sem("dt_act"), 2)
            nc.scalar.activation(cbuf[3][0:64, :], cbuf[2][0:64, :], ACT.Ln,
                                 bias=ones[0:64, 0:1]).then_inc(sem("dt_act"), 1)
            nc.scalar.activation(small[0:64, 0:1], prm("alog")[0:64], ACT.Exp).then_inc(sem("dt_act"), 1)

        def dve_dt(dve):
            n = [0]

            def step(ins):
                n[0] += 1
                ins.then_inc(sem("dt_dve"), 1)

            def done(k):
                dve.wait_ge(sem("dt_dve"), k)
            step(nc.vector.tensor_scalar(dt_f, mq[0:64, 0:T], prm("dtb")[0:64], 0.0, ALU.add, ALU.max))
            dve.wait_ge(sem("dt_act"), 3)
            done(1)
            step(nc.vector.tensor_tensor(dt_f, dt_f, cbuf[3][0:64, :], ALU.add))
            dve.wait_ge(sem("dt_act"), 4)
            done(2)
            step(nc.vector.tensor_scalar(dta_f, dt_f, small[0:64, 0:1], -1.0, ALU.mult, ALU.mult))
            done(3)
            for r in range(NREQ):
                f = slice(r * SEQ, (r + 1) * SEQ)
                step(nc.vector.tensor_tensor_scan(out=a_f[0:32, f], data0=ones[0:32, 0:SEQ], data1=dta_f[0:32, f],
                                                  initial=0.0, op0=ALU.mult, op1=ALU.add))
                step(nc.vector.tensor_tensor_scan(out=a_f[32:64, f][:, ::-1], data0=ones[32:64, 0:SEQ],
                                                  data1=dta_f[32:64, f][:, ::-1],
                                                  initial=0.0, op0=ALU.mult, op1=ALU.add))
            done(7)
            step(nc.vector.tensor_copy(at_hi[:], a_f))
            done(8)
            step(nc.vector.tensor_tensor(at_lo[:], a_f, at_hi[:].bitcast(F32), ALU.subtract))
            dve.wait_ge(sem("dt_T"), 1)
            by_token = bank[2][:].rearrange("p (b w n) -> p b w n", b=NBLK, w=2)
            step(nc.vector.tensor_copy(dtt[:].rearrange("p (b n) -> p b n", b=NBLK), by_token[:, :, 0, :]))
            acol4 = acol[:].rearrange("p (b n) -> p b n", b=NBLK)
            step(nc.vector.tensor_copy(acol4[:, :, 0:32], by_token[:, :, 1, 0:32]))
            step(nc.vector.tensor_scalar(acol4[:, :, 32:64], by_token[:, :, 1, 32:64], -1.0, None, ALU.mult))
            dve.wait_ge(mm, BASE["hin"] + 24)
            done(12)
            for i in range(2 * NBLK):
                blk, half = i // 2, i % 2
                dve.wait_ge(sem("xs_T"), i + 1)
                for d in range(2):
                    at = (d * NBLK + blk) * D + half * T
                    h0 = blk * 64 + d * 32 + half * 8
                    nc.vector.tensor_tensor(xdt[:, at:at + T].rearrange("p (h e) -> p h e", e=HDIM),
                                            bank[4 + i % 2][:].rearrange("p (h e) -> p h e", e=HDIM),
                                            dtt[:, h0:h0 + 8].unsqueeze(2).broadcast_to([P, 8, HDIM]),
                                            ALU.mult).then_inc(sem("xdt_set"), 1)
            for i in range(4):
                g, r = i // 2, i % 2
                dve.wait_ge(sem("cb_mm"), i + 1)
                ps = bank[6 + i % 2]
                for d, a, b, s0 in ((0, 0, 256, 0), (0, 256, 384, 384), (1, 0, 128, 0), (1, 128, 384, 256)):
                    at = ((g * 2 + d) * 2 + r) * 384
                    nc.vector.tensor_tensor(cbm[:, at + a:at + b], ps[:, s0:s0 + b - a],
                                            con("maskB" if d else "maskF", 384)[:, a:b],
                                            ALU.mult).then_inc(sem("cb_set"), 1)

        def pe_dt(pe):
            pe.wait_ge(sem("dt_dve"), 7)
            for b in range(NBLK):
                for w, src in enumerate((dt_f, a_f)):
                    last = nc.tensor.transpose(bank[2][:, b * P + w * 64:b * P + w * 64 + 64],
                                               src[:, b * P:(b + 1) * P], ident[0:64, 0:64])
            last.then_inc(sem("dt_T"), 1)
            pe.wait_ge(sem("hin_silu"), 12)
            for i in range(2 * NBLK):
                blk, half = i // 2, i % 2
                if i >= 2:
                    pe.wait_ge(sem("xdt_set"), 2 * i - 2)
                for c in range(4):
                    last = nc.tensor.transpose(bank[4 + i % 2][:, c * P:(c + 1) * P],
                                               ck(xbc, half * 4 + c)[:, blk * P:(blk + 1) * P], ident[:])
                last.then_inc(sem("xs_T"), 1)
            for i in range(4):
                g, r = i // 2, i % 2
                if i >= 2:
                    pe.wait_ge(sem("cb_set"), 4 * i - 4)
                for s in range(2):
                    last = nc.tensor.matmul(bank[6 + i % 2][:, s * SEQ:(s + 1) * SEQ],
                                            ck(xbc, 8 + g)[:, r * SEQ + s * P:r * SEQ + (s + 1) * P],
                                            ck(xbc, 10 + g)[:, r * SEQ:(r + 1) * SEQ], start=True, stop=True)
                last.then_inc(sem("cb_mm"), 1)

        TILES = [[(r, s, a, b, l0) for r in range(NREQ) for s, a, b, l0 in t]
                 for t in (((0, 0, 256, 0), (1, 256, 384, P)), ((0, 0, 128, 0), (1, 128, 384, 0)))]

        def dve_ssd(dve):
            def pick(n, v, first):
                if not first:
                    dve.wait_ge(sem("a_mm"), 2 * n - 2)
                for d in range(2):
                    nc.vector.tensor_copy(onehot[v % 2][:, d * P:(d + 1) * P],
                                          ident[0:64, bass.ds(32 * d + n, 1)].to_broadcast([64, P])).then_inc(
                                              sem("onehot_set"), 1)

            def least(n, v, first=False):
                dve.wait_ge(sem("a_mm"), 2 * n + 2)
                if not first:
                    dve.wait_ge(sem("y_mm"), n - 3)
                for r, s, a, b, l0 in TILES[1]:
                    nc.vector.tensor_scalar(ebuf[v][:, 768 + r * 384 + a:768 + r * 384 + b],
                                            bank[2 + v % 2][:, r * SEQ + l0:r * SEQ + l0 + b - a],
                                            acol[:, bass.ds((2 * r + s) * 64 + 32 + n, 1)], 0.0, ALU.add,
                                            ALU.min).then_inc(sem("ssd_min"), 1)

            def m(n, v, g):
                dve.wait_ge(sem("ssd_exp"), 2 * n + 2)
                nc.vector.tensor_tensor(ebuf[v][:], ebuf[v][:], cbm[:, g * 3 * T:(g + 1) * 3 * T],
                                        ALU.mult).then_inc(sem("ssd_m"), 1)
            dve.wait_ge(sem("cb_set"), 16)
            pick(0, 0, True)
            pick(1, 1, True)
            least(0, 0, True)
            pick(2, 2, False)
            least(1, 1, True)
            pick(3, 3, False)

            def gated(c):
                dve.wait_ge(sem("y_mm"), 2 * c + 2)
                nc.vector.scalar_tensor_tensor(out=ck(xbc, c), in0=ck(xbc, c), scalar=prm("dskip", c),
                                               in1=bank[4 + c % 2][:], op0=ALU.mult, op1=ALU.add).then_inc(
                                                   sem("ssd_y"), 1)
                dve.wait_ge(sem("ssd_y"), 2 * c + 1)
                nc.vector.tensor_tensor(ck(zbuf, c), ck(zbuf, c), ck(xbc, c), ALU.mult).then_inc(sem("ssd_y"), 1)

            def turn(n0, g, first=False, last=False):
                for v in range(4):
                    if v < 2 or not last:
                        least(n0 + v + 2, (v + 2) % 4, first and v < 2)
                    if not last:
                        pick(n0 + v + 4, v, False)
                    m(n0 + v, v, g)
                    if (n0 + v) % 2 and n0 + v >= 3:
                        gated((n0 + v - 3) // 2)
            turn(0, 0, first=True)
            turn(4, 0)
            turn(8, 1)
            turn(12, 1, last=True)
            gated(KD - 1)
            for g in range(2):
                dve.wait_ge(sem("ssd_sd"), g + 1)
                nc.vector.reciprocal(group_rstd[g][:], group_rstd[g][:]).then_inc(sem("ssd_rs"), 1)

        def act_ssd(act):
            def exps(n, v, first):
                act.wait_ge(sem("a_mm"), 2 * n + 2)
                if not first:
                    act.wait_ge(sem("y_mm"), n - 3)
                for r, s, a, b, l0 in TILES[0]:
                    nc.scalar.activation(ebuf[v][:, r * 384 + a:r * 384 + b],
                                         bank[v % 2][:, r * SEQ + l0:r * SEQ + l0 + b - a], ACT.Relu, scale=-1.0,
                                         bias=acol[:, bass.ds((2 * r + s) * 64 + n, 1)]).then_inc(
                                             sem("ssd_rel"), 1)
                act.wait_ge(sem("ssd_rel"), 4 * n + 4)
                nc.scalar.activation(ebuf[v][:, 0:768], ebuf[v][:, 0:768], ACT.Exp, scale=-1.0).then_inc(
                    sem("ssd_exp"), 1)
                act.wait_ge(sem("ssd_min"), 4 * n + 4)
                nc.scalar.activation(ebuf[v][:, 768:1536], ebuf[v][:, 768:1536], ACT.Exp).then_inc(
                    sem("ssd_exp"), 1)
            act.wait_ge(sem("dt_dve"), 12)
            def square(c):
                act.wait_ge(sem("ssd_y"), 2 * c + 2)
                if c >= 2:
                    act.wait_ge(sem("ssd_ss"), c - 1)
                nc.scalar.activation(sqbuf[c % 2][:], ck(zbuf, c), ACT.Square).then_inc(sem("ssd_sq"), 1)
            for n in range(HEADS):
                exps(n, n % 4, n < 4)
                if n % 2 and n >= 5:
                    square((n - 5) // 2)
            square(KD - 2)
            square(KD - 1)
            for g in range(2):
                act.wait_ge(sem("ssd_ss"), 4 * g + 4)
                nc.scalar.activation(group_rstd[g][:], bank[6 + g][:], ACT.Sqrt, bias=prm("eps"),
                                     scale=2.0 / D).then_inc(sem("ssd_sd"), 1)

        def dve_ssd_norm(dve, c):
            dve.wait_ge(sem("ssd_rs"), c // 4 + 1)
            nc.vector.tensor_tensor(ck(zbuf, c), ck(zbuf, c), group_rstd[c // 4][:], ALU.mult).then_inc(
                sem("ssd_n"), 1)

        def act_ssd_high(act, c):
            act.wait_ge(sem("ssd_n"), c + 1)
            nc.scalar.activation(ck(xw_hi, c), ck(zbuf, c), ACT.Copy, scale=prm("ssdn", c)).then_inc(
                sem("ssd_hi"), 1)

        def dve_ssd_low(dve, c):
            dve.wait_ge(sem("ssd_hi"), c + 1)
            nc.vector.scalar_tensor_tensor(out=ck(xw_lo, c), in0=ck(zbuf, c), scalar=prm("ssdn", c),
                                           in1=ck(xw_hi, c).bitcast(F32), op0=ALU.mult,
                                           op1=ALU.subtract).then_inc(sem("ssd_lo"), 1)

        def pe_ssd(pe):
            def spread(n, first=False):
                v = n % 2
                pe.wait_ge(sem("onehot_set"), 2 * n + 2)
                if not first:
                    pe.wait_ge(sem("ssd_rel"), 4 * n - 4)
                    pe.wait_ge(sem("ssd_min"), 4 * n - 4)
                for d in range(2):
                    nc.tensor.matmul(bank[2 * d + v][:], onehot[v][:, d * P:(d + 1) * P], at_hi[:],
                                     start=True, stop=False)
                    nc.tensor.matmul(bank[2 * d + v][:], onehot[v][:, d * P:(d + 1) * P], at_lo[:],
                                     start=False, stop=True).then_inc(sem("a_mm"), 1)

            def y(n):
                c, u = n // 2, n % 2
                pe.wait_ge(sem("ssd_m"), n + 1)
                if c >= 2 and u == 0:
                    pe.wait_ge(sem("ssd_y"), 2 * c - 3)
                for r in range(NREQ):
                    parts = ((0, 0, 0, 0, 256), (1, 1, 0, 128, 384), (0, 1, P, 256, 384), (1, 0, 0, 0, 128))
                    for i, (d, s, l0, a, b) in enumerate(parts):
                        at, x_at = (d * 2 + r) * 384, (d * NBLK + 2 * r + s) * D + n * HDIM
                        last = nc.tensor.matmul(bank[4 + c % 2][u * HDIM:(u + 1) * HDIM,
                                                                r * SEQ + l0:r * SEQ + l0 + b - a],
                                                xdt[:, x_at:x_at + HDIM], ebuf[n % 4][:, at + a:at + b],
                                                start=i == 0, stop=i == 3)
                last.then_inc(sem("y_mm"), 1)

            def square_sum(c):
                pe.wait_ge(sem("ssd_sq"), c + 1)
                nc.tensor.matmul(bank[6 + c // 4][:], ones[:, 0:P], sqbuf[c % 2][:], start=c % 4 == 0,
                                 stop=c % 4 == 3).then_inc(sem("ssd_ss"), 1)
            pe.wait_ge(sem("dt_dve"), 12)
            spread(0, True)
            spread(1, True)
            spread(2)
            pe.wait_ge(sem("cb_set"), 16)
            for n in range(HEADS):
                if n + 3 < HEADS:
                    spread(n + 3)
                y(n)
                if n % 2 and n >= 7:
                    square_sum((n - 7) // 2)
            for c in range(KD - 3, KD):
                square_sum(c)

        def act_mla_prep(act):
            act.wait_ge(sem("ssd_ss"), 8)
            for i, c in enumerate((1, 2, 3)):
                nc.scalar.activation(cbuf[i][:], ck(mq, c), ACT.Square).then_inc(sem("mla_sq"), 1)
            for i, n in enumerate((P, QLORA)):
                act.wait_ge(sem("mla_ss"), i + 1)
                nc.scalar.activation(ubuf[i][:], bank[6 + i][:], ACT.Sqrt, bias=prm("eps"),
                                     scale=1.0 / n).then_inc(sem("mla_sd"), 1)
            for i, (dst, w) in enumerate(((ckv_hi[:], prm("kvn")), (ck(qn_hi, 0), prm("qn", 0)),
                                          (ck(qn_hi, 1), prm("qn", 1)))):
                act.wait_ge(sem("mla_n"), i + 1)
                nc.scalar.activation(dst, ck(mq, 1 + i), ACT.Copy, scale=w).then_inc(sem("mla_hi"), 1)

        def dve_mla_low(dve):
            for i, (dst, src, w) in enumerate(((ckv_lo[:], ckv_hi[:], prm("kvn")),
                                               (ck(qn_lo, 0), ck(qn_hi, 0), prm("qn", 0)),
                                               (ck(qn_lo, 1), ck(qn_hi, 1), prm("qn", 1)))):
                dve.wait_ge(sem("mla_hi"), i + 1)
                nc.vector.scalar_tensor_tensor(out=dst, in0=ck(mq, 1 + i), scalar=w, in1=src.bitcast(F32),
                                               op0=ALU.mult, op1=ALU.subtract).then_inc(sem("mla_lo"), 1)

        def pe_mla_prep(pe):
            pe.wait_ge(sem("ssd_y"), 16)
            nc.tensor.matmul(bank[0][:], con("seldup"), ck(mq, 0), start=True, stop=True)
            nc.tensor.matmul(bank[1][:], con("selrot"), ck(mq, 0), start=True, stop=True).then_inc(sem("mla_kr"), 1)
            pe.wait_ge(sem("mla_sq"), 3)
            nc.tensor.matmul(bank[6][:], ones[:, 0:P], cbuf[0][:], start=True, stop=True).then_inc(sem("mla_ss"), 1)
            nc.tensor.matmul(bank[7][:], ones[:, 0:P], cbuf[1][:], start=True, stop=False)
            nc.tensor.matmul(bank[7][:], ones[:, 0:P], cbuf[2][:], start=False, stop=True).then_inc(sem("mla_ss"), 1)

        def dve_mla_prep(dve):
            for i in range(2):
                dve.wait_ge(sem("mla_sd"), i + 1)
                nc.vector.reciprocal(ubuf[i][:], ubuf[i][:]).then_inc(sem("mla_rs"), 1)
            dve.wait_ge(sem("mla_rs"), 2)
            for i in range(3):
                nc.vector.tensor_tensor(ck(mq, 1 + i), ck(mq, 1 + i), ubuf[min(i, 1)][:],
                                        ALU.mult).then_inc(sem("mla_n"), 1)
            dve_mla_low(dve)
            dve.wait_ge(sem("mla_n"), 3)
            dve.wait_ge(sem("mla_kr"), 1)
            nc.vector.tensor_tensor(ubuf[0][:], bank[0][:], cosin[:, 0:T], ALU.mult).then_inc(sem("mla_kd"), 1)
            nc.vector.tensor_tensor(ubuf[1][:], bank[1][:], cosin[:, T:2 * T], ALU.mult).then_inc(sem("mla_kd"), 1)
            dve.wait_ge(sem("mla_kd"), 2)
            for u in range(2):
                on, off = slice(64 * u, 64 * u + 64), slice(64 - 64 * u, 128 - 64 * u)
                nc.vector.tensor_tensor(kre[u][on, :], ubuf[0][on, :], ubuf[1][on, :],
                                        ALU.add).then_inc(sem("mla_kd"), 1)
                nc.vector.memset(kre[u][off, :], 0.0).then_inc(sem("mla_kd"), 1)

        def pe_mla(pe):
            base = BASE["mla"]

            def gen(i):
                s = (base + i) % 2
                outs = [("q", 0, 0, 2), ("q", 1, 2, 2), ("r", 0, 4, 2), ("k", 0, 6, 1), ("k", 1, 7, 1)]
                pe.wait_ge(w_lo, base + i + 1)
                if i == 0:
                    pe.wait_ge(sem("mla_lo"), 3)
                    pe.wait_ge(sem("mla_kd"), 6)
                for e, (kind, u, w0, kts) in enumerate(outs):
                    if e >= 2:
                        pe.wait_ge(sem("mla_gen"), 8 * i + e - 1)
                    elif i:
                        pe.wait_ge(sem("mla_gen"), 8 * i - 1 + e)
                    a_hi, a_lo = (ckv_hi, ckv_lo) if kind == "k" else (qn_hi, qn_lo)
                    product(pe, base, i, i, bank[e % 2][:], a_hi, a_lo, kts=kts, w0=w0, last_of_block=False,
                            wait=False).then_inc(sem("mla_g"), 1)
                for e in (5, 6):
                    pe.wait_ge(sem("mla_gen"), 8 * i + e - 1)
                    for h in range(2):
                        blk = 2 * (e - 5) + h
                        o = bank[e % 2][:, h * 256:(h + 1) * 256]
                        tok = slice(blk * P, (blk + 1) * P)
                        nc.tensor.matmul(o, ckv_hi[:, tok], whi[s][:, 8 * P:10 * P], start=True, stop=False)
                        nc.tensor.matmul(o, ckv_lo[:, tok], whi[s][:, 8 * P:10 * P], start=False, stop=False)
                        last = nc.tensor.matmul(o, ckv_hi[:, tok], wlo[s][:, 8 * P:10 * P], start=False, stop=True)
                    last.then_inc(mm if e == 6 else sem("mla_g"), 1)
                pe.wait_ge(sem("mla_gen"), 8 * i + 6)
                nc.tensor.matmul(bank[1][:], con("rot"), ubuf[0][:], start=True, stop=True).then_inc(sem("mla_g"), 1)

            def scores(n):
                i, u = n // 2, n % 2
                pe.wait_ge(sem("mla_gen"), 8 * i + 8)
                if n:
                    pe.wait_ge(sem("mla_exp"), 4 * n)
                for r in range(NREQ):
                    keys = slice(r * SEQ, (r + 1) * SEQ)
                    for qb in range(2):
                        o = bank[2 + r][:, qb * SEQ:(qb + 1) * SEQ]
                        q = slice(r * SEQ + qb * P, r * SEQ + (qb + 1) * P)
                        nc.tensor.matmul(o, qh[u][:, q], kh[u][:, keys], start=True, stop=False)
                        last = nc.tensor.matmul(o, qr[:, q], kre[u][:, keys], start=False, stop=True)
                    last.then_inc(sem("mla_s"), 1)

            def values(n):
                i, u = n // 2, n % 2
                pe.wait_ge(sem("mla_p"), 2 * n + 2)
                for r in range(NREQ):
                    if n:
                        pe.wait_ge(sem("mla_pT_dve" if r else "mla_pT_act"), n)
                    for kb in range(2):
                        for qb in range(2):
                            at = (2 * r + qb) * SEQ + kb * P
                            last = nc.tensor.transpose(bank[4 + r][:, kb * SEQ + qb * P:kb * SEQ + (qb + 1) * P],
                                                       prob[u][:, at:at + P], ident[:])
                    last.then_inc(sem("mla_T"), 1)
                if n >= 2:
                    pe.wait_ge(sem("mla_olo"), n - 1)
                for r in range(NREQ):
                    pe.wait_ge(sem("mla_pT_dve" if r else "mla_pT_act"), n + 1)
                    for kb in range(2):
                        at = (2 * r + kb) * 2 * P + u * P
                        last = nc.tensor.matmul(bank[6 + u][:, r * SEQ:(r + 1) * SEQ], vp[i % 2][:, at:at + P],
                                                probT[:, r * T + kb * SEQ:r * T + (kb + 1) * SEQ],
                                                start=kb == 0, stop=kb == 1)
                last.then_inc(sem("mla_o"), 1)
            for i in range(MHEADS // 2):
                gen(i)
                scores(2 * i)
                if i:
                    values(2 * i - 1)
                scores(2 * i + 1)
                values(2 * i)
            values(MHEADS - 1)

        def act_mla(act):
            base = BASE["mla"]

            def gen(i):
                for e, dst in ((0, qh[0]), (1, qh[1]), (3, kh[0]), (4, kh[1]), (5, None), (6, None)):
                    if e < 6:
                        act.wait_ge(sem("mla_g"), 7 * i + e + 1)
                    else:
                        act.wait_ge(mm, base + i + 1)
                    act.wait_ge(sem("mla_gen"), 8 * i + e)
                    if dst is not None:
                        if i and e == 0:
                            act.wait_ge(sem("mla_s"), 4 * i)
                        out_ap = dst[:]
                    else:
                        if i >= 2:
                            act.wait_ge(sem("mla_o"), 2 * i - 2)
                        out_ap = vp[i % 2][:, (e - 5) * T:(e - 4) * T]
                    nc.scalar.activation(out_ap, bank[e % 2][:], ACT.Copy).then_inc(sem("mla_gen"), 1)
                hi(act, base, i + 2, i + 2)

            def soft(n):
                u = n % 2
                act.wait_ge(sem("mla_nm"), n + 1)
                if n >= 2:
                    act.wait_ge(sem("mla_T"), 2 * n - 2)
                for i in range(4):
                    nc.scalar.activation(prob[u][:, i * SEQ:(i + 1) * SEQ],
                                         bank[2 + i // 2][:, (i % 2) * SEQ:(i % 2 + 1) * SEQ], ACT.Exp,
                                         bias=stat[:, 16 * u + 4 + i:16 * u + 5 + i], scale=QSCALE,
                                         accum_out=stat[:, 16 * u + 8 + i:16 * u + 9 + i]).then_inc(sem("mla_exp"), 1)

            def outs(n):
                act.wait_ge(sem("mla_T"), 2 * n + 1)
                if n:
                    act.wait_ge(sem("mla_o"), n)
                nc.scalar.activation(probT[:, 0:T], bank[4][:], ACT.Copy).then_inc(sem("mla_pT_act"), 1)
                act.wait_ge(sem("mla_o"), n + 1)
                nc.scalar.activation(ck(co_hi, n), bank[6 + n % 2][:], ACT.Copy).then_inc(sem("mla_ohi"), 1)
            for i in range(MHEADS // 2):
                gen(i)
                soft(2 * i)
                act_ssd_high(act, 2 * i)
                if i:
                    outs(2 * i - 1)
                soft(2 * i + 1)
                act_ssd_high(act, 2 * i + 1)
                outs(2 * i)
            outs(MHEADS - 1)

        def dve_mla(dve):
            def gen(i):
                dve.wait_ge(sem("mla_g"), 7 * i + 3)
                dve.wait_ge(sem("mla_gen"), 8 * i + 2)
                nc.vector.tensor_copy(ubuf[0][:], bank[0][:]).then_inc(sem("mla_gen"), 1)
                dve.wait_ge(sem("mla_gen"), 8 * i + 7)
                if i:
                    dve.wait_ge(sem("mla_s"), 4 * i)
                nc.vector.tensor_tensor(qr[:], ubuf[0][:], cosin[:, 0:T], ALU.mult).then_inc(sem("mla_qr"), 1)
                dve.wait_ge(sem("mla_g"), 7 * i + 7)
                nc.vector.tensor_tensor(ubuf[1][:], bank[1][:], cosin[:, T:2 * T], ALU.mult).then_inc(sem("mla_qr"), 1)
                dve.wait_ge(sem("mla_qr"), 2 * i + 2)
                nc.vector.tensor_tensor(qr[:], qr[:], ubuf[1][:], ALU.add).then_inc(sem("mla_gen"), 1)

            def top(n):
                u = n % 2
                for r in range(NREQ):
                    dve.wait_ge(sem("mla_s"), 2 * n + r + 1)
                    nc.vector.tensor_reduce(stat[:, 16 * u + 2 * r:16 * u + 2 * r + 2], req(bank[2 + r][:]), AX.X,
                                            ALU.max).then_inc(sem("mla_mx"), 1)
                dve.wait_ge(sem("mla_mx"), 2 * n + 2)
                nc.vector.tensor_scalar(stat[:, 16 * u + 4:16 * u + 8], stat[:, 16 * u:16 * u + 4], -QSCALE, None,
                                        ALU.mult).then_inc(sem("mla_nm"), 1)

            def norm(n):
                u = n % 2
                dve.wait_ge(sem("mla_exp"), 4 * n + 4)
                nc.vector.reciprocal(stat[:, 16 * u + 12:16 * u + 16],
                                     stat[:, 16 * u + 8:16 * u + 12]).then_inc(sem("mla_p"), 1)
                dve.wait_ge(sem("mla_p"), 2 * n + 1)
                pr = prob[u][:].rearrange("p (i k) -> p i k", i=4)
                nc.vector.tensor_tensor(pr, pr, stat[:, 16 * u + 12:16 * u + 16].unsqueeze(2).broadcast_to(
                    [P, 4, SEQ]), ALU.mult).then_inc(sem("mla_p"), 1)

            def outs(n):
                dve.wait_ge(sem("mla_T"), 2 * n + 2)
                if n:
                    dve.wait_ge(sem("mla_o"), n)
                nc.vector.tensor_copy(probT[:, T:2 * T], bank[5][:]).then_inc(sem("mla_pT_dve"), 1)
                dve.wait_ge(sem("mla_ohi"), n + 1)
                nc.vector.tensor_tensor(ck(co_lo, n), bank[6 + n % 2][:], ck(co_hi, n).bitcast(F32),
                                        ALU.subtract).then_inc(sem("mla_olo"), 1)
            for i in range(MHEADS // 2):
                gen(i)
                top(2 * i)
                dve_ssd_norm(dve, 2 * i)
                norm(2 * i)
                if i:
                    outs(2 * i - 1)
                    dve_ssd_low(dve, 2 * i - 1)
                top(2 * i + 1)
                dve_ssd_norm(dve, 2 * i + 1)
                norm(2 * i + 1)
                outs(2 * i)
                dve_ssd_low(dve, 2 * i)
            outs(MHEADS - 1)
            dve_ssd_low(dve, KD - 1)

        def pool_mla(pool):
            for i in range(4):
                lo(pool, BASE["mla"], i + 2, i + 2)


        G0 = 8

        def pe_gin(pe):
            base = BASE["gin"]
            product(pe, base, 0, 0, bank[0][:], xw_hi, xw_lo, by_chunk=("res_lo", 1))
            pe_res(pe, 1)

            def block(t, ft, u):
                j = 1 + 2 * t + u
                if ft or u:
                    pe.wait_ge(sem("gin_u"), j - 1)
                product(pe, base, j, 1 + 2 * ft + u, bank[1 - u][:], xw_hi, xw_lo)

            def body(t, ft):
                block(t, ft, 0)
                pe.wait_ge(sem("gate_w"), t + 1)
                if ft:
                    pe.wait_ge(sem("gate_min"), t)
                else:
                    pe.wait_ge(sem("gin_u"), 1)
                nc.tensor.matmul(bank[4][:], wsel[:], lrk[:], start=True, stop=True).then_inc(sem("gate_mm"), 1)
                block(t, ft, 1)
            turns(pe, 0, G0, body)
            for t in range(G0, 12):
                for u in range(2):
                    block(t, t, u)
                    i = 2 * (t - G0) + u
                    blk, half = i // 2, i % 2
                    if i == 0:
                        pe.wait_ge(sem("gin_u"), 17)
                    if i >= 2:
                        pe.wait_ge(sem("vtok_dve" if u else "vtok_act"), i // 2)
                    for c in range(4):
                        last = nc.tensor.transpose(bank[2 + u][:, c * P:(c + 1) * P],
                                                   ck(gqkv, 8 + half * 4 + c)[:, blk * P:(blk + 1) * P], ident[:])
                    last.then_inc(sem("v_T"), 1)

        def act_gin(act):
            base = BASE["gin"]

            def body(t, ft):
                hi(act, base, 2 * t + 3, 2 * ft + 3)
                act.wait_ge(sem("gate_mm"), t + 1)
                if ft:
                    act.wait_ge(sem("gate_act"), 3 * t)
                nc.scalar.activation(cbuf[0][:], bank[4][:], ACT.Abs, bias=prm("bgk", t)).then_inc(sem("gate_act"), 1)
                act.wait_ge(sem("gate_act"), 3 * t + 1)
                nc.scalar.activation(cbuf[0][:], cbuf[0][:], ACT.Exp, scale=-1.0).then_inc(sem("gate_act"), 1)
                act.wait_ge(sem("gate_act"), 3 * t + 2)
                if ft:
                    act.wait_ge(sem("gate_sub"), t)
                nc.scalar.activation(cbuf[1][:], cbuf[0][:], ACT.Ln, bias=ones[:, 0:1]).then_inc(sem("gate_act"), 1)
                hi(act, base, 2 * t + 4, 2 * ft + 4)
            act.wait_ge(sem("out_m"), of("out_m", 1) + KD)
            act.dma_start(wgk[:], w_gk).then_inc(sem("wgk_in"), 16)
            act.dma_start(gmask[:], glac[:, 0:T + CH]).then_inc(sem("gmask_in"), 16)
            act.dma_start(tri[:], glac[:, T + CH:T + CH + 2 * P]).then_inc(sem("tri_in"), 16)
            hi(act, base, 2, 2)
            turns(act, 0, G0, body)
            act.wait_ge(sem("carry_set"), CARRIES)
            nc.scalar.activation(carry[:], carry[:], ACT.Exp, scale=GK_NORM).then_inc(sem("carry_exp"), 1)
            for t in range(G0, 12):
                for u in range(2):
                    j = 1 + 2 * t + u
                    hi(act, base, j + 2, j + 2)
                    act.wait_ge(sem("gin_u"), j + 1)
                    nc.scalar.activation(ck(gg, j - 17), ubuf[u][:], ACT.Silu).then_inc(sem("gin_silu"), 1)
                act.wait_ge(sem("v_T"), 2 * (t - G0) + 1)
                nc.scalar.activation(vtok[:, (t - G0) * D:(t - G0) * D + T], bank[2][:], ACT.Copy).then_inc(
                    sem("vtok_act"), 1)

        def way(d, ap):
            return ap[:, ::-1] if d else ap

        CARRIES = 12

        def dve_carries(dve):
            chunks = gl[:].rearrange("p (d i c x) -> p d i c x", d=2, i=GLA_HEADS * NREQ, c=NCH)
            pairs = carry[:].rearrange("p (d i j) -> p d i j", d=2, j=6)
            for i, (src, j) in enumerate(((0, 0), (1, 2), (2, 5))):
                for d in range(2):
                    c, x = (src, CH - 1) if d == 0 else (3 - src, 0)
                    at = j if d == 0 else (0, 1, 3)[i]
                    nc.vector.tensor_copy(pairs[:, d, :, at:at + 1], chunks[:, d, :, c, x:x + 1]).then_inc(
                        sem("carry_set"), 1)
            dve.wait_ge(sem("carry_set"), 6)

            def add(d, to, a, c, x, n=1):
                ins = nc.vector.tensor_tensor(pairs[:, d, :, to:to + n], pairs[:, d, :, a:a + n],
                                              chunks[:, d, :, c, x:x + 1].broadcast_to([P, GLA_HEADS * NREQ, n]),
                                              ALU.add)
                ins.then_inc(sem("carry_set"), 1 if n == 1 else 2)
            add(0, 1, 0, 1, CH - 1)
            add(1, 2, 0, 2, 0)
            dve.wait_ge(sem("carry_set"), 8)
            add(0, 3, 1, 2, CH - 1, 2)
            add(1, 4, 1, 1, 0, 2)

        def dve_gin(dve):
            base = BASE["gin"]

            def pick(t):
                nc.vector.tensor_copy(wsel[:], wgk[:, bass.ds(t * P, P)]).then_inc(sem("gate_w"), 1)

            def part(d):
                def body(t, ft):
                    for u in range(2):
                        dve.wait_ge(mm, base + 2 * t + u + 2)
                        scaled(dve, ck(gqkv, 2 * t + u), bank[1 - u]).then_inc(sem("gin_u"), 1)
                        if u == 0:
                            if ft:
                                dve.wait_ge(sem("gate_scan"), t)
                            dve.wait_ge(sem("gate_act"), 3 * t + 1)
                            nc.vector.tensor_scalar(ubuf[0][:], bank[4][:], prm("bgk", t), 0.0, ALU.add,
                                                    ALU.min).then_inc(sem("gate_min"), 1)
                            if ft < G0 - 1:
                                pick(t + 1)
                    dve.wait_ge(sem("gate_act"), 3 * t + 3)
                    dve.wait_ge(sem("gate_min"), t + 1)
                    nc.vector.tensor_tensor(ubuf[0][:], ubuf[0][:], cbuf[1][:], ALU.subtract).then_inc(
                        sem("gate_sub"), 1)
                    dve.wait_ge(sem("gate_sub"), t + 1)
                    nc.vector.tensor_tensor_scan(out=way(d, gl[:, bass.ds(t * T, T)]),
                                                 data0=way(d, gmask[:, d:d + T]), data1=way(d, ubuf[0][:]),
                                                 initial=0.0, op0=ALU.mult, op1=ALU.add).then_inc(
                                                     sem("gate_scan"), 1)
                return body
            dve.wait_ge(sem("wgk_in"), 16)
            pick(0)
            dve.wait_ge(mm, base + 1)
            dve.wait_ge(sem("res_rstd"), of("res_rstd", 1) + 1)
            scaled(dve, lrk[:], bank[0]).then_inc(sem("gin_u"), 1)
            dve.wait_ge(sem("gmask_in"), 16)
            dve.wait_ge(sem("tri_in"), 16)
            turns(dve, 0, 4, part(0))
            turns(dve, 4, G0 - 1, part(1))
            part(1)(G0 - 1, G0 - 1)
            dve.wait_ge(sem("gate_scan"), G0)
            dve_carries(dve)
            for t in range(G0, 12):
                for u in range(2):
                    dve.wait_ge(mm, base + 2 * t + u + 2)
                    if t > G0:
                        dve.wait_ge(sem("gin_silu"), 2 * (t - G0) + u - 1)
                    scaled(dve, ubuf[u][:], bank[1 - u]).then_inc(sem("gin_u"), 1)
                dve.wait_ge(sem("v_T"), 2 * (t - G0) + 2)
                nc.vector.tensor_copy(vtok[:, (t - G0) * D + T:(t - G0 + 1) * D], bank[3][:]).then_inc(
                    sem("vtok_dve"), 1)

        def pool_gin(pool):
            base = BASE["gin"]
            lo(pool, base, 2, 2)

            def body(t, ft):
                for u in range(2):
                    lo(pool, base, 2 * t + u + 3, 2 * ft + u + 3)
            turns(pool, 0, 10, body)
            for j in range(21, 25):
                lo(pool, base, j + 2, j + 2)

        def kks(d):
            return kk[d][:].rearrange("p (r x) -> p r x", r=NREQ)

        def cross(d, c):
            n = c if d == 0 else NCH - 1 - c
            return (0 if d == 0 else c + 1), n, (0, 0, 1, 3)[n]

        def pe_gla(pe):
            def scores(n):
                hd, d = n // 2, n % 2
                pe.wait_ge(sem("gla_kk"), 5 * n + 5)
                pe.wait_ge(sem("gla_q"), n + 1)
                if hd:
                    pe.wait_ge(sem("gla_att_set"), 8 * hd)
                else:
                    pe.wait_ge(sem("vtok_act"), 4)
                    pe.wait_ge(sem("vtok_dve"), 4)
                for r in range(NREQ):
                    for c in range(NCH):
                        for s in (range(c // 2 + 1) if d == 0 else range(c // 2, 2)):
                            last = nc.tensor.matmul(bank[2 * d + r][:, s * SEQ + c * CH:s * SEQ + (c + 1) * CH],
                                                    kks(d)[:, r, c * SEQ + s * P:c * SEQ + (s + 1) * P],
                                                    qt[d][:, r * SEQ + c * CH:r * SEQ + (c + 1) * CH],
                                                    start=True, stop=True)
                last.then_inc(sem("gla_s"), 1)

            def values(hd):
                pe.wait_ge(sem("gla_att_set"), 8 * hd + 8)
                for w in range(2):
                    if hd:
                        pe.wait_ge(sem("gla_osq"), 2 * hd - 1 + w)
                    for r in range(NREQ):
                        for s in range(2):
                            at = (2 * r + s) * D + hd * 2 * P + w * P
                            last = nc.tensor.matmul(bank[5 + w][:, r * SEQ:(r + 1) * SEQ], vtok[:, at:at + P],
                                                    att[hd % 2][:, (2 * r + s) * SEQ:(2 * r + s + 1) * SEQ],
                                                    start=s == 0, stop=s == 1)
                    last.then_inc(sem("gla_o"), 1)

            def sums(hd):
                pe.wait_ge(sem("gla_osq"), 2 * hd + 2)
                for b in range(NBLK):
                    for w in range(2):
                        last = nc.tensor.matmul(bank[7][:, hd * NBLK + b:hd * NBLK + b + 1],
                                                cbuf[2 * (hd % 2) + w][:, b * P:(b + 1) * P], ones[:, 0:1],
                                                start=w == 0, stop=w == 1)
                last.then_inc(sem("gla_ss"), 1)
            for n in range(8):
                scores(n)
                if n % 2 == 0 and n:
                    values(n // 2 - 1)
                if n % 2 and n > 1:
                    sums(n // 2 - 1)
            values(GLA_HEADS - 1)
            sums(GLA_HEADS - 1)
            for hd in range(GLA_HEADS):
                pe.wait_ge(sem("gla_diag"), hd + 1)
                nc.tensor.matmul(bank[4 + hd][:], ones[:, 0:P], diag[:], start=True, stop=True).then_inc(
                    sem("gla_spread"), 1)

        def act_gla(act):
            def exps(n):
                hd, d = n // 2, n % 2
                if hd:
                    act.wait_ge(sem("gla_s"), n - 1)
                    act.wait_ge(sem("gla_kk"), 5 * n - 5)
                f = slice((d * GLA_HEADS + hd) * T, (d * GLA_HEADS + hd + 1) * T)
                nc.scalar.activation(qt[d][:], gl[:, f], ACT.Exp, scale=GK_NORM).then_inc(sem("gla_e"), 1)
                nc.scalar.activation(ek[d][:], gl[:, f], ACT.Exp, scale=-GK_NORM).then_inc(sem("gla_e"), 1)

            def cross_scores(hd):
                act.wait_ge(sem("gla_dg"), 2 * hd + 2)
                if hd >= 2:
                    act.wait_ge(sem("gla_o"), 2 * hd - 2)
                a = att[hd % 2]
                for r in range(NREQ):
                    nc.scalar.activation(a[:, 2 * r * SEQ + P:2 * r * SEQ + 2 * P], bank[r][:, P:2 * P],
                                         ACT.Copy).then_inc(sem("gla_att_set"), 2)
                    nc.scalar.activation(a[:, (2 * r + 1) * SEQ:(2 * r + 1) * SEQ + P],
                                         bank[2 + r][:, SEQ:SEQ + P], ACT.Copy).then_inc(sem("gla_att_set"), 2)

            def outs(hd):
                for w in range(2):
                    act.wait_ge(sem("gla_o"), 2 * hd + w + 1)
                    nc.scalar.activation(ck(gqkv, 8 + 2 * hd + w), bank[5 + w][:], ACT.Copy).then_inc(
                        sem("gla_om"), 1)
                    if hd >= 2:
                        act.wait_ge(sem("gla_ss"), hd - 1)
                    nc.scalar.activation(cbuf[2 * (hd % 2) + w][:], bank[5 + w][:], ACT.Square).then_inc(
                        sem("gla_osq"), 1)
            act.wait_ge(mm, BASE["gin"] + 25)
            exps(0)
            exps(1)
            for hd in range(GLA_HEADS):
                if hd + 1 < GLA_HEADS:
                    exps(2 * hd + 2)
                cross_scores(hd)
                if hd + 1 < GLA_HEADS:
                    exps(2 * hd + 3)
                if hd:
                    outs(hd - 1)
            outs(GLA_HEADS - 1)
            act.wait_ge(sem("gla_ss"), GLA_HEADS)
            nc.scalar.activation(gsum[:], bank[7][:, 0:GLA_HEADS * NBLK], ACT.Sqrt, bias=prm("eps"),
                                 scale=1.0 / (2 * P)).then_inc(sem("gla_sd"), 1)
            for c in range(KD):
                act.wait_ge(sem("gla_fin"), 2 * c + 2)
                nc.scalar.activation(ck(xw_hi, c), ck(gg, c), ACT.Copy).then_inc(sem("gla_hi"), 1)

        def dve_gla(dve):
            dve.wait_ge(mm, BASE["gin"] + 25)
            for d in range(2):
                for c in ((0, 2) if d == 0 else (1, 3)):
                    s0 = CH * (c + 1) if d == 0 else CH * (c - 1)
                    nc.vector.memset(kks(d)[:, :, c * SEQ + s0:c * SEQ + s0 + CH], 0.0).then_inc(sem("kk_zero"), 1)
            dve.wait_ge(sem("carry_exp"), 1)

            def keys(n):
                hd, d = n // 2, n % 2
                dve.wait_ge(sem("gla_e"), 2 * n + 2)
                if hd:
                    dve.wait_ge(sem("gla_s"), n - 1)
                k = ck(gqkv, 4 + hd).rearrange("p (r c x) -> p r c x", r=NREQ, x=CH)
                e = ek[d][:].rearrange("p (r c x) -> p r c x", r=NREQ, x=CH)
                step = SEQ + CH
                if d == 0:
                    own = kks(d)[:, :, 0:3 * step].rearrange("p r (c y) -> p r c y", y=step)[:, :, :, 0:CH]
                    first, other = 0, 3
                else:
                    own = kks(d)[:, :, CH:].rearrange("p r (c y) -> p r c y", y=step)[:, :, :, SEQ:]
                    first, other = 1, 0
                for to, c in ((own, slice(first, first + 3)),
                              (kks(d)[:, :, other * step:other * step + CH].unsqueeze(2), slice(other, other + 1))):
                    nc.vector.tensor_tensor(to, k[:, :, c], e[:, :, c], ALU.mult).then_inc(sem("gla_kk"), 1)
                nc.vector.scalar_tensor_tensor(out=qt[d][:], in0=ck(gqkv, hd), scalar=QG, in1=qt[d][:],
                                               op0=ALU.mult, op1=ALU.mult).then_inc(sem("gla_q"), 1)
                dve.wait_ge(sem("gla_kk"), 5 * n + 2)
                carries = carry[:].rearrange("p (m r j) -> p m r j", r=NREQ, j=6)[:, d * GLA_HEADS + hd]
                for c in range(NCH):
                    s0, m, j = cross(d, c)
                    if m:
                        to = kks(d)[:, :, c * SEQ + s0 * CH:c * SEQ + (s0 + m) * CH].rearrange(
                            "p r (c x) -> p r c x", x=CH)
                        by = carries[:, :, j:j + m].unsqueeze(3).broadcast_to([P, NREQ, m, CH])
                        nc.vector.tensor_tensor(to, own[:, :, s0 - first:s0 - first + m], by,
                                                ALU.mult).then_inc(sem("gla_kk"), 1)

            def gated(hd):
                dve.wait_ge(sem("gla_spread"), hd + 1)
                for w in range(2):
                    c = 2 * hd + w
                    if hd:
                        dve.wait_ge(sem("gla_fin"), 2 * c - 2)
                    nc.vector.scalar_tensor_tensor(out=ubuf[w][:], in0=ck(gqkv, 8 + c), scalar=prm("glan", w),
                                                   in1=bank[4 + hd][:], op0=ALU.mult, op1=ALU.mult).then_inc(
                                                       sem("gla_fin"), 1)
                    dve.wait_ge(sem("gla_fin"), 2 * c + 1)
                    nc.vector.tensor_tensor(ck(gg, c), ck(gg, c), ubuf[w][:], ALU.mult).then_inc(sem("gla_fin"), 1)

            def own_scores(hd):
                if hd >= 2:
                    dve.wait_ge(sem("gla_o"), 2 * hd - 2)
                dve.wait_ge(sem("gla_s"), 2 * hd + 2)
                blocks = [t.rearrange("p (b x) -> p b x", x=P)[:, 0::3] for t in
                          (bank[0][:], bank[1][:], bank[2][:], bank[3][:], att[hd % 2][:, 0:T],
                           att[hd % 2][:, T:2 * T])]
                masks = [tri[:, i * P:(i + 1) * P].unsqueeze(1).broadcast_to([P, 2, P]) for i in range(2)]
                other = [dg[:, r * SEQ:(r + 1) * SEQ].rearrange("p (b x) -> p b x", x=P) for r in range(NREQ)]
                for r in range(NREQ):
                    nc.vector.tensor_tensor(blocks[4 + r], blocks[r], masks[0], ALU.mult).then_inc(sem("gla_d"), 1)
                    nc.vector.tensor_tensor(other[r], blocks[2 + r], masks[1], ALU.mult).then_inc(sem("gla_d"), 1)
                dve.wait_ge(sem("gla_d"), 4 * hd + 4)
                for r in range(NREQ):
                    nc.vector.tensor_tensor(blocks[4 + r], blocks[4 + r], other[r], ALU.add).then_inc(
                        sem("gla_dg"), 1)
            keys(0)
            keys(1)
            for hd in range(GLA_HEADS):
                if hd + 1 < GLA_HEADS:
                    keys(2 * hd + 2)
                own_scores(hd)
                if hd + 1 < GLA_HEADS:
                    keys(2 * hd + 3)
            dve.wait_ge(sem("gla_sd"), 1)
            nc.vector.reciprocal(gsum[:], gsum[:]).then_inc(sem("gla_rs"), 1)
            dve.wait_ge(sem("gla_rs"), 1)
            for hd in range(GLA_HEADS):
                if hd:
                    dve.wait_ge(sem("gla_spread"), hd)
                nc.vector.tensor_tensor(diag[:].rearrange("p (b x) -> p b x", x=P),
                                        gsum[:, hd * NBLK:(hd + 1) * NBLK].unsqueeze(2).broadcast_to([P, NBLK, P]),
                                        ident[:].unsqueeze(1).broadcast_to([P, NBLK, P]), ALU.mult).then_inc(
                                            sem("gla_diag"), 1)
                if hd:
                    gated(hd - 1)
            gated(GLA_HEADS - 1)

        def pool_gla(pool):
            for c in range(KD):
                pool.wait_ge(sem("gla_hi"), c + 1)
                nc.gpsimd.tensor_tensor(ck(xw_lo, c), ck(gg, c), ck(xw_hi, c).bitcast(F32),
                                        ALU.subtract).then_inc(sem("gla_lo"), 1)

        block = ctx.enter_context(nc.Block())

        @block.sync
        def _(sp):
            sp.dma_start(par[:], params).then_inc(sem("par_in"), 16)
            for c in range(KD):
                sp.dma_start(ck(xres, c), x_in[:, c * T:(c + 1) * T]).then_inc(sem(f"x_in{c}"), 16)
            sp.dma_start(ident[:], consts[:, 0:P]).then_inc(sem("ident_in"), 16)
            g = 0
            for name, count, kt in STREAM:
                n = kt * P
                base = BASE[name]
                for u in range(2):
                    if g >= 2:
                        sp.wait_ge(w_lo, base + u - 1)
                    sp.dma_start(raw[(base + u) % 2][:, 0:n], w_stream[name][u]).then_inc(raw_in[(base + u) % 2], 16)
                with sp.Fori(1, count // 2) as t:
                    for u in range(2):
                        sp.wait_ge(w_lo, 2 * t + (base + u - 1))
                        sp.dma_start(raw[(base + u) % 2][:, 0:n],
                                     w_stream[name][bass.ds(2 * t + u, 1)].rearrange("b p n -> (b p) n")).then_inc(
                                         raw_in[(base + u) % 2], 16)
                if count % 2:
                    sp.wait_ge(w_lo, base + count - 2)
                    sp.dma_start(raw[(base + count - 1) % 2][:, 0:n], w_stream[name][count - 1]).then_inc(
                        raw_in[(base + count - 1) % 2], 16)
                g += count
            for c in range(KD):
                sp.wait_ge(sem("res_x"), of("res_x", 3) + c + 1)
                sp.dma_start(out[:, c * T:(c + 1) * T], ck(xres, c)).then_inc(sem("out_stored"), 16)
            sp.wait_ge(sem("out_stored"), KD * 16)

        def first_two(eng, split):
            for j in range(2):
                split(eng, 0, j, j)

        @block.scalar
        def _(act):
            act.dma_start(cst[:], consts[:, P:NCONST]).then_inc(sem("cst_in"), 16)
            act.dma_start(cosin[:], rope).then_inc(sem("rope_in"), 16)
            first_two(act, hi)
            act_res(act, -1)
            act_hin(act)
            act_dt(act)
            act_ssd(act)
            act_mla_prep(act)
            act_mla(act)
            act_out(act, 0, "hout", 2, m_hyb)
            act_res(act, 0)
            act_fin(act, 0)
            act_out(act, 1, "fout0", 2, m_ffn)
            act_res(act, 1)
            act_gin(act)
            act_gla(act)
            act_out(act, 2, "gout", 1, m_gla)
            act_res(act, 2)
            act_fin(act, 1)
            act_out(act, 3, "fout1", 2, m_ffn)

        @block.gpsimd
        def _(pool):
            first_two(pool, lo)
            pool_res(pool, -1)
            pool_hin(pool)
            pool_mla(pool)
            pool_out(pool, 0, "hout", 2)
            pool_res(pool, 0)
            pool_fin(pool, 0)
            pool_out(pool, 1, "fout0", 2)
            pool_res(pool, 1)
            pool_gin(pool)
            pool_gla(pool)
            pool_out(pool, 2, "gout", 1)
            pool_res(pool, 2)
            pool_fin(pool, 1)
            pool_out(pool, 3, "fout1", 2)

        @block.vector
        def _(dve):
            nc.vector.memset(ones[:], 1.0).then_inc(sem("ones_set"), 1)
            dve.wait_ge(sem("ones_set"), 1)
            dve_res(dve, -1, None)
            dve_hin(dve)
            dve.wait_ge(sem("cst_in"), 16)
            dve.wait_ge(sem("ident_in"), 16)
            dve.wait_ge(sem("rope_in"), 16)
            dve_dt(dve)
            dve_ssd(dve)
            dve_mla_prep(dve)
            dve_mla(dve)
            dve_res(dve, 0, m_hyb)
            dve_fin(dve, 0)
            dve_res(dve, 1, m_ffn)
            dve_gin(dve)
            dve_gla(dve)
            dve_res(dve, 2, m_gla)
            dve_fin(dve, 1)
            dve_res(dve, 3, m_ffn)

        @block.tensor
        def _(pe):
            pe_hin(pe)
            pe.wait_ge(sem("ident_in"), 16)
            pe.wait_ge(sem("cst_in"), 16)
            pe_dt(pe)
            pe_ssd(pe)
            pe_mla_prep(pe)
            pe_mla(pe)
            pe_out(pe, 0, "hout", 2,
                   lambda b: (co_hi, co_lo, 0, [("mla_olo", MHEADS)]) if b else (xw_hi, xw_lo, 0, [("ssd_lo", KD)]))
            pe_fin(pe, 0)
            pe_out(pe, 1, "fout0", 2, ffn_operand(0))
            pe_gin(pe)
            pe_gla(pe)
            pe_out(pe, 2, "gout", 1, lambda b: (xw_hi, xw_lo, 0, None), first_by_chunk=("gla_lo", 0))
            pe_fin(pe, 1)
            pe_out(pe, 3, "fout1", 2, ffn_operand(1))


def _tiles(w, cols):
    kt = w.shape[0] // P
    return w[:, cols].reshape(kt, P, -1, P).transpose(2, 1, 0, 3)


def _by_chunk(v):
    return v.reshape(-1, P).T


def _layout(i):
    a = np.arange
    f32 = np.float32
    sample = {}
    x = np.concatenate([i["x_prompt"][0], i["x_sample"][0]], 0)
    sample["x"] = x.T.reshape(KD, P, T).transpose(1, 0, 2).reshape(P, KD * T)
    dt0, q0, kv0 = 2560, 2592, 2848
    kr0 = kv0 + P
    misc = np.concatenate([dt0 + a(16), kr0 + a(16), dt0 + 16 + a(16), kr0 + a(16), kr0 + a(ROPE)])
    cols = np.concatenate([misc, kv0 + a(P), q0 + a(QLORA), 1024 + a(1536), a(1024)])
    sample["hin"] = _tiles(i["hyb_w_in"][0], cols)
    qb, kvb = i["mla_w_qb"][0], i["mla_w_kvb"][0]
    pairs = []
    for h in range(0, MHEADS, 2):
        q_at, kv_at = h * (NOPE + ROPE), h * 2 * P
        nope = [q_at + a(P), q_at + NOPE + ROPE + a(P)]
        rope = np.concatenate([q_at + NOPE + a(ROPE), q_at + 2 * NOPE + ROPE + a(ROPE)])
        parts = [_tiles(qb, c)[0] for c in (*nope, rope)]
        parts += [kvb[:, kv_at + o:kv_at + o + P].reshape(P, 1, P) for o in (0, 2 * P, P, 3 * P)]
        pairs.append(np.concatenate(parts, 1))
    sample["mla"] = np.stack(pairs)
    sample["hout"] = _tiles(i["hyb_w_out"][0], a(D)).reshape(KD, P, 2, KD, P).transpose(0, 2, 1, 3, 4)
    for l in range(2):
        inner = np.stack([a(FF * P).reshape(FF, P), FF * P + a(FF * P).reshape(FF, P)], 1).reshape(-1)
        sample[f"fin{l}"] = _tiles(i["ffn_w_in"][l], inner)
        sample[f"fout{l}"] = _tiles(i["ffn_w_out"][l], a(D)).reshape(KD, P, 2, FF // 2, P).transpose(0, 2, 1, 3, 4)
    lr0 = 3072
    lr = np.concatenate([lr0 + a(16), lr0 + a(16), lr0 + 16 + a(16), lr0 + a(16), lr0 + a(32), lr0 + a(32)])
    sample["gin"] = _tiles(i["gla_w_in"][0], np.concatenate([lr, a(2048), 2048 + a(1024)]))
    sample["gout"] = _tiles(i["gla_w_out"][0], a(D))
    for n, c, k in STREAM:
        sample[n] = np.ascontiguousarray(sample[n]).reshape(c, P, k * P)
    wgk = np.zeros((P, 2, 4 * P), f32)
    wgk[0:16, 0] = i["gla_w_gk2"][0, 0]
    wgk[32:48, 1] = i["gla_w_gk2"][0, 1]
    sample["wgk"] = wgk.reshape(P, -1)
    par = np.zeros((P, NPARAM), f32)

    def put(name, v, rows=slice(None)):
        par[rows, PCOLS[name]:PCOLS[name] + v.shape[1]] = v
    put("norm", _by_chunk(i["norm_w"]))
    put("cw", _by_chunk(i["ssd_conv_w"][0]))
    put("cb", _by_chunk(i["ssd_conv_b"][0]))
    for d in range(2):
        rows = slice(32 * d, 32 * d + 16)
        put("dtb", i["ssd_dt_bias"][0].reshape(2, 16, 1)[d], rows)
        put("alog", i["ssd_a_log"][0].reshape(2, 16, 1)[d], rows)
    put("dskip", _by_chunk(np.repeat(i["ssd_d"][0], HDIM)))
    put("ssdn", _by_chunk(i["ssd_norm_w"][0]))
    put("qn", _by_chunk(i["mla_q_norm_w"][0]))
    put("kvn", _by_chunk(i["mla_kv_norm_w"][0]))
    put("bgk", _by_chunk(i["gla_b_gk"][0]))
    put("glan", _by_chunk(i["gla_norm_w"][0]))
    for l in range(2):
        put(f"fw{l}", _by_chunk(i["ffn_conv_w"][l]))
        put(f"fb{l}", _by_chunk(i["ffn_conv_b"][l]))
    put("eps", np.full((P, 1), EPS, f32))
    sample["par"] = par
    return sample


def _constants():
    f32 = np.float32
    n = np.arange(P)
    eye = np.eye(P, dtype=f32)
    up = (n[None, :] >= n[:, None]).astype(f32)
    one = np.ones((P, P), f32)
    half = n % ROPE
    rot = np.zeros((P, P), f32)
    src = np.where(half < ROPE // 2, n + ROPE // 2, n - ROPE // 2)
    rot[src, n] = np.where(half < ROPE // 2, -1, 1)
    dup = np.zeros((P, P), f32)
    dup[64 + half, n] = 1
    selrot = np.zeros((P, P), f32)
    selrot[64 + src % ROPE, n] = np.where(half < ROPE // 2, -1, 1)
    cst = np.concatenate([eye, up, one, up, up.T, one, up.T, rot, dup, selrot], 1)
    inv = (f32(1.0) / (f32(10000.0) ** (np.arange(0, ROPE, 2, dtype=f32) / f32(ROPE)))).astype(f32)
    ang = np.arange(SEQ, dtype=f32)[:, None] * inv[None, :]
    table = [np.tile(np.tile(t(ang).T.astype(f32), (4, 1)), (1, NREQ)) for t in (np.cos, np.sin)]
    gmask = np.tile((np.arange(T + CH) % CH != 0).astype(f32), (P, 1))
    return cst, np.concatenate(table, 1), np.concatenate([gmask, up, up.T], 1)


def kernel(**inputs):
    import concourse.bacc as bacc
    from concourse.bass_utils import run_bass_kernel_spmd

    nc = bacc.Bacc("TRN2", target_bir_lowering=False, num_devices=1)
    data = _layout({k: np.asarray(v) for k, v in inputs.items()})
    cst, rope, glac = _constants()
    data |= {"cst": cst, "rope": rope, "glac": glac}
    arrays, aps = {}, {}
    for name, a in data.items():
        arrays[f"in_{name}"] = np.ascontiguousarray(a)
        aps[name] = nc.dram_tensor(f"in_{name}", a.shape, F32, kind="ExternalInput").ap()
    out = nc.dram_tensor("out_y", (P, KD * T), F32, kind="ExternalOutput").ap()
    build_program(nc, aps["x"], {n: aps[n] for n, _, _ in STREAM}, aps["wgk"], aps["par"], aps["cst"], aps["rope"],
                  aps["glac"], out)
    r = run_bass_kernel_spmd(nc, [arrays], core_ids=[0])
    y = r.results[0]["out_y"].reshape(P, KD, T).transpose(2, 1, 0).reshape(NREQ, SEQ, D)
    return np.ascontiguousarray(y[0:1]), np.ascontiguousarray(y[1:2])
```

```python
from contextlib import ExitStack

import concourse.bass as bass
import numpy as np
from concourse import mybir

F32, F32R = mybir.dt.float32, mybir.dt.float32r
ACT, ALU, AX = mybir.ActivationFunctionType, mybir.AluOpType, mybir.AxisListType

P = 128
D = 1024
KD = D // P
SEQ, NREQ = 256, 2
T = SEQ * NREQ
NBLK = T // P
EPS = 1e-6

HEADS, HDIM = 16, 64
GHEADS = 8
QLORA, NOPE, ROPE, MHEADS = 256, 128, 64, 8
QSCALE = float(NOPE + ROPE) ** -0.5
GLA_HEADS, CH = 4, 64
NCH = SEQ // CH
GK_NORM = 1.0 / 16.0
QG = float(P) ** -0.5
FF = 2816 // P

STREAM = [("hin", 24, KD), ("mla", 4, 10), ("hout", 16, KD), ("fin0", 2 * FF, KD), ("fout0", 16, FF // 2),
          ("gin", 25, KD), ("gout", 8, KD), ("fin1", 2 * FF, KD), ("fout1", 16, FF // 2)]
BASE, _at = {}, 0
for _n, _c, _k in STREAM:
    BASE[_n] = _at
    _at += _c
TOTAL = _at
KT_OF = [k for _, c, k in STREAM for _ in range(c)]
KT_MAX = max(KT_OF)

PCOLS = {}
_at = 0
for _n, _c in [("norm", 64), ("cw", 36), ("cb", 12), ("dtb", 1), ("alog", 1), ("dskip", 8), ("ssdn", 8), ("qn", 2),
               ("kvn", 1), ("bgk", 8), ("glan", 2), ("fw0", 132), ("fw1", 132), ("fb0", 44), ("fb1", 44), ("eps", 1)]:
    PCOLS[_n] = _at
    _at += _c
NPARAM = _at

CCOLS = {"ident": 0, "maskF": 128, "maskB": 512, "rot": 896, "seldup": 1024, "selrot": 1152}
NCONST = 1280


def build_program(nc, x_in, w_stream, w_gk, params, consts, rope, glac, out):
    ctx = ExitStack()
    with ctx:
        sems = {}

        def sem(name):
            if name not in sems:
                sems[name] = ctx.enter_context(nc.semaphore(name))
            return sems[name]

        def sb(name, cols, dtype=F32, stack=ctx, parts=P):
            return stack.enter_context(nc.sbuf_tensor(name, [parts, cols], dtype))

        xres = sb("xres", KD * T)
        raw = [sb(f"raw{i}", KT_MAX * P) for i in range(2)]
        whi = [sb(f"whi{i}", KT_MAX * P, F32R) for i in range(2)]
        wlo = [sb(f"wlo{i}", KT_MAX * P, F32R) for i in range(2)]
        rstd = sb("rstd", T)
        sqacc = sb("sqacc", T)
        ubuf = [sb(f"ubuf{i}", T) for i in range(2)]
        with ExitStack() as s:
            xtok_late = sb("xtok1", NBLK * T, F32, s)
        with ExitStack() as s:
            vp1 = sb("vp1", NBLK * 2 * P, F32, s)
            prob1 = sb("prob1", 4 * SEQ, F32, s)
        cbuf = [sb(f"cbuf{i}", T) for i in range(4)]
        par = sb("par", NPARAM)
        ident = sb("ident", P)
        ones = sb("ones", SEQ)
        small = sb("small", 5)
        with ExitStack() as s:
            xw_hi = sb("xw_hi", KD * T, F32R, s)
            xw_lo = sb("xw_lo", KD * T, F32R, s)
        with ExitStack() as s:
            m_ffn = sb("m_ffn", KD * T, F32, s)
        with ExitStack() as s:
            xdt = sb("xdt", 2 * NBLK * D, F32, s)
        with ExitStack() as s:
            kk1 = sb("kk1", NREQ * NCH * SEQ, F32, s)
            dg = sb("dg", NREQ * SEQ, F32, s)
            sb("to_xw_low_part", 7 * T, F32, s)
            att = [sb(f"att{i}", NREQ * 2 * SEQ, F32, s) for i in range(2)]
        sb("xw_region", 2 * KD * T)

        with ExitStack() as s:
            zbuf = sb("zbuf", KD * T, F32, s)
            mq = sb("mq", 4 * T, F32, s)
            co_hi = sb("co_hi", MHEADS * T, F32R, s)
            co_lo = sb("co_lo", MHEADS * T, F32R, s)
            cosin = sb("cosin", 2 * T, F32, s)
            cst = sb("cst", NCONST - P, F32, s)
            with ExitStack() as q:
                xbc = sb("xbc", 12 * T, F32, q)
                with ExitStack() as q2:
                    xtok = [sb("xtok0", NBLK * T, F32, q2), xtok_late]
                ebuf_late = [sb(f"ebuf{i}", 3 * T, F32, q) for i in (2, 3)]
                sqbuf = [sb(f"sqbuf{i}", T, F32, q) for i in range(2)]
            with ExitStack() as q:
                m_hyb = sb("m_hyb", KD * T, F32, q)
            with ExitStack() as q:
                qn_hi = sb("qn_hi", 2 * T, F32R, q)
                qn_lo = sb("qn_lo", 2 * T, F32R, q)
                ckv_hi = sb("ckv_hi", T, F32R, q)
                ckv_lo = sb("ckv_lo", T, F32R, q)
                kre = [sb(f"kre{i}", T, F32, q) for i in range(2)]
                qh = [sb(f"qh{i}", T, F32, q) for i in range(2)]
                qr = sb("qr", T, F32, q)
                kh = [sb(f"kh{i}", T, F32, q) for i in range(2)]
                vp0 = sb("vp0", NBLK * 2 * P, F32, q)
                prob0 = sb("prob0", 4 * SEQ, F32, q)
                probT = sb("probT", 4 * SEQ, F32, q)
                stat = sb("stat", 32, F32, q)
            vp, prob = [vp0, vp1], [prob0, prob1]
        with ExitStack() as s:
            sb("zbuf_mq", 12 * T, F32, s)
            ebuf = [sb(f"ebuf{i}", 3 * T, F32, s) for i in range(2)] + ebuf_late
            cbm = sb("cbm", 4 * 3 * SEQ, F32, s)
            at_hi = sb("at_hi", T, F32R, s, 64)
            at_lo = sb("at_lo", T, F32R, s, 64)
            onehot = [sb(f"onehot{i}", 2 * P, F32R, s, 64) for i in range(2)]
            dtt = sb("dtt", NBLK * 64, F32, s)
            acol = sb("acol", NBLK * 64, F32, s)
        with ExitStack() as s:
            g_hi = sb("g_hi", FF * T, F32R, s)
            g_lo = sb("g_lo", FF * T, F32R, s)
        with ExitStack() as s:
            gqkv = sb("gqkv", 16 * T, F32, s)
            gg = sb("gg", 8 * T, F32, s)
            with ExitStack() as q:
                vtok = sb("vtok", NBLK * D, F32, q)
                lrk = sb("lrk", T, F32, q)
                gl = sb("gl", 2 * GLA_HEADS * T, F32, q)
                carry = sb("carry", 2 * GLA_HEADS * NREQ * 8, F32, q)
                gsum = sb("gsum", 4 * NBLK, F32, q)
                ek = [sb(f"ek{i}", T, F32, q) for i in range(2)]
                qt = [sb(f"qt{i}", T, F32, q) for i in range(2)]
                kk = [sb("kk0", NREQ * NCH * SEQ, F32, q), kk1]
                with ExitStack() as q2:
                    qx = [sb(f"qx{i}", NREQ * P, F32, q2) for i in range(2)]
                    diag = sb("diag", 4 * P, F32, q2)
                wgk = sb("wgk", 2 * 4 * P, F32, q)
                wsel = sb("wsel", P, F32, q)
                gmask = sb("gmask", T + CH, F32, q)
                tri = sb("tri", 2 * P, F32, q)
            with ExitStack() as q:
                m_gla = sb("m_gla", KD * T, F32, q)
        bank = [ctx.enter_context(nc.psum_tensor(f"bank{i}", [P, T], F32)) for i in range(8)]

        def ck(t, c, n=1):
            return t[:, bass.ds(c * T, n * T)]

        def prm(name, c=0):
            return par[:, bass.ds(PCOLS[name] + c, 1)]

        def con(name, n=P):
            return cst[:, CCOLS[name] - P:CCOLS[name] - P + n]

        def req(ap):
            return ap.rearrange("p (r s) -> p r s", r=NREQ)

        ADDS = {"res_hi": 8, "res_sq": 8, "res_lo": 8, "res_acc": 7, "res_ss": 1, "res_sd": 1, "res_rstd": 1,
                "res_rstdm": 1, "res_t": 6, "res_x": 6, "res_pool": 4, "out_m": 8, "out_sq": 8, "out_acc": 6, "out_ss": 1,
                "out_sd": 1, "fin_u": 2 * FF, "fin_mid": 2 * FF, "fin_taps": 4 * FF, "fin_gelu": FF,
                "fin_prod": FF, "fin_hi": FF, "fin_lo": FF, "ssd_lo": KD, "gla_lo": KD}
        FROM_START = ("res_hi", "res_sq", "res_lo", "res_acc", "res_ss", "res_sd", "res_rstd")

        def of(name, k):
            return ADDS[name] * (k + 1 if name in FROM_START else k)

        raw_in = [sem("raw_in0"), sem("raw_in1")]
        w_hi, w_lo, mm = sem("w_hi"), sem("w_lo"), sem("mm_block")

        def turns(eng, t0, t1, body):
            body(t0, t0)
            if t1 - t0 > 3:
                with eng.Fori(t0 + 1, t1) as t:
                    body(t, t0 + 1)
            else:
                for t in range(t0 + 1, t1):
                    body(t, t)

        def hi(act, base, j, fj):
            f = base + fj
            if f >= TOTAL:
                return
            s, n = f % 2, KT_OF[f] * P
            act.wait_ge(raw_in[s], (j - fj) * 8 + (f // 2 + 1) * 16)
            if f >= 2:
                act.wait_ge(mm, base + j - 1)
            nc.scalar.activation(whi[s][:, 0:n], raw[s][:, 0:n], ACT.Copy).then_inc(w_hi, 1)

        def lo(pool, base, j, fj):
            f = base + fj
            if f >= TOTAL:
                return
            s, n = f % 2, KT_OF[f] * P
            pool.wait_ge(w_hi, base + j + 1)
            nc.gpsimd.tensor_tensor(wlo[s][:, 0:n], raw[s][:, 0:n], whi[s][:, 0:n].bitcast(F32),
                                    ALU.subtract).then_inc(w_lo, 1)

        def product(pe, base, j, fj, out_ap, a_hi, a_lo, kts=None, k0=0, w0=0, start=True, stop=True, by_chunk=None,
                    last_of_block=True, wait=True):
            f = base + fj
            s = f % 2
            kts = KT_OF[f] if kts is None else kts
            if wait:
                pe.wait_ge(w_lo, base + j + 1)
            for k in range(kts):
                if by_chunk is not None:
                    pe.wait_ge(sem(by_chunk[0]), of(*by_chunk) + k0 + k + 1)
                ah, al = ck(a_hi, k0 + k), ck(a_lo, k0 + k)
                wh, wl = whi[s][:, (w0 + k) * P:(w0 + k + 1) * P], wlo[s][:, (w0 + k) * P:(w0 + k + 1) * P]
                nc.tensor.matmul(out_ap, wh, ah, start=start and k == 0, stop=False)
                nc.tensor.matmul(out_ap, wh, al, start=False, stop=False)
                last = nc.tensor.matmul(out_ap, wl, ah, start=False, stop=stop and k == kts - 1)
            if last_of_block:
                last.then_inc(mm, 1)
            return last

        def m_norm(k):
            return (k // 2) * 32 + (k % 2) * 16 + 8

        def x_norm(k):
            return ((k + 1) // 2) * 32 + ((k + 1) % 2) * 16

        def obank(u):
            return bank[u]

        def pe_out(pe, k, name, per, a_of_block, first_by_chunk=None, between=None):
            base = BASE[name]

            def body(t, ft):
                for u in range(2):
                    c, fc = 2 * t + u, 2 * ft + u
                    if fc >= 2:
                        pe.wait_ge(sem("out_m"), of("out_m", k) + c - 1)
                    for b in range(per):
                        src_hi, src_lo, k0, ready = a_of_block(b)
                        if ready is not None and fc == 0:
                            for stage, n in ready:
                                pe.wait_ge(sem(stage), n)
                        product(pe, base, c * per + b, fc * per + b, obank(u)[:], src_hi, src_lo, k0=k0,
                                start=b == 0, stop=b == per - 1,
                                by_chunk=first_by_chunk if fc == 0 and b == 0 else None)
                        if between and fc == 0 and b == 0:
                            between()
            turns(pe, 0, KD // 2, body)
            pe.wait_ge(sem("out_acc"), of("out_acc", k) + KD - 2)
            nc.tensor.matmul(bank[7][:], ones[:, 0:P], sqacc[:], start=True, stop=False)
            pe.wait_ge(sem("out_sq"), of("out_sq", k) + KD)
            nc.tensor.matmul(bank[7][:], ones[:, 0:P], cbuf[1][:], start=False, stop=True).then_inc(sem("out_ss"), 1)

        def act_out(act, k, name, per, m_tile):
            base = BASE[name]

            def body(t, ft):
                for u in range(2):
                    c, fc = 2 * t + u, 2 * ft + u
                    last = fc == KD - 1
                    for b in range(per - last):
                        hi(act, base, c * per + b + 2, fc * per + b + 2)
                    if last:
                        nc.scalar.activation(small[:, k + 1:k + 2], prm("eps"), ACT.Sqrt)
                    act.wait_ge(mm, base + (c + 1) * per)
                    if fc > 2:
                        act.wait_ge(sem("out_acc"), of("out_acc", k) + c - 2)
                    nc.scalar.activation(sqacc[:] if fc == 0 else cbuf[u][:], obank(u)[:],
                                         ACT.Square).then_inc(sem("out_sq"), 1)
                    if last:
                        hi(act, base, (c + 1) * per + 1, (fc + 1) * per + 1)
                    nc.scalar.activation(ck(m_tile, c), obank(u)[:], ACT.Copy,
                                         scale=prm("norm", m_norm(k) + c)).then_inc(sem("out_m"), 1)
            body(0, 0)
            body(1, 1)
            body(2, 2)
            body(3, 3)
            act.wait_ge(sem("out_ss"), of("out_ss", k) + 1)
            nc.scalar.activation(ubuf[0][:], bank[7][:], ACT.Sqrt, bias=prm("eps"),
                                 scale=1.0 / D).then_inc(sem("out_sd"), 1)

        def pool_add_square(pool, k, what, c, fc, u):
            pool.wait_ge(sem(f"{what}_sq"), of(f"{what}_sq", k) + c + 1)
            if fc > 1:
                pool.wait_ge(sem(f"{what}_acc"), of(f"{what}_acc", k) + c - 1)
            nc.gpsimd.tensor_tensor(sqacc[:], sqacc[:], cbuf[u][:], ALU.add).then_inc(sem(f"{what}_acc"), 1)

        def pool_out(pool, k, name, per):
            base = BASE[name]
            for c in range(KD):
                for b in range(per):
                    lo(pool, base, c * per + b + 2, c * per + b + 2)
                if 0 < c < KD - 1:
                    pool_add_square(pool, k, "out", c, c, c % 2)

        def dve_res(dve, k, m_tile):
            if k >= 0:
                dve.wait_ge(sem("out_sd"), of("out_sd", k) + 1)
                nc.vector.reciprocal(rstd[:], ubuf[0][:]).then_inc(sem("res_rstdm"), 1)
                dve.wait_ge(sem("res_rstdm"), of("res_rstdm", k) + 1)
                dve.wait_ge(sem("out_m"), of("out_m", k) + KD)

            def low(c):
                dve.wait_ge(sem("res_hi"), of("res_hi", k) + c + 1)
                nc.vector.scalar_tensor_tensor(out=ck(xw_lo, c), in0=ck(xres, c), scalar=prm("norm", x_norm(k) + c),
                                               in1=ck(xw_hi, c).bitcast(F32), op0=ALU.mult,
                                               op1=ALU.subtract).then_inc(sem("res_lo"), 1)

            own = [c for c in range(KD) if k < 0 or c not in pool_chunks(k)]

            def scale(i):
                if i > 1:
                    dve.wait_ge(sem("res_x"), of("res_x", k) + i - 1)
                nc.vector.tensor_tensor(cbuf[2 + i % 2][:], ck(m_tile, own[i]), rstd[:], ALU.mult).then_inc(
                    sem("res_t"), 1)
            if k >= 0:
                scale(0)
            lows = 0
            for i, c in enumerate(own):
                if k >= 0:
                    if i + 1 < len(own):
                        scale(i + 1)
                    dve.wait_ge(sem("res_t"), of("res_t", k) + i + 1)
                    nc.vector.tensor_tensor(ck(xres, c), ck(xres, c), cbuf[2 + i % 2][:],
                                            ALU.add).then_inc(sem("res_x"), 1)
                while k < 3 and lows < c:
                    low(lows)
                    lows += 1
            if k < 3:
                low(KD - 1)
            if k < 3:
                dve.wait_ge(sem("res_sd"), of("res_sd", k) + 1)
                nc.vector.reciprocal(rstd[:], ubuf[0][:]).then_inc(sem("res_rstd"), 1)
                dve.wait_ge(sem("res_rstd"), of("res_rstd", k) + 1)

        def pool_chunks(k):
            return (5, 6, 7) if k == 3 else (3, 6)

        def wait_x(engine, k, c):
            if c in pool_chunks(k):
                engine.wait_ge(sem("res_pool"), of("res_pool", k) + 2 * pool_chunks(k).index(c) + 2)
            else:
                engine.wait_ge(sem("res_x"), of("res_x", k) + c + 1 - sum(q < c for q in pool_chunks(k)))

        def act_res(act, k):
            for c in range(KD):
                if k < 0:
                    act.wait_ge(sem(f"x_in{c}"), 16)
                    if c == 0:
                        act.wait_ge(sem("par_in"), 16)
                else:
                    wait_x(act, k, c)
                nc.scalar.activation(ck(xw_hi, c), ck(xres, c), ACT.Copy,
                                     scale=prm("norm", x_norm(k) + c)).then_inc(sem("res_hi"), 1)
                if c > 2:
                    act.wait_ge(sem("res_acc"), of("res_acc", k) + c - 2)
                nc.scalar.activation(sqacc[:] if c == 0 else cbuf[c % 2][:], ck(xres, c),
                                     ACT.Square).then_inc(sem("res_sq"), 1)
                if k < 0 and c == 4:
                    hi(act, 0, 1, 1)
            base = BASE[{-1: "hin", 0: "fin0", 1: "gin", 2: "fin1"}[k]]
            hi(act, base, 2, 2)
            act.wait_ge(sem("res_ss"), of("res_ss", k) + 1)
            nc.scalar.activation(ubuf[0][:], bank[7][:], ACT.Sqrt, bias=prm("eps"),
                                 scale=1.0 / D).then_inc(sem("res_sd"), 1)

        def pool_res(pool, k, m_tile):
            def update(c):
                n = of("res_pool", k) + 2 * pool_chunks(k).index(c) + 1
                nc.gpsimd.tensor_tensor(ck(m_tile, c), ck(m_tile, c), rstd[:], ALU.mult).then_inc(sem("res_pool"), 1)
                pool.wait_ge(sem("res_pool"), n)
                nc.gpsimd.tensor_tensor(ck(xres, c), ck(xres, c), ck(m_tile, c), ALU.add).then_inc(
                    sem("res_pool"), 1)
            if k >= 0:
                pool.wait_ge(sem("res_rstdm"), of("res_rstdm", k) + 1)
                pool.wait_ge(sem("out_m"), of("out_m", k) + KD)
            if k == 3:
                for c in pool_chunks(k):
                    update(c)
                return
            for c in range(1, KD):
                if k >= 0 and c in (1, 3):
                    update(pool_chunks(k)[c // 2])
                pool_add_square(pool, k, "res", c, c, c % 2)
                if k < 0 and c == 4:
                    lo(pool, 0, 1, 1)

        def pe_res(pe, k):
            pe.wait_ge(sem("res_acc"), of("res_acc", k) + KD - 1)
            nc.tensor.matmul(bank[7][:], ones[:, 0:P], sqacc[:], start=True, stop=True).then_inc(sem("res_ss"), 1)

        def product_and_res(pe, k, base, j, out_ap):
            half = KD // 2
            product(pe, base, j, j, out_ap, xw_hi, xw_lo, kts=half, stop=False, last_of_block=False)
            pe_res(pe, k)
            product(pe, base, j, j, out_ap, xw_hi, xw_lo, kts=half, k0=half, w0=half, start=False, wait=False)

        def dve_taps(dve, src, dst, w, n, of, center, taps, count):
            dve.wait_ge(sem(center), count + 1)
            nc.vector.scalar_tensor_tensor(out=req(dst[:])[:, :, 1:SEQ], in0=req(src[:])[:, :, 0:SEQ - 1],
                                           scalar=prm(w, of), in1=req(dst[:])[:, :, 1:SEQ], op0=ALU.mult,
                                           op1=ALU.add).then_inc(sem(taps), 1)
            dve.wait_ge(sem(taps), 2 * count + 1)
            nc.vector.scalar_tensor_tensor(out=req(dst[:])[:, :, 0:SEQ - 1], in0=req(src[:])[:, :, 1:SEQ],
                                           scalar=prm(w, of + 2 * n), in1=req(dst[:])[:, :, 0:SEQ - 1], op0=ALU.mult,
                                           op1=ALU.add).then_inc(sem(taps), 1)

        def scaled(dve, out_ap, src):
            return nc.vector.tensor_tensor(out_ap, src[:], rstd[:], ALU.mult)

        def fbank(ft, u):
            return bank[u if ft == 0 else 2 + u]

        def pe_fin(pe, l):
            base = BASE[f"fin{l}"]
            r = 2 * l

            def body(t, ft):
                for u in range(2):
                    if ft >= 2:
                        pe.wait_ge(sem("fin_u"), of("fin_u", l) + 2 * t - 1 + u)
                    if ft == 0 and u == 1:
                        product_and_res(pe, r, base, 1, fbank(ft, u)[:])
                    else:
                        product(pe, base, 2 * t + u, 2 * ft + u, fbank(ft, u)[:], xw_hi, xw_lo,
                                by_chunk=("res_lo", r) if ft == 0 else None)
            body(0, 0)
            turns(pe, 1, FF, body)

        def act_fin(act, l):
            base = BASE[f"fin{l}"]

            def body(t, ft):
                for u in range(2):
                    j = 2 * t + u
                    if ft == 0:
                        hi(act, base, 3 + u, 3 + u)
                    elif ft > 1 or u:
                        hi(act, base, j + 2, 2 * ft + u + 2)
                    act.wait_ge(sem("fin_u"), of("fin_u", l) + j + 1)
                    if u == 0 and ft >= 1:
                        act.wait_ge(sem("fin_prod"), of("fin_prod", l) + t)
                    nc.scalar.activation(cbuf[u][:], ubuf[u][:], ACT.Identity, bias=prm(f"fb{l}", u * FF + t),
                                         scale=prm(f"fw{l}", 2 * FF + u * FF + t)).then_inc(sem("fin_mid"), 1)
                    if u == 0:
                        act.wait_ge(sem("fin_taps"), of("fin_taps", l) + 4 * t + 2)
                        if ft >= 1:
                            act.wait_ge(sem("fin_prod"), of("fin_prod", l) + t)
                        nc.scalar.activation(cbuf[2][:], cbuf[0][:], ACT.Gelu_apprx_tanh).then_inc(
                            sem("fin_gelu"), 1)
                act.wait_ge(sem("fin_prod"), of("fin_prod", l) + t + 1)
                nc.scalar.activation(ck(g_hi, t), cbuf[3][:], ACT.Copy).then_inc(sem("fin_hi"), 1)
            body(0, 0)
            turns(act, 1, FF - 1, body)
            body(FF - 1, FF - 1)

        def dve_fin(dve, l):
            base = BASE[f"fin{l}"]

            def body(t, ft):
                for u in range(2):
                    j = 2 * t + u
                    dve.wait_ge(mm, base + j + 1)
                    if ft >= 1:
                        dve.wait_ge(sem("fin_taps"), of("fin_taps", l) + 2 * j - 2)
                    scaled(dve, ubuf[u][:], fbank(ft, u)).then_inc(sem("fin_u"), 1)
                    dve_taps(dve, ubuf[u], cbuf[u], f"fw{l}", 2 * FF, u * FF + t, "fin_mid", "fin_taps",
                             2 * FF * l + j)
                dve.wait_ge(sem("fin_taps"), of("fin_taps", l) + 4 * t + 4)
                dve.wait_ge(sem("fin_gelu"), of("fin_gelu", l) + t + 1)
                if ft >= 1:
                    dve.wait_ge(sem("fin_lo"), of("fin_lo", l) + t)
                nc.vector.tensor_tensor(cbuf[3][:], cbuf[2][:], cbuf[1][:], ALU.mult).then_inc(
                    sem("fin_prod"), 1)
                dve.wait_ge(sem("fin_hi"), of("fin_hi", l) + t + 1)
                nc.vector.tensor_tensor(ck(g_lo, t), cbuf[3][:], ck(g_hi, t).bitcast(F32), ALU.subtract).then_inc(
                    sem("fin_lo"), 1)
            body(0, 0)
            turns(dve, 1, FF, body)

        def pool_fin(pool, l):
            base = BASE[f"fin{l}"]

            def body(t, ft):
                for u in range(2):
                    lo(pool, base, 2 * t + u + 2, 2 * ft + u + 2)
            turns(pool, 0, FF - 1, body)
            body(FF - 1, FF - 1)

        def ffn_operand(l):
            half = FF // 2
            return lambda b: (g_hi, g_lo, b * half, [("fin_lo", of("fin_lo", l) + half * (b + 1))])


        CONV0, Z0 = 2, 8
        SIDE = 6

        def pe_hin(pe):
            base = BASE["hin"]
            pe.wait_ge(sem("ones_set"), 1)

            def body(t, ft):
                for u in range(2):
                    if ft >= 2:
                        pe.wait_ge(sem("hin_u"), 2 * t - 1 + u)
                    if ft == 0 and u == 1:
                        product_and_res(pe, -1, base, 1, bank[5][:])
                    else:
                        product(pe, base, 2 * t + u, 2 * ft + u, bank[u if ft else 4 + u][:], xw_hi, xw_lo,
                                by_chunk=("res_lo", -1) if ft == 0 else None)
            body(0, 0)
            body(1, 1)
            pe.wait_ge(sem("ident_in"), 16)
            pe.wait_ge(sem("cst_in"), 16)
            turns(pe, CONV0, SIDE, body)
            pe_dt_turn(pe)
            pe_mla_squares(pe)
            turns(pe, SIDE, Z0, body)
            for t in range(Z0, 12):
                if t == 11:
                    pe_spread(pe, 0, True)
                body(t, t)
                pe_x_turn(pe, t - Z0)

        def act_hin(act):
            base = BASE["hin"]

            def his(t, ft, u):
                hi(act, base, 2 * t + u + 2, 2 * ft + u + 2)

            def conv(t, ft):
                for u in range(2):
                    c, fc = 2 * t + u - 4, 2 * ft + u - 4
                    his(t, ft, u)
                    act.wait_ge(sem("hin_u"), 2 * t + u + 1)
                    if fc >= 2:
                        act.wait_ge(sem("hin_silu"), c - 1)
                    nc.scalar.activation(cbuf[u][:], ubuf[u][:], ACT.Identity, bias=prm("cb", c),
                                         scale=prm("cw", 12 + c)).then_inc(sem("hin_mid"), 1)
                    act.wait_ge(sem("hin_taps"), 2 * c + 2)
                    nc.scalar.activation(ck(xbc, c), cbuf[u][:], ACT.Silu).then_inc(sem("hin_silu"), 1)

            def gate(t, ft):
                for u in range(2):
                    his(t, ft, u)
                    act.wait_ge(sem("hin_u"), 2 * t + u + 1)
                    nc.scalar.activation(ck(zbuf, 2 * t + u - 16), ubuf[u][:], ACT.Silu).then_inc(sem("hin_zsilu"), 1)
            his(0, 0, 1)
            act_dt(act)
            his(1, 1, 0)
            his(1, 1, 1)
            act_mla_squares(act)
            turns(act, CONV0, SIDE, conv)
            act_mla_deviation(act)
            turns(act, SIDE, Z0, conv)
            for t in range(Z0, 12):
                gate(t, t)
                act.wait_ge(sem("xs_T"), 2 * (t - Z0) + 1)
                nc.scalar.activation(xtok[0][:, (t - Z0) * T:(t - Z0 + 1) * T], bank[4][:],
                                     ACT.Copy).then_inc(sem("xtok_act"), 1)

        def dve_hin(dve):
            base = BASE["hin"]
            for j in range(4):
                dve.wait_ge(mm, base + j + 1)
                if j == 0:
                    dve.wait_ge(sem("res_rstd"), of("res_rstd", -1) + 1)
                scaled(dve, ck(mq, j), bank[4 + j if j < 2 else j % 2]).then_inc(sem("hin_u"), 1)
                if j == 1:
                    dve_dt(dve)

            def conv(t, ft):
                for u in range(2):
                    c, fc = 2 * t + u - 4, 2 * ft + u - 4
                    dve.wait_ge(mm, base + 2 * t + u + 1)
                    if fc >= 2:
                        dve.wait_ge(sem("hin_taps"), 2 * c - 2)
                    scaled(dve, ubuf[u][:], bank[u]).then_inc(sem("hin_u"), 1)
                    dve_taps(dve, ubuf[u], cbuf[u], "cw", 12, c, "hin_mid", "hin_taps", c)
            turns(dve, CONV0, SIDE, conv)
            dve_dt_by_token(dve)
            turns(dve, SIDE, Z0, conv)
            dve.wait_ge(sem("cst_in"), 16)
            dve.wait_ge(sem("ident_in"), 16)
            for t in range(Z0, 12):
                for u in range(2):
                    dve.wait_ge(mm, base + 2 * t + u + 1)
                    if t == Z0:
                        dve.wait_ge(sem("hin_taps"), 22 + 2 * u)
                    else:
                        dve.wait_ge(sem("hin_zsilu"), 2 * (t - Z0) + u - 1)
                    scaled(dve, ubuf[u][:], bank[u]).then_inc(sem("hin_u"), 1)
                    if t == Z0:
                        dve_mla_rstd(dve, u)
                dve_x_turn(dve, t - Z0)

        def pool_hin(pool):
            base = BASE["hin"]

            def body(t, ft):
                for u in range(2):
                    lo(pool, base, 2 * t + u + 2, 2 * ft + u + 2)
            turns(pool, 0, 11, body)
            lo(pool, base, 24, 24)

        group_rstd = [rstd, sqacc]
        dt_f, dta_f, a_f = (ebuf[0][0:64, i * T:(i + 1) * T] for i in range(3))

        def act_dt(act):
            act.wait_ge(sem("hin_u"), 1)
            nc.scalar.activation(cbuf[2][0:64, :], mq[0:64, 0:T], ACT.Abs,
                                 bias=prm("dtb")[0:64]).then_inc(sem("dt_act"), 1)
            act.wait_ge(sem("dt_act"), 1)
            nc.scalar.activation(cbuf[2][0:64, :], cbuf[2][0:64, :], ACT.Exp, scale=-1.0).then_inc(sem("dt_act"), 1)
            act.wait_ge(sem("dt_act"), 2)
            nc.scalar.activation(cbuf[3][0:64, :], cbuf[2][0:64, :], ACT.Ln,
                                 bias=ones[0:64, 0:1]).then_inc(sem("dt_act"), 1)
            nc.scalar.activation(small[0:64, 0:1], prm("alog")[0:64], ACT.Exp).then_inc(sem("dt_act"), 1)

        def dve_dt(dve):
            def step(ins):
                ins.then_inc(sem("dt_dve"), 1)

            def done(k):
                dve.wait_ge(sem("dt_dve"), k)
            dve.wait_ge(sem("hin_u"), 1)
            step(nc.vector.tensor_scalar(dt_f, mq[0:64, 0:T], prm("dtb")[0:64], 0.0, ALU.add, ALU.max))
            dve.wait_ge(sem("dt_act"), 3)
            done(1)
            step(nc.vector.tensor_tensor(dt_f, dt_f, cbuf[3][0:64, :], ALU.add))
            dve.wait_ge(sem("dt_act"), 4)
            done(2)
            step(nc.vector.tensor_scalar(dta_f, dt_f, small[0:64, 0:1], -1.0, ALU.mult, ALU.mult))
            done(3)
            for r in range(NREQ):
                f = slice(r * SEQ, (r + 1) * SEQ)
                step(nc.vector.tensor_tensor_scan(out=a_f[0:32, f], data0=ones[0:32, 0:SEQ], data1=dta_f[0:32, f],
                                                  initial=0.0, op0=ALU.mult, op1=ALU.add))
                step(nc.vector.tensor_tensor_scan(out=a_f[32:64, f][:, ::-1], data0=ones[32:64, 0:SEQ],
                                                  data1=dta_f[32:64, f][:, ::-1],
                                                  initial=0.0, op0=ALU.mult, op1=ALU.add))
            done(7)
            step(nc.vector.tensor_copy(at_hi[:], a_f))
            done(8)
            step(nc.vector.tensor_tensor(at_lo[:], a_f, at_hi[:].bitcast(F32), ALU.subtract))

        def dve_dt_by_token(dve):
            dve.wait_ge(sem("dt_T"), 1)
            by_token = bank[2][:].rearrange("p (b w n) -> p b w n", b=NBLK, w=2)
            nc.vector.tensor_copy(dtt[:].rearrange("p (b n) -> p b n", b=NBLK), by_token[:, :, 0, :]).then_inc(
                sem("dt_dve"), 1)
            acol4 = acol[:].rearrange("p (b n) -> p b n", b=NBLK)
            nc.vector.tensor_copy(acol4[:, :, 0:32], by_token[:, :, 1, 0:32]).then_inc(sem("dt_dve"), 1)
            nc.vector.tensor_scalar(acol4[:, :, 32:64], by_token[:, :, 1, 32:64], -1.0, None, ALU.mult).then_inc(
                sem("dt_dve"), 1)

        def pe_dt_turn(pe):
            pe.wait_ge(sem("dt_dve"), 7)
            for b in range(NBLK):
                for w, src in enumerate((dt_f, a_f)):
                    last = nc.tensor.transpose(bank[2][:, b * P + w * 64:b * P + w * 64 + 64],
                                               src[:, b * P:(b + 1) * P], ident[0:64, 0:64])
            last.then_inc(sem("dt_T"), 1)

        def pe_x_turn(pe, i):
            if i == 0:
                pe.wait_ge(sem("hin_silu"), 12)
            else:
                pe.wait_ge(sem("xtok_act"), i)
                pe.wait_ge(sem("xtok_dve"), i)
            for half in range(2):
                for c in range(4):
                    last = nc.tensor.transpose(bank[4 + half][:, c * P:(c + 1) * P],
                                               ck(xbc, half * 4 + c)[:, i * P:(i + 1) * P], ident[:])
                last.then_inc(sem("xs_T"), 1)
            g, r = i // 2, i % 2
            if i:
                pe.wait_ge(sem("cb_set"), 4 * i)
            if i < 2:
                pe.wait_ge(sem("mla_sd"), 2)
            for s in range(2):
                last = nc.tensor.matmul(bank[6][:, s * SEQ:(s + 1) * SEQ],
                                        ck(xbc, 8 + g)[:, r * SEQ + s * P:r * SEQ + (s + 1) * P],
                                        ck(xbc, 10 + g)[:, r * SEQ:(r + 1) * SEQ], start=True, stop=True)
            last.then_inc(sem("cb_mm"), 1)

        def dve_x_turn(dve, i):
            g, r = i // 2, i % 2
            dve.wait_ge(sem("xs_T"), 2 * i + 2)
            nc.vector.tensor_copy(xtok[1][:, i * T:(i + 1) * T], bank[5][:]).then_inc(sem("xtok_dve"), 1)
            dve.wait_ge(sem("cb_mm"), i + 1)
            for d, a, b, s0 in ((0, 0, 256, 0), (0, 256, 384, 384), (1, 0, 128, 0), (1, 128, 384, 256)):
                at = ((g * 2 + d) * 2 + r) * 384
                nc.vector.tensor_tensor(cbm[:, at + a:at + b], bank[6][:, s0:s0 + b - a],
                                        con("maskB" if d else "maskF", 384)[:, a:b],
                                        ALU.mult).then_inc(sem("cb_set"), 1)
            if i == 0:
                dve_mla_scale(dve)
            if i == 2:
                dve_pick(dve, 0, 0, True)
                dve_pick(dve, 1, 1, True)

        def xdt_part(engine, d, half, blk):
            at = (d * NBLK + blk) * D + half * T
            h0 = blk * 64 + d * 32 + half * 8
            return engine.tensor_tensor(xdt[:, at:at + T].rearrange("p (h e) -> p h e", e=HDIM),
                                        xtok[half][:, blk * T:(blk + 1) * T].rearrange("p (h e) -> p h e", e=HDIM),
                                        dtt[:, h0:h0 + 8].unsqueeze(2).broadcast_to([P, 8, HDIM]), ALU.mult)

        def dve_xdt(dve):
            dve.wait_ge(mm, BASE["hin"] + 24)
            dve.wait_ge(sem("xtok_act"), NBLK)
            dve.wait_ge(sem("dt_dve"), 12)
            for blk in range(NBLK):
                xdt_part(nc.vector, 0, 0, blk).then_inc(sem("xdt_dve"), 1)

        def pool_xdt(pool):
            pool.wait_ge(mm, BASE["hin"] + 24)
            pool.wait_ge(sem("xtok_act"), NBLK)
            pool.wait_ge(sem("dt_dve"), 12)
            for blk in range(NBLK):
                xdt_part(nc.gpsimd, 1, 0, blk).then_inc(sem("xdt_pool"), 1)
            pool.wait_ge(sem("xtok_dve"), NBLK)

        def group_adds(c):
            return c - c // 4

        def pool_ssd(pool):
            def add_square(c):
                pool.wait_ge(sem("ssd_sq"), c + 1)
                if c % 4:
                    if c % 4 > 1:
                        pool.wait_ge(sem("ssd_acc"), group_adds(c) - 1)
                    acc = group_rstd[c // 4]
                    nc.gpsimd.tensor_tensor(acc[:], acc[:], sqbuf[c % 2][:], ALU.add).then_inc(sem("ssd_acc"), 1)
            for n in range(HEADS):
                v, at = n % 4, (n // 8) * 3 * T + 768
                pool.wait_ge(sem("ssd_exp"), 2 * n + 2)
                nc.gpsimd.tensor_tensor(ebuf[v][:, 768:1536], ebuf[v][:, 768:1536], cbm[:, at:at + 768],
                                        ALU.mult).then_inc(sem("ssd_mb"), 1)
                if n < 2 * NBLK:
                    xdt_part(nc.gpsimd, n % 2, 1, n // 2).then_inc(sem("xdt_pool"), 1)
                if n % 2 and n >= 7:
                    add_square((n - 7) // 2)
                if n == HEADS // 2:
                    lo(pool, BASE["hin"], 25, 25)
            for c in range(KD - 3, KD):
                add_square(c)

        TILES = [[(r, s, a, b, l0) for r in range(NREQ) for s, a, b, l0 in t]
                 for t in (((0, 0, 256, 0), (1, 256, 384, P)), ((0, 0, 128, 0), (1, 128, 384, 0)))]

        def abank(n, d):
            return bank[2 * (1 - n % 2) + d]

        def dve_pick(dve, n, v, first):
            if not first:
                dve.wait_ge(sem("a_mm"), 2 * n - 2)
            for d in range(2):
                nc.vector.tensor_copy(onehot[v % 2][:, d * P:(d + 1) * P],
                                      ident[0:64, bass.ds(32 * d + n, 1)].to_broadcast([64, P])).then_inc(
                                          sem("onehot_set"), 1)

        def dve_ssd(dve):
            def least(n, v, first=False):
                dve.wait_ge(sem("a_mm"), 2 * n + 2)
                if not first:
                    dve.wait_ge(sem("y_mm"), n - 3)
                for r, s, a, b, l0 in TILES[1]:
                    nc.vector.tensor_scalar(ebuf[v][:, 768 + r * 384 + a:768 + r * 384 + b],
                                            abank(v, 1)[:, r * SEQ + l0:r * SEQ + l0 + b - a],
                                            acol[:, bass.ds((2 * r + s) * 64 + 32 + n, 1)], 0.0, ALU.add,
                                            ALU.min).then_inc(sem("ssd_min"), 1)

            def m(n, v, g):
                dve.wait_ge(sem("ssd_exp"), 2 * n + 1)
                nc.vector.tensor_tensor(ebuf[v][:, 0:768], ebuf[v][:, 0:768], cbm[:, g * 3 * T:g * 3 * T + 768],
                                        ALU.mult).then_inc(sem("ssd_m"), 1)
            dve.wait_ge(sem("cb_set"), 16)
            least(0, 0, True)
            dve_pick(dve, 2, 2, False)
            least(1, 1, True)
            dve_pick(dve, 3, 3, False)
            dve_xdt(dve)
            dve.wait_ge(sem("xdt_pool"), NBLK)
            dve.wait_ge(sem("xdt_dve"), NBLK)

            def gated(c):
                dve.wait_ge(sem("y_mm"), 2 * c + 2)
                nc.vector.scalar_tensor_tensor(out=ck(xbc, c), in0=ck(xbc, c), scalar=prm("dskip", c),
                                               in1=bank[4 + c % 2][:], op0=ALU.mult, op1=ALU.add).then_inc(
                                                   sem("ssd_y"), 1)
                dve.wait_ge(sem("ssd_y"), 2 * c + 1)
                nc.vector.tensor_tensor(ck(zbuf, c), ck(zbuf, c), ck(xbc, c), ALU.mult).then_inc(sem("ssd_y"), 1)

            def turn(n0, g, first=False, last=False):
                for v in range(4):
                    if v < 2 or not last:
                        least(n0 + v + 2, (v + 2) % 4, first and v < 2)
                    if not last:
                        dve_pick(dve, n0 + v + 4, v, False)
                    m(n0 + v, v, g)
                    if (n0 + v) % 2 and n0 + v >= 3:
                        gated((n0 + v - 3) // 2)
            turn(0, 0, first=True)
            turn(4, 0)
            turn(8, 1)
            turn(12, 1, last=True)
            gated(KD - 1)

        def dve_group_rstd(dve, g):
            dve.wait_ge(sem("ssd_sd"), g + 1)
            nc.vector.reciprocal(group_rstd[g][:], group_rstd[g][:]).then_inc(sem("ssd_rs"), 1)

        def act_ssd(act):
            def exps(n, v, first):
                act.wait_ge(sem("a_mm"), 2 * n + 2)
                if n == 2:
                    act.wait_ge(sem("xdt_pool"), NBLK)
                    act.wait_ge(sem("xdt_dve"), NBLK)
                if not first:
                    act.wait_ge(sem("y_mm"), n - 3)
                for r, s, a, b, l0 in TILES[0]:
                    nc.scalar.activation(ebuf[v][:, r * 384 + a:r * 384 + b],
                                         abank(v, 0)[:, r * SEQ + l0:r * SEQ + l0 + b - a], ACT.Relu, scale=-1.0,
                                         bias=acol[:, bass.ds((2 * r + s) * 64 + n, 1)]).then_inc(
                                             sem("ssd_rel"), 1)
                act.wait_ge(sem("ssd_rel"), 4 * n + 4)
                nc.scalar.activation(ebuf[v][:, 0:768], ebuf[v][:, 0:768], ACT.Exp, scale=-1.0).then_inc(
                    sem("ssd_exp"), 1)
                act.wait_ge(sem("ssd_min"), 4 * n + 4)
                nc.scalar.activation(ebuf[v][:, 768:1536], ebuf[v][:, 768:1536], ACT.Exp).then_inc(
                    sem("ssd_exp"), 1)
            act.wait_ge(sem("dt_dve"), 12)
            def square(c):
                act.wait_ge(sem("ssd_y"), 2 * c + 2)
                if c >= 3:
                    act.wait_ge(sem("ssd_acc"), group_adds(c - 2))
                nc.scalar.activation(group_rstd[c // 4][:] if c % 4 == 0 else sqbuf[c % 2][:], ck(zbuf, c),
                                     ACT.Square).then_inc(sem("ssd_sq"), 1)
            for n in range(HEADS):
                exps(n, n % 4, n < 4)
                if n % 2 and n >= 5:
                    square((n - 5) // 2)
            square(KD - 2)
            square(KD - 1)

        def act_group_deviation(act):
            for g in range(2):
                act.wait_ge(sem("ssd_ss"), g + 1)
                nc.scalar.activation(group_rstd[g][:], bank[6 + g][:], ACT.Sqrt, bias=prm("eps"),
                                     scale=2.0 / D).then_inc(sem("ssd_sd"), 1)

        def beside(n):
            return () if n == 0 else (KD - 2, KD - 1) if n == MHEADS - 1 else (n - 1,)

        def dve_ssd_norm(dve, c):
            dve.wait_ge(sem("ssd_rs"), c // 4 + 1)
            nc.vector.tensor_tensor(ck(zbuf, c), ck(zbuf, c), group_rstd[c // 4][:], ALU.mult).then_inc(
                sem("ssd_n"), 1)

        def act_ssd_high(act, c):
            act.wait_ge(sem("ssd_n"), c + 1)
            nc.scalar.activation(ck(xw_hi, c), ck(zbuf, c), ACT.Copy, scale=prm("ssdn", c)).then_inc(
                sem("ssd_hi"), 1)

        def dve_ssd_low(dve, c):
            dve.wait_ge(sem("ssd_hi"), c + 1)
            nc.vector.scalar_tensor_tensor(out=ck(xw_lo, c), in0=ck(zbuf, c), scalar=prm("ssdn", c),
                                           in1=ck(xw_hi, c).bitcast(F32), op0=ALU.mult,
                                           op1=ALU.subtract).then_inc(sem("ssd_lo"), 1)

        def pe_spread(pe, n, first=False):
            v = n % 2
            pe.wait_ge(sem("onehot_set"), 2 * n + 2)
            if first:
                pe.wait_ge(sem("dt_dve"), 12)
            else:
                pe.wait_ge(sem("ssd_rel"), 4 * n - 4)
                pe.wait_ge(sem("ssd_min"), 4 * n - 4)
            for d in range(2):
                nc.tensor.matmul(abank(v, d)[:], onehot[v][:, d * P:(d + 1) * P], at_hi[:],
                                 start=True, stop=False)
                nc.tensor.matmul(abank(v, d)[:], onehot[v][:, d * P:(d + 1) * P], at_lo[:],
                                 start=False, stop=True).then_inc(sem("a_mm"), 1)

        def pe_ssd(pe):
            def y(n):
                c, u = n // 2, n % 2
                pe.wait_ge(sem("ssd_m"), n + 1)
                pe.wait_ge(sem("ssd_mb"), n + 1)
                if c >= 2 and u == 0:
                    pe.wait_ge(sem("ssd_y"), 2 * c - 3)
                for r in range(NREQ):
                    parts = ((0, 0, 0, 0, 256), (1, 1, 0, 128, 384), (0, 1, P, 256, 384), (1, 0, 0, 0, 128))
                    for i, (d, s, l0, a, b) in enumerate(parts):
                        at, x_at = (d * 2 + r) * 384, (d * NBLK + 2 * r + s) * D + n * HDIM
                        last = nc.tensor.matmul(bank[4 + c % 2][u * HDIM:(u + 1) * HDIM,
                                                                r * SEQ + l0:r * SEQ + l0 + b - a],
                                                xdt[:, x_at:x_at + HDIM], ebuf[n % 4][:, at + a:at + b],
                                                start=i == 0, stop=i == 3)
                last.then_inc(sem("y_mm"), 1)

            pe.wait_ge(sem("hin_u"), 24)
            pe_spread(pe, 1, True)
            pe_spread(pe, 2)
            pe.wait_ge(sem("xdt_dve"), NBLK)
            pe.wait_ge(sem("xdt_pool"), NBLK)
            for n in range(HEADS):
                if n + 3 < HEADS:
                    pe_spread(pe, n + 3)
                if n == 8:
                    pe.wait_ge(sem("xdt_pool"), 3 * NBLK)
                y(n)
                if n == 13:
                    pe.wait_ge(sem("ssd_acc"), 3)
                    nc.tensor.matmul(bank[6][:], ones[:, 0:P], group_rstd[0][:], start=True, stop=True).then_inc(
                        sem("ssd_ss"), 1)

        def act_mla_squares(act):
            act.wait_ge(sem("hin_u"), 4)
            for i in range(3):
                nc.scalar.activation(ebuf[1][:, i * T:(i + 1) * T], ck(mq, 1 + i), ACT.Square).then_inc(
                    sem("mla_sq"), 1)

        def act_mla_deviation(act):
            act.wait_ge(sem("dt_dve"), 2)
            for i, n in enumerate((P, QLORA)):
                act.wait_ge(sem("mla_ss"), i + 1)
                nc.scalar.activation(cbuf[2 + i][:], bank[6 + i][:], ACT.Sqrt, bias=prm("eps"),
                                     scale=1.0 / n).then_inc(sem("mla_sd"), 1)

        def pe_mla_squares(pe):
            pe.wait_ge(sem("mla_sq"), 3)
            sq = [ebuf[1][:, i * T:(i + 1) * T] for i in range(3)]
            nc.tensor.matmul(bank[6][:], ones[:, 0:P], sq[0], start=True, stop=True).then_inc(sem("mla_ss"), 1)
            nc.tensor.matmul(bank[7][:], ones[:, 0:P], sq[1], start=True, stop=False)
            nc.tensor.matmul(bank[7][:], ones[:, 0:P], sq[2], start=False, stop=True).then_inc(sem("mla_ss"), 1)

        def dve_mla_rstd(dve, i):
            dve.wait_ge(sem("mla_sd"), i + 1)
            nc.vector.reciprocal(cbuf[2 + i][:], cbuf[2 + i][:]).then_inc(sem("mla_rs"), 1)

        def dve_mla_scale(dve):
            for i in range(3):
                dve.wait_ge(sem("mla_rs"), min(i, 1) + 1)
                nc.vector.tensor_tensor(ck(mq, 1 + i), ck(mq, 1 + i), cbuf[2 + min(i, 1)][:],
                                        ALU.mult).then_inc(sem("mla_n"), 1)

        def act_mla_prep(act):
            act.wait_ge(sem("mla_n"), 3)
            act.wait_ge(sem("ssd_y"), 2 * KD)
            for i, (dst, w) in enumerate(((ckv_hi[:], prm("kvn")), (ck(qn_hi, 0), prm("qn", 0)),
                                          (ck(qn_hi, 1), prm("qn", 1)))):
                nc.scalar.activation(dst, ck(mq, 1 + i), ACT.Copy, scale=w).then_inc(sem("mla_hi"), 1)

        def dve_mla_low(dve):
            for i, (dst, src, w) in enumerate(((ckv_lo[:], ckv_hi[:], prm("kvn")),
                                               (ck(qn_lo, 0), ck(qn_hi, 0), prm("qn", 0)),
                                               (ck(qn_lo, 1), ck(qn_hi, 1), prm("qn", 1)))):
                dve.wait_ge(sem("mla_hi"), i + 1)
                nc.vector.scalar_tensor_tensor(out=dst, in0=ck(mq, 1 + i), scalar=w, in1=src.bitcast(F32),
                                               op0=ALU.mult, op1=ALU.subtract).then_inc(sem("mla_lo"), 1)

        def pe_mla_prep(pe):
            pe.wait_ge(sem("ssd_y"), 16)
            nc.tensor.matmul(bank[4][:], con("seldup"), ck(mq, 0), start=True, stop=True)
            nc.tensor.matmul(bank[5][:], con("selrot"), ck(mq, 0), start=True, stop=True).then_inc(sem("mla_kr"), 1)

        def dve_mla_prep(dve):
            dve_mla_low(dve)
            dve.wait_ge(sem("mla_kr"), 1)
            nc.vector.tensor_tensor(ubuf[0][:], bank[4][:], cosin[:, 0:T], ALU.mult).then_inc(sem("mla_kd"), 1)
            nc.vector.tensor_tensor(ubuf[1][:], bank[5][:], cosin[:, T:2 * T], ALU.mult).then_inc(sem("mla_kd"), 1)
            dve.wait_ge(sem("mla_kd"), 2)
            for u in range(2):
                on = slice(64 * u, 64 * u + 64)
                nc.vector.tensor_tensor(kre[u][on, :], ubuf[0][on, :], ubuf[1][on, :],
                                        ALU.add).then_inc(sem("mla_kd"), 1)

        def pe_mla(pe):
            base = BASE["mla"]

            def gen(i):
                s = (base + i) % 2
                outs = [("q", 0, 0, 2), ("q", 1, 2, 2), ("r", 0, 4, 2), ("k", 0, 6, 1), ("k", 1, 7, 1)]
                pe.wait_ge(w_lo, base + i + 1)
                if i == 0:
                    pe.wait_ge(sem("mla_lo"), 3)
                for e, (kind, u, w0, kts) in enumerate(outs):
                    if e >= 2:
                        pe.wait_ge(sem("mla_gen"), 7 * i + e - 1)
                    elif i:
                        pe.wait_ge(sem("mla_gen"), 7 * i - 1 + e)
                    a_hi, a_lo = (ckv_hi, ckv_lo) if kind == "k" else (qn_hi, qn_lo)
                    product(pe, base, i, i, bank[e % 2][:], a_hi, a_lo, kts=kts, w0=w0, last_of_block=False,
                            wait=False).then_inc(sem("mla_g"), 1)
                pe.wait_ge(sem("mla_gen"), 7 * i + 3)
                if i:
                    pe.wait_ge(sem("mla_pT_act"), 2 * i - 1)
                else:
                    pe.wait_ge(sem("mla_kd"), 2)
                nc.tensor.matmul(bank[4][:], con("rot"), ubuf[0][:], start=True, stop=True).then_inc(sem("mla_g"), 1)
                for e in (5, 6):
                    pe.wait_ge(sem("mla_gen"), 7 * i + e - 1)
                    for h in range(2):
                        blk = 2 * (e - 5) + h
                        o = bank[e % 2][:, h * 256:(h + 1) * 256]
                        tok = slice(blk * P, (blk + 1) * P)
                        nc.tensor.matmul(o, ckv_hi[:, tok], whi[s][:, 8 * P:10 * P], start=True, stop=False)
                        nc.tensor.matmul(o, ckv_lo[:, tok], whi[s][:, 8 * P:10 * P], start=False, stop=False)
                        last = nc.tensor.matmul(o, ckv_hi[:, tok], wlo[s][:, 8 * P:10 * P], start=False, stop=True)
                    last.then_inc(mm if e == 6 else sem("mla_g"), 1)

            def scores(n):
                i, u = n // 2, n % 2
                pe.wait_ge(sem("mla_gen"), 7 * i + 5)
                pe.wait_ge(sem("mla_qr"), 3 * i + 3)
                if n:
                    pe.wait_ge(sem("mla_exp"), 4 * n)
                for r in range(NREQ):
                    keys = slice(r * SEQ, (r + 1) * SEQ)
                    for qb in range(2):
                        o = bank[2 + r][:, qb * SEQ:(qb + 1) * SEQ]
                        q = slice(r * SEQ + qb * P, r * SEQ + (qb + 1) * P)
                        nc.tensor.matmul(o, qh[u][:, q], kh[u][:, keys], start=True, stop=False)
                        last = nc.tensor.matmul(o, qr[:, q], kre[u][:, keys], start=False, stop=True)
                    last.then_inc(sem("mla_s"), 1)

            def values(n):
                i, u = n // 2, n % 2
                pe.wait_ge(sem("mla_p"), 2 * n + 2)
                pe.wait_ge(sem("mla_gen"), 7 * i + 7)
                for r in range(NREQ):
                    if n:
                        pe.wait_ge(sem("mla_pT_dve" if r else "mla_pT_act"), n)
                    for kb in range(2):
                        for qb in range(2):
                            at = (2 * r + qb) * SEQ + kb * P
                            last = nc.tensor.transpose(bank[4 + r][:, kb * SEQ + qb * P:kb * SEQ + (qb + 1) * P],
                                                       prob[u][:, at:at + P], ident[:])
                    last.then_inc(sem("mla_T"), 1)
                if n >= 2:
                    pe.wait_ge(sem("mla_olo"), n - 1)
                for r in range(NREQ):
                    pe.wait_ge(sem("mla_pT_dve" if r else "mla_pT_act"), n + 1)
                    for kb in range(2):
                        at = (2 * r + kb) * 2 * P + u * P
                        last = nc.tensor.matmul(bank[6 + u][:, r * SEQ:(r + 1) * SEQ], vp[i % 2][:, at:at + P],
                                                probT[:, r * T + kb * SEQ:r * T + (kb + 1) * SEQ],
                                                start=kb == 0, stop=kb == 1)
                last.then_inc(sem("mla_o"), 1)
            for i in range(MHEADS // 2):
                gen(i)
                if i == 0:
                    pe.wait_ge(sem("ssd_acc"), 6)
                    nc.tensor.matmul(bank[7][:], ones[:, 0:P], group_rstd[1][:], start=True, stop=True).then_inc(
                        sem("ssd_ss"), 1)
                    pe.wait_ge(sem("mla_kd"), 4)
                    pe.wait_ge(sem("mla_kz"), 2)
                scores(2 * i)
                if i:
                    values(2 * i - 1)
                scores(2 * i + 1)
                values(2 * i)
            return lambda: values(MHEADS - 1)

        def act_mla(act):
            base = BASE["mla"]

            def gen(i):
                for e, dst in ((0, qh[0]), (1, qh[1]), (3, kh[0]), (4, kh[1]), (5, None), (6, None)):
                    if e < 6:
                        act.wait_ge(sem("mla_g"), 7 * i + e + (2 if e == 5 else 1))
                    else:
                        act.wait_ge(mm, base + i + 1)
                    act.wait_ge(sem("mla_gen"), 7 * i + e)
                    if dst is not None:
                        if i and e == 0:
                            act.wait_ge(sem("mla_s"), 4 * i)
                        out_ap = dst[:]
                    else:
                        if i >= 2:
                            act.wait_ge(sem("mla_o"), 2 * i - 2)
                        out_ap = vp[i % 2][:, (e - 5) * T:(e - 4) * T]
                    nc.scalar.activation(out_ap, bank[e % 2][:], ACT.Copy).then_inc(sem("mla_gen"), 1)
                hi(act, base, i + 2, i + 2)

            def soft(n):
                u = n % 2
                act.wait_ge(sem("mla_nm"), n + 1)
                if n >= 2:
                    act.wait_ge(sem("mla_T"), 2 * n - 2)
                for i in range(4):
                    nc.scalar.activation(prob[u][:, i * SEQ:(i + 1) * SEQ],
                                         bank[2 + i // 2][:, (i % 2) * SEQ:(i % 2 + 1) * SEQ], ACT.Exp,
                                         bias=stat[:, 16 * u + 4 + i:16 * u + 5 + i], scale=QSCALE,
                                         accum_out=stat[:, 16 * u + 8 + i:16 * u + 9 + i]).then_inc(sem("mla_exp"), 1)

            def turned(n):
                act.wait_ge(sem("mla_T"), 2 * n + 1)
                if n:
                    act.wait_ge(sem("mla_o"), n)
                nc.scalar.activation(probT[:, 0:T], bank[4][:], ACT.Copy).then_inc(sem("mla_pT_act"), 1)

            def outs(n):
                act.wait_ge(sem("mla_o"), n + 1)
                nc.scalar.activation(ck(co_hi, n), bank[6 + n % 2][:], ACT.Copy).then_inc(sem("mla_ohi"), 1)
            for i in range(MHEADS // 2):
                gen(i)
                for n in (2 * i, 2 * i + 1):
                    if n:
                        turned(n - 1)
                    soft(n)
                    if n == 0:
                        act_group_deviation(act)
                    for c in beside(n):
                        act_ssd_high(act, c)
                    if n:
                        outs(n - 1)
            turned(MHEADS - 1)
            outs(MHEADS - 1)

        def dve_mla(dve):
            def gen(i):
                dve.wait_ge(sem("mla_g"), 7 * i + 3)
                dve.wait_ge(sem("mla_gen"), 7 * i + 2)
                if i == 0:
                    dve.wait_ge(sem("mla_kd"), 4)
                nc.vector.tensor_copy(ubuf[0][:], bank[0][:]).then_inc(sem("mla_gen"), 1)
                dve.wait_ge(sem("mla_gen"), 7 * i + 3)
                if i:
                    dve.wait_ge(sem("mla_s"), 4 * i)
                nc.vector.tensor_tensor(qr[:], ubuf[0][:], cosin[:, 0:T], ALU.mult).then_inc(sem("mla_qr"), 1)
                dve.wait_ge(sem("mla_g"), 7 * i + 6)
                nc.vector.tensor_tensor(ubuf[1][:], bank[4][:], cosin[:, T:2 * T], ALU.mult).then_inc(sem("mla_qr"), 1)
                dve.wait_ge(sem("mla_qr"), 3 * i + 2)
                nc.vector.tensor_tensor(qr[:], qr[:], ubuf[1][:], ALU.add).then_inc(sem("mla_qr"), 1)

            def top(n):
                u = n % 2
                for r in range(NREQ):
                    dve.wait_ge(sem("mla_s"), 2 * n + r + 1)
                    nc.vector.tensor_reduce(stat[:, 16 * u + 2 * r:16 * u + 2 * r + 2], req(bank[2 + r][:]), AX.X,
                                            ALU.max).then_inc(sem("mla_mx"), 1)
                dve.wait_ge(sem("mla_mx"), 2 * n + 2)
                nc.vector.tensor_scalar(stat[:, 16 * u + 4:16 * u + 8], stat[:, 16 * u:16 * u + 4], -QSCALE, None,
                                        ALU.mult).then_inc(sem("mla_nm"), 1)

            def norm(n):
                u = n % 2
                dve.wait_ge(sem("mla_exp"), 4 * n + 4)
                nc.vector.reciprocal(stat[:, 16 * u + 12:16 * u + 16],
                                     stat[:, 16 * u + 8:16 * u + 12]).then_inc(sem("mla_p"), 1)
                dve.wait_ge(sem("mla_p"), 2 * n + 1)
                pr = prob[u][:].rearrange("p (i k) -> p i k", i=4)
                nc.vector.tensor_tensor(pr, pr, stat[:, 16 * u + 12:16 * u + 16].unsqueeze(2).broadcast_to(
                    [P, 4, SEQ]), ALU.mult).then_inc(sem("mla_p"), 1)

            def turned(n):
                dve.wait_ge(sem("mla_T"), 2 * n + 2)
                if n:
                    dve.wait_ge(sem("mla_o"), n)
                nc.vector.tensor_copy(probT[:, T:2 * T], bank[5][:]).then_inc(sem("mla_pT_dve"), 1)

            def outs(n):
                dve.wait_ge(sem("mla_ohi"), n + 1)
                nc.vector.tensor_tensor(ck(co_lo, n), bank[6 + n % 2][:], ck(co_hi, n).bitcast(F32),
                                        ALU.subtract).then_inc(sem("mla_olo"), 1)
            for i in range(MHEADS // 2):
                gen(i)
                for n in (2 * i, 2 * i + 1):
                    top(n)
                    if n:
                        turned(n - 1)
                    for c in beside(n):
                        dve_ssd_norm(dve, c)
                    norm(n)
                    if n:
                        outs(n - 1)
                        for c in beside(n - 1):
                            dve_ssd_low(dve, c)
                    if n % 4 == 0:
                        dve_group_rstd(dve, n // 4)
            for c in beside(MHEADS - 1):
                dve_ssd_low(dve, c)
            turned(MHEADS - 1)
            outs(MHEADS - 1)

        def pool_mla(pool):
            pool.wait_ge(sem("ssd_y"), 2 * KD)
            pool.wait_ge(sem("ssd_acc"), group_adds(KD - 1))
            for u in range(2):
                nc.gpsimd.memset(kre[u][64 - 64 * u:128 - 64 * u, :], 0.0).then_inc(sem("mla_kz"), 1)
                pool.wait_ge(sem("mla_kz"), u + 1)
            for i in range(4):
                lo(pool, BASE["mla"], i + 2, i + 2)


        G0 = 8

        def gbank(ft, u):
            return bank[1 if ft == 0 and u == 0 else 5 + u]

        def pe_gin(pe):
            base = BASE["gin"]
            product(pe, base, 0, 0, bank[0][:], xw_hi, xw_lo, by_chunk=("res_lo", 1))

            def block(t, ft, u):
                j = 1 + 2 * t + u
                if ft + u >= 2:
                    pe.wait_ge(sem("gin_u"), j - 1)
                if ft + u == 0:
                    product_and_res(pe, 1, base, 1, gbank(0, 0)[:])
                else:
                    product(pe, base, j, 1 + 2 * ft + u, gbank(ft, u)[:], xw_hi, xw_lo)

            def body(t, ft):
                block(t, ft, 0)
                pe.wait_ge(sem("gate_w"), t + 1)
                if ft:
                    pe.wait_ge(sem("gate_min"), t)
                else:
                    pe.wait_ge(sem("gin_u"), 1)
                nc.tensor.matmul(bank[4][:], wsel[:], lrk[:], start=True, stop=True).then_inc(sem("gate_mm"), 1)
                block(t, ft, 1)
            body(0, 0)
            turns(pe, 1, G0, body)
            for t in range(G0, 12):
                block(t, t, 0)
                blk = t - G0
                if blk:
                    pe.wait_ge(sem("vtok_act"), blk)
                    pe.wait_ge(sem("vtok_dve"), blk)
                else:
                    pe.wait_ge(sem("gin_u"), 17)
                for half in range(2):
                    for c in range(4):
                        last = nc.tensor.transpose(bank[2 + half][:, c * P:(c + 1) * P],
                                                   ck(gqkv, 8 + half * 4 + c)[:, blk * P:(blk + 1) * P], ident[:])
                    last.then_inc(sem("v_T"), 1)
                block(t, t, 1)

        def act_gin(act):
            base = BASE["gin"]

            def body(t, ft):
                hi(act, base, 2 * t + 3, 2 * ft + 3)
                act.wait_ge(sem("gate_mm"), t + 1)
                if ft:
                    act.wait_ge(sem("gate_act"), 3 * t)
                nc.scalar.activation(cbuf[0][:], bank[4][:], ACT.Abs, bias=prm("bgk", t)).then_inc(sem("gate_act"), 1)
                act.wait_ge(sem("gate_act"), 3 * t + 1)
                nc.scalar.activation(cbuf[0][:], cbuf[0][:], ACT.Exp, scale=-1.0).then_inc(sem("gate_act"), 1)
                act.wait_ge(sem("gate_act"), 3 * t + 2)
                if ft:
                    act.wait_ge(sem("gate_sub"), t)
                nc.scalar.activation(cbuf[1][:], cbuf[0][:], ACT.Ln, bias=ones[:, 0:1]).then_inc(sem("gate_act"), 1)
                hi(act, base, 2 * t + 4, 2 * ft + 4)
            act.wait_ge(sem("out_m"), of("out_m", 1) + KD)
            act.dma_start(wgk[:], w_gk).then_inc(sem("wgk_in"), 16)
            act.dma_start(gmask[:], glac[:, 0:T + CH]).then_inc(sem("gmask_in"), 16)
            act.dma_start(tri[:], glac[:, T + CH:T + CH + 2 * P]).then_inc(sem("tri_in"), 16)
            turns(act, 0, G0, body)
            act.wait_ge(sem("carry_set"), CARRIES)
            nc.scalar.activation(carry[:], carry[:], ACT.Exp, scale=GK_NORM).then_inc(sem("carry_exp"), 1)
            act_gate_exps(act, 0)
            act_gate_exps(act, 1)
            for t in range(G0, 12):
                for u in range(2):
                    j = 1 + 2 * t + u
                    hi(act, base, j + 2, j + 2)
                    act.wait_ge(sem("gin_u"), j + 1)
                    nc.scalar.activation(ck(gg, j - 17), ubuf[u][:], ACT.Silu).then_inc(sem("gin_silu"), 1)
                    if u == 0:
                        act.wait_ge(sem("v_T"), 2 * (t - G0) + 1)
                        nc.scalar.activation(vtok[:, (t - G0) * D:(t - G0) * D + T], bank[2][:], ACT.Copy).then_inc(
                            sem("vtok_act"), 1)

        def way(d, ap):
            return ap[:, ::-1] if d else ap

        CARRIES = 18

        def dve_carries(dve):
            chunks = gl[:].rearrange("p (d i c x) -> p d i c x", d=2, i=GLA_HEADS * NREQ, c=NCH)
            pairs = carry[:].rearrange("p (d i j) -> p d i j", d=2, j=8)
            for d in range(2):
                own, other = (6, 7) if d == 0 else (7, 6)
                c, x = (2, CH - 1) if d == 0 else (1, 0)
                nc.vector.memset(pairs[:, d, :, own:own + 1], 0.0).then_inc(sem("carry_set"), 1)
                nc.vector.tensor_copy(pairs[:, d, :, other:other + 1], chunks[:, d, :, c, x:x + 1]).then_inc(
                    sem("carry_set"), 2)
            for i, (src, j) in enumerate(((0, 0), (1, 2), (2, 5))):
                for d in range(2):
                    c, x = (src, CH - 1) if d == 0 else (3 - src, 0)
                    at = j if d == 0 else (0, 1, 3)[i]
                    nc.vector.tensor_copy(pairs[:, d, :, at:at + 1], chunks[:, d, :, c, x:x + 1]).then_inc(
                        sem("carry_set"), 1)
            dve.wait_ge(sem("carry_set"), 12)

            def add(d, to, a, c, x, n=1):
                ins = nc.vector.tensor_tensor(pairs[:, d, :, to:to + n], pairs[:, d, :, a:a + n],
                                              chunks[:, d, :, c, x:x + 1].broadcast_to([P, GLA_HEADS * NREQ, n]),
                                              ALU.add)
                ins.then_inc(sem("carry_set"), 1 if n == 1 else 2)
            add(0, 1, 0, 1, CH - 1)
            add(1, 2, 0, 2, 0)
            dve.wait_ge(sem("carry_set"), 14)
            add(0, 3, 1, 2, CH - 1, 2)
            add(1, 4, 1, 1, 0, 2)

        def dve_gin(dve):
            base = BASE["gin"]

            def pick(t):
                nc.vector.tensor_copy(wsel[:], wgk[:, bass.ds(t * P, P)]).then_inc(sem("gate_w"), 1)

            def part(d):
                def body(t, ft):
                    for u in range(2):
                        dve.wait_ge(mm, base + 2 * t + u + 2)
                        scaled(dve, ck(gqkv, 2 * t + u), gbank(ft, u)).then_inc(sem("gin_u"), 1)
                        if u == 0:
                            if ft:
                                dve.wait_ge(sem("gate_scan"), t)
                            dve.wait_ge(sem("gate_act"), 3 * t + 1)
                            nc.vector.tensor_scalar(ubuf[0][:], bank[4][:], prm("bgk", t), 0.0, ALU.add,
                                                    ALU.min).then_inc(sem("gate_min"), 1)
                            if ft < G0 - 1:
                                pick(t + 1)
                    dve.wait_ge(sem("gate_act"), 3 * t + 3)
                    dve.wait_ge(sem("gate_min"), t + 1)
                    nc.vector.tensor_tensor(ubuf[0][:], ubuf[0][:], cbuf[1][:], ALU.subtract).then_inc(
                        sem("gate_sub"), 1)
                    dve.wait_ge(sem("gate_sub"), t + 1)
                    nc.vector.tensor_tensor_scan(out=way(d, gl[:, bass.ds(t * T, T)]),
                                                 data0=way(d, gmask[:, d:d + T]), data1=way(d, ubuf[0][:]),
                                                 initial=0.0, op0=ALU.mult, op1=ALU.add).then_inc(
                                                     sem("gate_scan"), 1)
                return body
            dve.wait_ge(sem("wgk_in"), 16)
            pick(0)
            dve.wait_ge(mm, base + 1)
            dve.wait_ge(sem("res_rstd"), of("res_rstd", 1) + 1)
            scaled(dve, lrk[:], bank[0]).then_inc(sem("gin_u"), 1)
            dve.wait_ge(sem("gmask_in"), 16)
            dve.wait_ge(sem("tri_in"), 16)
            part(0)(0, 0)
            turns(dve, 1, 4, part(0))
            turns(dve, 4, G0 - 1, part(1))
            part(1)(G0 - 1, G0 - 1)
            dve.wait_ge(sem("gate_scan"), G0)
            dve_carries(dve)
            for t in range(G0, 12):
                for u in range(2):
                    dve.wait_ge(mm, base + 2 * t + u + 2)
                    if t > G0:
                        dve.wait_ge(sem("gin_silu"), 2 * (t - G0) + u - 1)
                    scaled(dve, ubuf[u][:], gbank(t, u)).then_inc(sem("gin_u"), 1)
                    if u == 0:
                        dve.wait_ge(sem("v_T"), 2 * (t - G0) + 2)
                        nc.vector.tensor_copy(vtok[:, (t - G0) * D + T:(t - G0 + 1) * D], bank[3][:]).then_inc(
                            sem("vtok_dve"), 1)
                if t == G0 + 1:
                    dve.wait_ge(sem("gate_w"), G0)
                    dve_zero_keys(dve, 0)
                    dve_keys(dve, 0)

        def pool_gin(pool):
            base = BASE["gin"]
            lo(pool, base, 2, 2)

            def body(t, ft):
                for u in range(2):
                    lo(pool, base, 2 * t + u + 3, 2 * ft + u + 3)
            turns(pool, 0, 10, body)
            for j in range(21, 25):
                lo(pool, base, j + 2, j + 2)

        def kks(d):
            return kk[d][:].rearrange("p (r x) -> p r x", r=NREQ)

        def cross(d, c):
            return {(0, 1): (0, 1, 0), (0, 2): (0, 2, 1), (0, 3): (2, 1, 5),
                    (1, 2): (3, 1, 0), (1, 1): (2, 2, 1), (1, 0): (1, 1, 3)}.get((d, c))

        def act_gate_exps(act, n):
            hd, d = n // 2, n % 2
            if hd:
                act.wait_ge(sem("gla_s"), n - 1)
                act.wait_ge(sem("gla_kk"), 5 * n - 5)
            f = slice((d * GLA_HEADS + hd) * T, (d * GLA_HEADS + hd + 1) * T)
            nc.scalar.activation(qt[d][:], gl[:, f], ACT.Exp, scale=GK_NORM).then_inc(sem("gla_e"), 1)
            nc.scalar.activation(ek[d][:], gl[:, f], ACT.Exp, scale=-GK_NORM).then_inc(sem("gla_e"), 1)

        def dve_zero_keys(dve, d):
            for c in ((0, 2) if d == 0 else (1, 3)):
                s0 = CH * (c + 1) if d == 0 else CH * (c - 1)
                nc.vector.memset(kks(d)[:, :, c * SEQ + s0:c * SEQ + s0 + CH], 0.0).then_inc(sem("kk_zero"), 1)

        def dve_keys(dve, n):
            hd, d = n // 2, n % 2
            if n == 0:
                dve.wait_ge(sem("carry_exp"), 1)
            dve.wait_ge(sem("gla_e"), 2 * n + 2)
            if hd:
                dve.wait_ge(sem("gla_s"), n - 1)
            k = ck(gqkv, 4 + hd).rearrange("p (r c x) -> p r c x", r=NREQ, x=CH)
            e = ek[d][:].rearrange("p (r c x) -> p r c x", r=NREQ, x=CH)
            step = SEQ + CH
            if d == 0:
                own = kks(d)[:, :, 0:3 * step].rearrange("p r (c y) -> p r c y", y=step)[:, :, :, 0:CH]
                first, other = 0, 3
            else:
                own = kks(d)[:, :, CH:].rearrange("p r (c y) -> p r c y", y=step)[:, :, :, SEQ:]
                first, other = 1, 0
            for to, c in ((own, slice(first, first + 3)),
                          (kks(d)[:, :, other * step:other * step + CH].unsqueeze(2), slice(other, other + 1))):
                nc.vector.tensor_tensor(to, k[:, :, c], e[:, :, c], ALU.mult).then_inc(sem("gla_kk"), 1)
            nc.vector.scalar_tensor_tensor(out=qt[d][:], in0=ck(gqkv, hd), scalar=QG, in1=qt[d][:],
                                           op0=ALU.mult, op1=ALU.mult).then_inc(sem("gla_q"), 1)
            dve.wait_ge(sem("gla_kk"), 5 * n + 2)
            carries = carry[:].rearrange("p (m r j) -> p m r j", r=NREQ, j=8)[:, d * GLA_HEADS + hd]
            for c in range(NCH):
                if cross(d, c):
                    s0, m, j = cross(d, c)
                    to = kks(d)[:, :, c * SEQ + s0 * CH:c * SEQ + (s0 + m) * CH].rearrange(
                        "p r (c x) -> p r c x", x=CH)
                    by = carries[:, :, j:j + m].unsqueeze(3).broadcast_to([P, NREQ, m, CH])
                    nc.vector.tensor_tensor(to, own[:, :, s0 - first:s0 - first + m], by,
                                            ALU.mult).then_inc(sem("gla_kk"), 1)
            dve.wait_ge(sem("gla_q"), 2 * n + 1)
            c0 = 2 if d == 0 else 0
            nc.vector.tensor_tensor(qx[d][:].rearrange("p (r c x) -> p r c x", r=NREQ, x=CH),
                                    qt[d][:].rearrange("p (r c x) -> p r c x", r=NREQ, x=CH)[:, :, c0:c0 + 2],
                                    carries[:, :, 6:8].unsqueeze(3).broadcast_to([P, NREQ, 2, CH]),
                                    ALU.mult).then_inc(sem("gla_q"), 1)

        def rstd_bank(hd):
            return bank[5 if hd == 3 else 4]

        def sbank(d, r):
            return bank[2 * (1 - d) + r]

        def pe_gla(pe):
            def scores(n):
                hd, d = n // 2, n % 2
                pe.wait_ge(sem("gla_kk"), 5 * n + 5)
                pe.wait_ge(sem("gla_q"), 2 * n + 2)
                if hd:
                    pe.wait_ge(sem("gla_att_b" if d else "gla_att_f"), 2 * hd)
                elif d == 0:
                    pe.wait_ge(sem("vtok_act"), 4)
                    pe.wait_ge(sem("vtok_dve"), 4)
                else:
                    pe.wait_ge(sem("gin_u"), 25)
                for r in range(NREQ):
                    out = sbank(d, r)
                    for c in range(NCH):
                        s = c // 2
                        nc.tensor.matmul(out[:, s * SEQ + c * CH:s * SEQ + (c + 1) * CH],
                                         kks(d)[:, r, c * SEQ + s * P:c * SEQ + (s + 1) * P],
                                         qt[d][:, r * SEQ + c * CH:r * SEQ + (c + 1) * CH], start=True, stop=True)
                    c, s = (2, 0) if d == 0 else (1, 1)
                    last = nc.tensor.matmul(out[:, s * SEQ + (1 - s) * P:s * SEQ + (2 - s) * P],
                                            kks(d)[:, r, c * SEQ + s * P:c * SEQ + (s + 1) * P],
                                            qx[d][:, r * P:(r + 1) * P], start=True, stop=True)
                last.then_inc(sem("gla_s"), 1)

            def values(hd):
                pe.wait_ge(sem("gla_att_f"), 2 * hd + 2)
                pe.wait_ge(sem("gla_att_b"), 2 * hd + 2)
                for w in range(2):
                    if hd:
                        pe.wait_ge(sem("gla_osq"), 2 * hd - 1 + w)
                    for r in range(NREQ):
                        for s in range(2):
                            at = (2 * r + s) * D + hd * 2 * P + w * P
                            last = nc.tensor.matmul(bank[5 + w][:, r * SEQ:(r + 1) * SEQ], vtok[:, at:at + P],
                                                    att[hd % 2][:, (2 * r + s) * SEQ:(2 * r + s + 1) * SEQ],
                                                    start=s == 0, stop=s == 1)
                    last.then_inc(sem("gla_o"), 1)

            def sums(hd):
                pe.wait_ge(sem("gla_sq"), hd + 1)
                if hd:
                    pe.wait_ge(sem("gla_sd"), hd)
                for b in range(NBLK):
                    last = nc.tensor.matmul(bank[7][:, hd * NBLK + b:hd * NBLK + b + 1],
                                            cbuf[2 * (hd % 2)][:, b * P:(b + 1) * P], ones[:, 0:1],
                                            start=True, stop=True)
                last.then_inc(sem("gla_ss"), 1)

            def spread(hd):
                pe.wait_ge(sem("gla_diag"), hd + 1)
                if hd in (1, 2):
                    pe.wait_ge(sem("gla_fin"), 4 * hd)
                nc.tensor.matmul(rstd_bank(hd)[:], ones[:, 0:P], diag[:], start=True, stop=True).then_inc(
                    sem("gla_spread"), 1)
            scores(0)
            scores(1)
            for hd in range(GLA_HEADS):
                if hd < 3:
                    scores(2 * hd + 2)
                values(hd)
                if hd:
                    sums(hd - 1)
                if hd < 3:
                    scores(2 * hd + 3)
                if hd:
                    spread(hd - 1)
            sums(GLA_HEADS - 1)
            spread(GLA_HEADS - 1)

        def act_gla(act):
            def cross_scores(hd, d):
                act.wait_ge(sem("gla_dg" if d else "gla_df"), 2 * hd + 2)
                if hd >= 2:
                    act.wait_ge(sem("gla_o"), 2 * hd - 2)
                for r in range(NREQ):
                    at = (2 * r + d) * SEQ + (1 - d) * P
                    nc.scalar.activation(att[hd % 2][:, at:at + P],
                                         sbank(d, r)[:, d * SEQ + (1 - d) * P:d * SEQ + (2 - d) * P],
                                         ACT.Copy).then_inc(sem("gla_att_b" if d else "gla_att_f"), 1)

            def outs(hd):
                for w in range(2):
                    act.wait_ge(sem("gla_o"), 2 * hd + w + 1)
                    nc.scalar.activation(ck(gqkv, 8 + 2 * hd + w), bank[5 + w][:], ACT.Copy).then_inc(
                        sem("gla_om"), 1)
                    if hd >= 2:
                        act.wait_ge(sem("gla_ss"), hd - 1)
                    nc.scalar.activation(cbuf[2 * (hd % 2) + w][:], bank[5 + w][:], ACT.Square).then_inc(
                        sem("gla_osq"), 1)
            def deviation(hd):
                act.wait_ge(sem("gla_ss"), hd + 1)
                at = slice(hd * NBLK, (hd + 1) * NBLK)
                nc.scalar.activation(gsum[:, at], bank[7][:, at], ACT.Sqrt, bias=prm("eps"),
                                     scale=1.0 / (2 * P)).then_inc(sem("gla_sd"), 1)

            def high(hd):
                for c in (2 * hd, 2 * hd + 1):
                    act.wait_ge(sem("gla_fin"), 2 * c + 2)
                    nc.scalar.activation(ck(xw_hi, c), ck(gg, c), ACT.Copy).then_inc(sem("gla_hi"), 1)
            act.wait_ge(mm, BASE["gin"] + 25)
            act_gate_exps(act, 2)
            cross_scores(0, 0)
            for hd in range(GLA_HEADS):
                cross_scores(hd, 1)
                if hd < 3:
                    act_gate_exps(act, 2 * hd + 3)
                    cross_scores(hd + 1, 0)
                    if hd < 2:
                        act_gate_exps(act, 2 * hd + 4)
                else:
                    act.wait_ge(sem("gla_s"), 8)
                    high(0)
                outs(hd)
                if hd:
                    deviation(hd - 1)
            high(1)
            deviation(3)
            high(2)
            high(3)

        def dve_gla(dve):
            dve.wait_ge(mm, BASE["gin"] + 25)
            dve_zero_keys(dve, 1)

            def gated(hd):
                dve.wait_ge(sem("gla_spread"), hd + 1)
                for w in range(2):
                    c = 2 * hd + w
                    if hd:
                        dve.wait_ge(sem("gla_fin"), 2 * c - 2)
                    nc.vector.scalar_tensor_tensor(out=ubuf[w][:], in0=ck(gqkv, 8 + c), scalar=prm("glan", w),
                                                   in1=rstd_bank(hd)[:], op0=ALU.mult, op1=ALU.mult).then_inc(
                                                       sem("gla_fin"), 1)
                    dve.wait_ge(sem("gla_fin"), 2 * c + 1)
                    nc.vector.tensor_tensor(ck(gg, c), ck(gg, c), ubuf[w][:], ALU.mult).then_inc(sem("gla_fin"), 1)

            def blocks(ap):
                return ap.rearrange("p (b x) -> p b x", x=P)[:, 0::3]

            def own_scores(hd, d):
                if hd >= 2 and d == 0:
                    dve.wait_ge(sem("gla_o"), 2 * hd - 2)
                dve.wait_ge(sem("gla_s"), 2 * hd + d + 1)
                mask = tri[:, d * P:(d + 1) * P].unsqueeze(1).broadcast_to([P, 2, P])
                scores = [blocks(att[hd % 2][:, r * T:(r + 1) * T]) for r in range(NREQ)]
                other = [dg[:, r * SEQ:(r + 1) * SEQ].rearrange("p (b x) -> p b x", x=P) for r in range(NREQ)]
                for r in range(NREQ):
                    nc.vector.tensor_tensor((other if d else scores)[r], blocks(sbank(d, r)[:]), mask,
                                            ALU.mult).then_inc(sem("gla_db" if d else "gla_df"), 1)
                if d:
                    dve.wait_ge(sem("gla_db"), 2 * hd + 2)
                    dve.wait_ge(sem("gla_df"), 2 * hd + 2)
                    for r in range(NREQ):
                        nc.vector.tensor_tensor(scores[r], scores[r], other[r], ALU.add).then_inc(sem("gla_dg"), 1)

            def diagonal(hd):
                at = slice(hd * NBLK, (hd + 1) * NBLK)
                dve.wait_ge(sem("gla_sd"), hd + 1)
                nc.vector.reciprocal(gsum[:, at], gsum[:, at]).then_inc(sem("gla_rs"), 1)
                dve.wait_ge(sem("gla_rs"), hd + 1)
                if hd:
                    dve.wait_ge(sem("gla_spread"), hd)
                nc.vector.tensor_tensor(diag[:].rearrange("p (b x) -> p b x", x=P),
                                        gsum[:, hd * NBLK:(hd + 1) * NBLK].unsqueeze(2).broadcast_to([P, NBLK, P]),
                                        ident[:].unsqueeze(1).broadcast_to([P, NBLK, P]), ALU.mult).then_inc(
                                            sem("gla_diag"), 1)
            dve_keys(dve, 1)
            own_scores(0, 0)
            dve_keys(dve, 2)
            for hd in range(GLA_HEADS):
                own_scores(hd, 1)
                if hd < 3:
                    dve_keys(dve, 2 * hd + 3)
                if hd >= 2:
                    gated(hd - 2)
                if hd < 3:
                    own_scores(hd + 1, 0)
                    if hd < 2:
                        dve_keys(dve, 2 * hd + 4)
                if hd:
                    diagonal(hd - 1)
            diagonal(3)
            gated(2)
            gated(3)

        def pool_gla(pool):
            def squares(hd):
                pool.wait_ge(sem("gla_osq"), 2 * hd + 2)
                s0, s1 = cbuf[2 * (hd % 2)], cbuf[2 * (hd % 2) + 1]
                nc.gpsimd.tensor_tensor(s0[:], s0[:], s1[:], ALU.add).then_inc(sem("gla_sq"), 1)

            def low(hd):
                for c in (2 * hd, 2 * hd + 1):
                    pool.wait_ge(sem("gla_hi"), c + 1)
                    if hd >= 2:
                        pool.wait_ge(sem("gla_o"), 2 * hd + 2)
                    nc.gpsimd.tensor_tensor(ck(xw_lo, c), ck(gg, c), ck(xw_hi, c).bitcast(F32),
                                            ALU.subtract).then_inc(sem("gla_lo"), 1)
            for hd in range(3):
                squares(hd)
            low(0)
            squares(3)
            for hd in range(1, GLA_HEADS):
                low(hd)

        block = ctx.enter_context(nc.Block())

        @block.sync
        def _(sp):
            sp.dma_start(par[:], params).then_inc(sem("par_in"), 16)
            for c in range(KD):
                if c in (0, 4):
                    sp.dma_start(raw[c // 4][:, 0:KD * P], w_stream["hin"][c // 4]).then_inc(raw_in[c // 4], 16)
                sp.dma_start(ck(xres, c), x_in[:, c * T:(c + 1) * T]).then_inc(sem(f"x_in{c}"), 16)
            sp.dma_start(ident[:], consts[:, 0:P]).then_inc(sem("ident_in"), 16)
            g = 0
            for name, count, kt in STREAM:
                n = kt * P
                base = BASE[name]
                for u in range(2 if g else 0):
                    sp.wait_ge(w_lo, base + u - 1)
                    sp.dma_start(raw[(base + u) % 2][:, 0:n], w_stream[name][u]).then_inc(raw_in[(base + u) % 2], 16)
                with sp.Fori(1, count // 2) as t:
                    for u in range(2):
                        sp.wait_ge(w_lo, 2 * t + (base + u - 1))
                        sp.dma_start(raw[(base + u) % 2][:, 0:n],
                                     w_stream[name][bass.ds(2 * t + u, 1)].rearrange("b p n -> (b p) n")).then_inc(
                                         raw_in[(base + u) % 2], 16)
                if count % 2:
                    sp.wait_ge(w_lo, base + count - 2)
                    sp.dma_start(raw[(base + count - 1) % 2][:, 0:n], w_stream[name][count - 1]).then_inc(
                        raw_in[(base + count - 1) % 2], 16)
                g += count
            for c in (0, 1, 5, 2, 3, 6, 4, 7):
                wait_x(sp, 3, c)
                sp.dma_start(out[:, c * T:(c + 1) * T], ck(xres, c)).then_inc(sem("out_stored"), 16)
            sp.wait_ge(sem("out_stored"), KD * 16)

        @block.scalar
        def _(act):
            hi(act, 0, 0, 0)
            act_res(act, -1)
            act.dma_start(cst[:], consts[:, P:NCONST]).then_inc(sem("cst_in"), 16)
            act.dma_start(cosin[:], rope).then_inc(sem("rope_in"), 16)
            act_hin(act)
            act_ssd(act)
            act_mla_prep(act)
            act_mla(act)
            act_out(act, 0, "hout", 2, m_hyb)
            act_res(act, 0)
            act_fin(act, 0)
            act_out(act, 1, "fout0", 2, m_ffn)
            act_res(act, 1)
            act_gin(act)
            act_gla(act)
            act_out(act, 2, "gout", 1, m_gla)
            act_res(act, 2)
            act_fin(act, 1)
            act_out(act, 3, "fout1", 2, m_ffn)

        @block.gpsimd
        def _(pool):
            lo(pool, 0, 0, 0)
            pool_res(pool, -1, None)
            pool_hin(pool)
            pool_xdt(pool)
            pool_ssd(pool)
            pool_mla(pool)
            pool_out(pool, 0, "hout", 2)
            pool_res(pool, 0, m_hyb)
            pool_fin(pool, 0)
            pool_out(pool, 1, "fout0", 2)
            pool_res(pool, 1, m_ffn)
            pool_gin(pool)
            pool_gla(pool)
            pool_out(pool, 2, "gout", 1)
            pool_res(pool, 2, m_gla)
            pool_fin(pool, 1)
            pool_out(pool, 3, "fout1", 2)
            pool_res(pool, 3, m_ffn)

        @block.vector
        def _(dve):
            nc.vector.memset(ones[:], 1.0).then_inc(sem("ones_set"), 1)
            dve.wait_ge(sem("ones_set"), 1)
            dve_res(dve, -1, None)
            dve_hin(dve)
            dve_ssd(dve)
            dve.wait_ge(sem("rope_in"), 16)
            dve_mla_prep(dve)
            dve_mla(dve)
            dve_res(dve, 0, m_hyb)
            dve_fin(dve, 0)
            dve_res(dve, 1, m_ffn)
            dve_gin(dve)
            dve_gla(dve)
            dve_res(dve, 2, m_gla)
            dve_fin(dve, 1)
            dve_res(dve, 3, m_ffn)

        @block.tensor
        def _(pe):
            pe_hin(pe)
            pe_ssd(pe)
            pe_mla_prep(pe)
            last_values = pe_mla(pe)
            pe_out(pe, 0, "hout", 2,
                   lambda b: (co_hi, co_lo, 0, [("mla_olo", MHEADS)]) if b else (xw_hi, xw_lo, 0, None),
                   first_by_chunk=("ssd_lo", 0), between=last_values)
            pe_fin(pe, 0)
            pe_out(pe, 1, "fout0", 2, ffn_operand(0))
            pe_gin(pe)
            pe_gla(pe)
            pe_out(pe, 2, "gout", 1, lambda b: (xw_hi, xw_lo, 0, None), first_by_chunk=("gla_lo", 0))
            pe_fin(pe, 1)
            pe_out(pe, 3, "fout1", 2, ffn_operand(1))


def _tiles(w, cols):
    kt = w.shape[0] // P
    return w[:, cols].reshape(kt, P, -1, P).transpose(2, 1, 0, 3)


def _by_chunk(v):
    return v.reshape(-1, P).T


def _layout(i):
    a = np.arange
    f32 = np.float32
    sample = {}
    x = np.concatenate([i["x_prompt"][0], i["x_sample"][0]], 0)
    sample["x"] = x.T.reshape(KD, P, T).transpose(1, 0, 2).reshape(P, KD * T)
    dt0, q0, kv0 = 2560, 2592, 2848
    kr0 = kv0 + P
    misc = np.concatenate([dt0 + a(16), kr0 + a(16), dt0 + 16 + a(16), kr0 + a(16), kr0 + a(ROPE)])
    cols = np.concatenate([misc, kv0 + a(P), q0 + a(QLORA), 1024 + a(1536), a(1024)])
    sample["hin"] = _tiles(i["hyb_w_in"][0], cols)
    qb, kvb = i["mla_w_qb"][0], i["mla_w_kvb"][0]
    pairs = []
    for h in range(0, MHEADS, 2):
        q_at, kv_at = h * (NOPE + ROPE), h * 2 * P
        nope = [q_at + a(P), q_at + NOPE + ROPE + a(P)]
        rope = np.concatenate([q_at + NOPE + a(ROPE), q_at + 2 * NOPE + ROPE + a(ROPE)])
        parts = [_tiles(qb, c)[0] for c in (*nope, rope)]
        parts += [kvb[:, kv_at + o:kv_at + o + P].reshape(P, 1, P) for o in (0, 2 * P, P, 3 * P)]
        pairs.append(np.concatenate(parts, 1))
    sample["mla"] = np.stack(pairs)
    sample["hout"] = _tiles(i["hyb_w_out"][0], a(D)).reshape(KD, P, 2, KD, P).transpose(0, 2, 1, 3, 4)
    for l in range(2):
        inner = np.stack([a(FF * P).reshape(FF, P), FF * P + a(FF * P).reshape(FF, P)], 1).reshape(-1)
        sample[f"fin{l}"] = _tiles(i["ffn_w_in"][l], inner)
        sample[f"fout{l}"] = _tiles(i["ffn_w_out"][l], a(D)).reshape(KD, P, 2, FF // 2, P).transpose(0, 2, 1, 3, 4)
    lr0 = 3072
    lr = np.concatenate([lr0 + a(16), lr0 + a(16), lr0 + 16 + a(16), lr0 + a(16), lr0 + a(32), lr0 + a(32)])
    sample["gin"] = _tiles(i["gla_w_in"][0], np.concatenate([lr, a(2048), 2048 + a(1024)]))
    sample["gout"] = _tiles(i["gla_w_out"][0], a(D))
    for n, c, k in STREAM:
        sample[n] = np.ascontiguousarray(sample[n]).reshape(c, P, k * P)
    wgk = np.zeros((P, 2, 4 * P), f32)
    wgk[0:16, 0] = i["gla_w_gk2"][0, 0]
    wgk[32:48, 1] = i["gla_w_gk2"][0, 1]
    sample["wgk"] = wgk.reshape(P, -1)
    par = np.zeros((P, NPARAM), f32)

    def put(name, v, rows=slice(None)):
        par[rows, PCOLS[name]:PCOLS[name] + v.shape[1]] = v
    put("norm", _by_chunk(i["norm_w"]))
    put("cw", _by_chunk(i["ssd_conv_w"][0]))
    put("cb", _by_chunk(i["ssd_conv_b"][0]))
    for d in range(2):
        rows = slice(32 * d, 32 * d + 16)
        put("dtb", i["ssd_dt_bias"][0].reshape(2, 16, 1)[d], rows)
        put("alog", i["ssd_a_log"][0].reshape(2, 16, 1)[d], rows)
    put("dskip", _by_chunk(np.repeat(i["ssd_d"][0], HDIM)))
    put("ssdn", _by_chunk(i["ssd_norm_w"][0]))
    put("qn", _by_chunk(i["mla_q_norm_w"][0]))
    put("kvn", _by_chunk(i["mla_kv_norm_w"][0]))
    put("bgk", _by_chunk(i["gla_b_gk"][0]))
    put("glan", _by_chunk(i["gla_norm_w"][0]))
    for l in range(2):
        put(f"fw{l}", _by_chunk(i["ffn_conv_w"][l]))
        put(f"fb{l}", _by_chunk(i["ffn_conv_b"][l]))
    put("eps", np.full((P, 1), EPS, f32))
    sample["par"] = par
    return sample


def _constants():
    f32 = np.float32
    n = np.arange(P)
    eye = np.eye(P, dtype=f32)
    up = (n[None, :] >= n[:, None]).astype(f32)
    one = np.ones((P, P), f32)
    half = n % ROPE
    rot = np.zeros((P, P), f32)
    src = np.where(half < ROPE // 2, n + ROPE // 2, n - ROPE // 2)
    rot[src, n] = np.where(half < ROPE // 2, -1, 1)
    dup = np.zeros((P, P), f32)
    dup[64 + half, n] = 1
    selrot = np.zeros((P, P), f32)
    selrot[64 + src % ROPE, n] = np.where(half < ROPE // 2, -1, 1)
    cst = np.concatenate([eye, up, one, up, up.T, one, up.T, rot, dup, selrot], 1)
    inv = (f32(1.0) / (f32(10000.0) ** (np.arange(0, ROPE, 2, dtype=f32) / f32(ROPE)))).astype(f32)
    ang = np.arange(SEQ, dtype=f32)[:, None] * inv[None, :]
    table = [np.tile(np.tile(t(ang).T.astype(f32), (4, 1)), (1, NREQ)) for t in (np.cos, np.sin)]
    gmask = np.tile((np.arange(T + CH) % CH != 0).astype(f32), (P, 1))
    return cst, np.concatenate(table, 1), np.concatenate([gmask, up, up.T], 1)


def kernel(**inputs):
    import concourse.bacc as bacc
    from concourse.bass_utils import run_bass_kernel_spmd

    nc = bacc.Bacc("TRN2", target_bir_lowering=False, num_devices=1)
    data = _layout({k: np.asarray(v) for k, v in inputs.items()})
    cst, rope, glac = _constants()
    data |= {"cst": cst, "rope": rope, "glac": glac}
    arrays, aps = {}, {}
    for name, a in data.items():
        arrays[f"in_{name}"] = np.ascontiguousarray(a)
        aps[name] = nc.dram_tensor(f"in_{name}", a.shape, F32, kind="ExternalInput").ap()
    out = nc.dram_tensor("out_y", (P, KD * T), F32, kind="ExternalOutput").ap()
    build_program(nc, aps["x"], {n: aps[n] for n, _, _ in STREAM}, aps["wgk"], aps["par"], aps["cst"], aps["rope"],
                  aps["glac"], out)
    r = run_bass_kernel_spmd(nc, [arrays], core_ids=[0])
    y = r.results[0]["out_y"].reshape(P, KD, T).transpose(2, 1, 0).reshape(NREQ, SEQ, D)
    return np.ascontiguousarray(y[0:1]), np.ascontiguousarray(y[1:2])
```
